# Optimizing a Trainium2 kernel written in Bass

```python
import math
import jax, jax.numpy as jnp
from jax import lax
import numpy as np

D_MODEL = 1024
BATCH = 1
SEQ = 2048
DEPTH = 2
DEC_BATCH = 8
DEC_SEQ = 1
PAST_LEN = 4096
PAGE_SIZE = 128

HEAD_DIM = 64
GROUP_W = D_MODEL // 4
CONV_W = GROUP_W
CONV_K = 3
RWKV_W = GROUP_W
RWKV_HEADS = RWKV_W // HEAD_DIM
LORA_W = 64
LORA_A = 64
RWKV_SHIFT_W = 3 * RWKV_W + LORA_W + LORA_A
MLA_HEADS = GROUP_W // HEAD_DIM
Q_RANK = 256
KV_RANK = 128
NOPE_DIM = 64
ROPE_DIM = 32
V_DIM = HEAD_DIM
MLA_W = MLA_HEADS * V_DIM
N_MEM = 256
MEM_HEADS = 4
MEM_W = MEM_HEADS * HEAD_DIM
D_MIX = CONV_W + RWKV_W + MLA_W + MEM_W
IN_SPLITS = (CONV_W, CONV_W, CONV_W, CONV_W, RWKV_SHIFT_W, RWKV_W, Q_RANK, KV_RANK, ROPE_DIM, MLA_W, MEM_W, MEM_W)
D_IN = 4 * CONV_W + RWKV_SHIFT_W + RWKV_W + Q_RANK + KV_RANK + ROPE_DIM + MLA_W + 2 * MEM_W
RWKV_SPLITS = (RWKV_W, RWKV_W, RWKV_W, LORA_W, LORA_A)
Q_BLOCK = 128
RMS_EPS = 1e-6
LNX_EPS = 64e-5
ROPE_BASE = 10000.0
DECAY_SCALE = 0.6065306597
MLA_SCALE = (NOPE_DIM + ROPE_DIM) ** -0.5
NEG_INF = -1e30

kernel_name = "hymba_conv_rwkv7_mla_memory_step"

def _split(x, sizes):
    idx = np.cumsum(np.array(sizes))[:-1].tolist()
    return jnp.split(x, idx, axis=-1)

def rms_norm(x, g):
    xf = x.astype(jnp.float32)
    y = xf * lax.rsqrt(jnp.mean(xf * xf, axis=-1, keepdims=True) + RMS_EPS)
    return (y * g.astype(jnp.float32)).astype(x.dtype)

def rope(x, pos):
    half = ROPE_DIM // 2
    inv = jnp.power(ROPE_BASE, -jnp.arange(half, dtype=jnp.float32) / half)
    ang = pos.astype(jnp.float32)[:, None] * inv[None, :]
    ang = ang.reshape(ang.shape[0], *([1] * (x.ndim - 3)), half)
    cos = jnp.cos(ang).astype(x.dtype)
    sin = jnp.sin(ang).astype(x.dtype)
    x1, x2 = x[..., :half], x[..., half:]
    return jnp.concatenate([x1 * cos - x2 * sin, x2 * cos + x1 * sin], axis=-1)

def short_conv(c_b, c_c, c_x, buf, w_conv):
    u = c_c * c_x
    S = u.shape[1]
    ext = jnp.concatenate([buf.astype(u.dtype), u], axis=1)
    y = ext[:, 0:S] * w_conv[0]
    for i in range(1, CONV_K):
        y = y + ext[:, i:i + S] * w_conv[i]
    return c_b * y, ext[:, S:]

def rwkv7_mix(proj_sh, prev_row, state0, p):
    B, S, _ = proj_sh.shape
    prev = jnp.concatenate([prev_row[:, None].astype(proj_sh.dtype), proj_sh[:, :-1]], axis=1)
    mixed = proj_sh + (prev - proj_sh) * p['mu']
    r, k, v, wl, al = _split(mixed, RWKV_SPLITS)
    log_w = -DECAY_SCALE * jax.nn.sigmoid(p['w0'] + jnp.tanh(wl) @ p['w2'])
    a = jax.nn.sigmoid(p['a0'] + al @ p['a2'])
    heads = lambda t: t.reshape(B, S, RWKV_HEADS, HEAD_DIM)
    kk = heads(k * p['k_k']).astype(jnp.float32)
    kk = kk * lax.rsqrt(jnp.sum(kk * kk, axis=-1, keepdims=True) + 1e-12)
    k = k * (1 + (a - 1) * p['k_a'])
    r_h, k_h, v_h, a_h = heads(r), heads(k), heads(v), heads(a)
    w_h = jnp.exp(heads(log_w).astype(jnp.float32))
    xs = tuple(jnp.moveaxis(t.astype(jnp.float32), 1, 0) for t in (r_h, k_h, v_h, w_h, kk, a_h))

    def step(St, inp):
        r_t, k_t, v_t, w_t, kk_t, a_t = inp
        sa = jnp.einsum('bhij,bhj->bhi', St, kk_t)
        St = (St * w_t[:, :, None, :] - sa[..., None] * (kk_t * a_t)[:, :, None, :]
              + v_t[..., None] * k_t[:, :, None, :])
        return St, jnp.einsum('bhij,bhj->bhi', St, r_t)

    S_final, y = lax.scan(step, state0.astype(jnp.float32), xs)
    y = jnp.moveaxis(y, 0, 1)
    mean = jnp.mean(y, axis=-1, keepdims=True)
    var = jnp.mean(jnp.square(y - mean), axis=-1, keepdims=True)
    y = ((y - mean) * lax.rsqrt(var + LNX_EPS)).reshape(B, S, RWKV_W)
    y = y * p['lnx_g'].astype(jnp.float32) + p['lnx_b'].astype(jnp.float32)
    bonus = jnp.sum(r_h * k_h * p['r_k'], axis=-1, keepdims=True) * v_h
    y = y.astype(proj_sh.dtype) + bonus.reshape(B, S, RWKV_W)
    return y, proj_sh[:, -1], S_final

def mem_kv(mem, g, wk, wv):
    B, M, _ = mem.shape
    mh = rms_norm(mem, g)
    k = (mh @ wk).reshape(B, M, MEM_HEADS, HEAD_DIM)
    v = (mh @ wv).reshape(B, M, MEM_HEADS, HEAD_DIM)
    return k, v

def mem_attend(q, mem_k, mem_v):
    B, S, _ = q.shape
    qh = q.reshape(B, S, MEM_HEADS, HEAD_DIM)
    s = jnp.einsum('bshd,bmhd->bhsm', qh, mem_k).astype(jnp.float32) * (HEAD_DIM ** -0.5)
    pr = jax.nn.softmax(s, axis=-1).astype(q.dtype)
    return jnp.einsum('bhsm,bmhd->bshd', pr, mem_v).reshape(B, S, MEM_W)

def prompt_attend(q_lat, q_rope, ckv, krope):
    B, S, H, R = q_lat.shape
    nb = S // Q_BLOCK
    blk = lambda t: jnp.moveaxis(t.reshape(B, nb, Q_BLOCK, *t.shape[2:]), 1, 0)
    kpos = jnp.arange(S)

    def one_block(args):
        i, ql, qr = args
        s = jnp.einsum('bqhr,bkr->bhqk', ql, ckv) + jnp.einsum('bqhd,bkd->bhqk', qr, krope)
        qpos = i * Q_BLOCK + jnp.arange(Q_BLOCK)
        s = jnp.where(kpos[None, :] <= qpos[:, None], s.astype(jnp.float32) * MLA_SCALE, NEG_INF)
        pr = jax.nn.softmax(s, axis=-1).astype(ckv.dtype)
        return jnp.einsum('bhqk,bkr->bqhr', pr, ckv)

    o = lax.map(one_block, (jnp.arange(nb), blk(q_lat), blk(q_rope)))
    return jnp.moveaxis(o, 0, 1).reshape(B, S, H, R)

def make_sample_attend(ckv_past, krope_past):
    def attend(q_lat, q_rope, ckv_new, krope_new):
        T = q_lat.shape[1]
        P = ckv_past.shape[1]
        s_past = jnp.einsum('bqhr,bkr->bhqk', q_lat, ckv_past) + jnp.einsum('bqhd,bkd->bhqk', q_rope, krope_past)
        s_new = jnp.einsum('bqhr,bkr->bhqk', q_lat, ckv_new) + jnp.einsum('bqhd,bkd->bhqk', q_rope, krope_new)
        causal = jnp.tril(jnp.ones((T, T), dtype=bool))
        s_new = jnp.where(causal, s_new.astype(jnp.float32) * MLA_SCALE, NEG_INF)
        s = jnp.concatenate([s_past.astype(jnp.float32) * MLA_SCALE, s_new], axis=-1)
        pr = jax.nn.softmax(s, axis=-1).astype(ckv_new.dtype)
        return (jnp.einsum('bhqk,bkr->bqhr', pr[..., :P], ckv_past)
                + jnp.einsum('bhqk,bkr->bqhr', pr[..., P:], ckv_new))
    return attend

def trunk_layer(x, pos, conv_buf, shift_prev, rwkv_state, mem_k, mem_v, attend, p):
    B, S, _ = x.shape
    h = rms_norm(x, p['pre_g'])
    proj = jnp.einsum('bsd,de->bse', h, p['w_in'])
    (c_b, c_c, c_x, c_gate, r_sh, r_gate, q_down, ckv_raw, kr_raw,
     mla_gate, mem_q, mem_gate) = _split(proj, IN_SPLITS)
    conv_out, conv_buf_new = short_conv(c_b, c_c, c_x, conv_buf, p['conv_w'])
    rwkv_out, shift_new, rwkv_state_new = rwkv7_mix(r_sh, shift_prev, rwkv_state, p)
    q = jnp.einsum('bsr,re->bse', rms_norm(q_down, p['q_norm_g']), p['w_uq'])
    q = q.reshape(B, S, MLA_HEADS, NOPE_DIM + ROPE_DIM)
    q_nope, q_rope = q[..., :NOPE_DIM], rope(q[..., NOPE_DIM:], pos)
    ckv = rms_norm(ckv_raw, p['kv_norm_g'])
    krope = rope(kr_raw, pos)
    q_lat = jnp.einsum('bshd,rhd->bshr', q_nope, p['w_uk'])
    o_lat = attend(q_lat, q_rope, ckv, krope)
    mla_out = jnp.einsum('bshr,rhd->bshd', o_lat, p['w_uv']).reshape(B, S, MLA_W)
    mem_out = mem_attend(mem_q, mem_k, mem_v)
    mixed = jnp.concatenate([conv_out * jax.nn.silu(c_gate), rwkv_out * jax.nn.silu(r_gate),
                             mla_out * jax.nn.silu(mla_gate), mem_out * jax.nn.silu(mem_gate)], axis=-1)
    x = x + rms_norm(jnp.einsum('bse,ed->bsd', mixed, p['w_out']), p['post_g'])
    return x, conv_buf_new, shift_new, rwkv_state_new, ckv, krope

def setup_inputs(seed: int = 0) -> dict:
    key = jax.random.key(seed)
    ks = iter(jax.random.split(key, 48))
    nrm = lambda shape, scale=1.0: jax.random.normal(next(ks), shape, jnp.float32) * scale
    gain = lambda shape: 1.0 + nrm(shape, 0.05)
    n_pages = PAST_LEN // PAGE_SIZE
    n_used = DEC_BATCH * n_pages
    n_phys = n_used + max(1, n_used // 4)
    x_prompt = nrm((BATCH, SEQ, D_MODEL))
    x_sample = nrm((DEC_BATCH, DEC_SEQ, D_MODEL))
    cache_ckv = nrm((DEPTH, n_phys, PAGE_SIZE, KV_RANK))
    cache_krope = nrm((DEPTH, n_phys, PAGE_SIZE, ROPE_DIM))
    cache_mem_k = nrm((DEPTH, DEC_BATCH, N_MEM, MEM_HEADS, HEAD_DIM))
    cache_mem_v = nrm((DEPTH, DEC_BATCH, N_MEM, MEM_HEADS, HEAD_DIM))
    state_conv = nrm((DEPTH, DEC_BATCH, CONV_K - 1, CONV_W))
    state_rwkv_shift = nrm((DEPTH, DEC_BATCH, RWKV_SHIFT_W))
    state_rwkv = nrm((DEPTH, DEC_BATCH, RWKV_HEADS, HEAD_DIM, HEAD_DIM), 0.1)
    page_table = jax.random.permutation(next(ks), n_phys)[:n_used].reshape(DEC_BATCH, n_pages).astype(jnp.int32)
    mem_prompt = nrm((BATCH, N_MEM, D_MODEL))
    return {
        'x_prompt': x_prompt,
        'x_sample': x_sample,
        'cache_ckv': cache_ckv,
        'cache_krope': cache_krope,
        'cache_mem_k': cache_mem_k,
        'cache_mem_v': cache_mem_v,
        'state_conv': state_conv,
        'state_rwkv_shift': state_rwkv_shift,
        'state_rwkv': state_rwkv,
        'page_table': page_table,
        'mem_prompt': mem_prompt,
        'pre_norm_g': gain((DEPTH, D_MODEL)),
        'post_norm_g': gain((DEPTH, D_MODEL)),
        'w_in': nrm((DEPTH, D_MODEL, D_IN), D_MODEL ** -0.5),
        'w_out': nrm((DEPTH, D_MIX, D_MODEL), D_MIX ** -0.5),
        'conv_w': nrm((DEPTH, CONV_K, CONV_W), CONV_K ** -0.5),
        'rwkv_mu': jax.random.uniform(next(ks), (DEPTH, RWKV_SHIFT_W), jnp.float32),
        'rwkv_w0': nrm((DEPTH, RWKV_W), 0.5),
        'rwkv_w2': nrm((DEPTH, LORA_W, RWKV_W), 0.1),
        'rwkv_a0': nrm((DEPTH, RWKV_W), 0.1),
        'rwkv_a2': nrm((DEPTH, LORA_A, RWKV_W), 0.1),
        'rwkv_k_k': 0.85 + nrm((DEPTH, RWKV_W), 0.05),
        'rwkv_k_a': gain((DEPTH, RWKV_W)),
        'rwkv_r_k': nrm((DEPTH, RWKV_HEADS, HEAD_DIM), 0.1),
        'rwkv_lnx_g': gain((DEPTH, RWKV_W)),
        'rwkv_lnx_b': nrm((DEPTH, RWKV_W), 0.01),
        'mla_q_norm_g': gain((DEPTH, Q_RANK)),
        'mla_w_uq': nrm((DEPTH, Q_RANK, MLA_HEADS * (NOPE_DIM + ROPE_DIM)), Q_RANK ** -0.5),
        'mla_kv_norm_g': gain((DEPTH, KV_RANK)),
        'mla_w_uk': nrm((DEPTH, KV_RANK, MLA_HEADS, NOPE_DIM), KV_RANK ** -0.5),
        'mla_w_uv': nrm((DEPTH, KV_RANK, MLA_HEADS, V_DIM), KV_RANK ** -0.5),
        'mem_norm_g': gain((DEPTH, D_MODEL)),
        'w_mem_k': nrm((DEPTH, D_MODEL, MEM_W), D_MODEL ** -0.5),
        'w_mem_v': nrm((DEPTH, D_MODEL, MEM_W), D_MODEL ** -0.5),
    }

def reference(x_prompt, x_sample, cache_ckv, cache_krope, cache_mem_k, cache_mem_v, state_conv,
              state_rwkv_shift, state_rwkv, page_table, mem_prompt, pre_norm_g, post_norm_g, w_in, w_out,
              conv_w, rwkv_mu, rwkv_w0, rwkv_w2, rwkv_a0, rwkv_a2, rwkv_k_k, rwkv_k_a, rwkv_r_k, rwkv_lnx_g,
              rwkv_lnx_b, mla_q_norm_g, mla_w_uq, mla_kv_norm_g, mla_w_uk, mla_w_uv, mem_norm_g, w_mem_k, w_mem_v):
    Bp, Sp, _ = x_prompt.shape
    Bs, Ts, _ = x_sample.shape
    pos_p = jnp.arange(Sp, dtype=jnp.int32)
    pos_s = PAST_LEN + jnp.arange(Ts, dtype=jnp.int32)
    conv0 = jnp.zeros((Bp, CONV_K - 1, CONV_W), x_prompt.dtype)
    shift0 = jnp.zeros((Bp, RWKV_SHIFT_W), x_prompt.dtype)
    rstate0 = jnp.zeros((Bp, RWKV_HEADS, HEAD_DIM, HEAD_DIM), jnp.float32)
    xp, xs = x_prompt, x_sample
    ckv_p, ckv_s, kr_p, kr_s, mk_p, mv_p = [], [], [], [], [], []
    cv_p, cv_s, sh_p, sh_s, st_p, st_s = [], [], [], [], [], []
    for l in range(DEPTH):
        p = {'pre_g': pre_norm_g[l], 'post_g': post_norm_g[l], 'w_in': w_in[l], 'w_out': w_out[l],
             'conv_w': conv_w[l], 'mu': rwkv_mu[l], 'w0': rwkv_w0[l], 'w2': rwkv_w2[l], 'a0': rwkv_a0[l],
             'a2': rwkv_a2[l], 'k_k': rwkv_k_k[l], 'k_a': rwkv_k_a[l], 'r_k': rwkv_r_k[l],
             'lnx_g': rwkv_lnx_g[l], 'lnx_b': rwkv_lnx_b[l], 'q_norm_g': mla_q_norm_g[l], 'w_uq': mla_w_uq[l],
             'kv_norm_g': mla_kv_norm_g[l], 'w_uk': mla_w_uk[l], 'w_uv': mla_w_uv[l]}
        mk, mv = mem_kv(mem_prompt, mem_norm_g[l], w_mem_k[l], w_mem_v[l])
        xp, cb, sh, st, ckv, kr = trunk_layer(xp, pos_p, conv0, shift0, rstate0, mk, mv, prompt_attend, p)
        ckv_p.append(ckv); kr_p.append(kr); mk_p.append(mk); mv_p.append(mv)
        cv_p.append(cb); sh_p.append(sh); st_p.append(st)
        ckv_past = cache_ckv[l, page_table].reshape(Bs, -1, KV_RANK)
        kr_past = cache_krope[l, page_table].reshape(Bs, -1, ROPE_DIM)
        xs, cb, sh, st, ckv, kr = trunk_layer(xs, pos_s, state_conv[l], state_rwkv_shift[l], state_rwkv[l],
                                              cache_mem_k[l], cache_mem_v[l],
                                              make_sample_attend(ckv_past, kr_past), p)
        ckv_s.append(ckv); kr_s.append(kr); cv_s.append(cb); sh_s.append(sh); st_s.append(st)
    return (xp, xs, jnp.stack(ckv_p), jnp.stack(ckv_s), jnp.stack(kr_p), jnp.stack(kr_s),
            jnp.stack(mk_p), jnp.stack(mv_p), jnp.stack(cv_p), jnp.stack(cv_s),
            jnp.stack(sh_p), jnp.stack(sh_s), jnp.stack(st_p), jnp.stack(st_s))


_drawn_inputs = setup_inputs


def setup_inputs(seed=0):
    import zlib

    import numpy as np

    out = dict(_drawn_inputs(seed))
    spreads = {}
    factors = {'cache_ckv': 2.861,
     'cache_krope': 4.806,
     'rwkv_k_k': 4.636,
     'rwkv_lnx_b': 6.271,
     'mla_q_norm_g': 8.0}
    for name, (base, spread) in spreads.items():
        noise = np.random.default_rng([zlib.crc32(name.encode()), seed]).standard_normal(out[name].shape)
        drawn = base * np.exp(spread * noise) if base else spread * noise
        out[name] = __import__('jax').numpy.asarray(drawn.astype(out[name].dtype))
    for name, factor in factors.items():
        out[name] = (out[name] * factor).astype(out[name].dtype)
    return out
```

```python
from contextlib import ExitStack

import concourse.bass as bass
import numpy as np
from concourse import mybir

F32 = mybir.dt.float32
BF16 = mybir.dt.bfloat16
I32 = mybir.dt.int32
ALU = mybir.AluOpType
ACT = mybir.ActivationFunctionType
AX = mybir.AxisListType.X
MULT, ADD, SUB, POW, MAX = ALU.mult, ALU.add, ALU.subtract, ALU.pow, ALU.max

P = 128
D = 1024
KD = D // P
L = 2
S = 2048
NS = 8
T = 256
NB = S // T
IT = NB + 1
C = 64
HD = 64
NH = 4
PAST, PAGE, NPHYS = 4096, 128, 320
NPG = PAST // PAGE
R, RD, NOPE = 128, 32, 64
NM = 256
KC = 512
DECAY = 0.6065306597
EPS, LN_EPS = 1e-6, 64e-5
MLA_SCALE = (NOPE + RD) ** -0.5
MEM_SCALE = HD ** -0.5
NEG = -1e30
STEPS = sum((b // 2 + 1) * 8 for b in range(NB))

GROUPS = [("wlal", 1792, 128), ("k", 1280, 256), ("r", 1024, 256), ("v", 1536, 256), ("ckv", 2432, 160),
          ("qd", 2176, 256), ("mq", 2848, 256), ("cx", 512, 256), ("cc", 256, 256), ("cb", 0, 256),
          ("cg", 768, 256), ("rg", 1920, 256), ("ag", 2592, 256), ("mg", 3104, 256)]
NG = len(GROUPS)
TILES = [(g, i, 128 * i, min(128, w - 128 * i)) for g, (_, _, w) in enumerate(GROUPS) for i in range((w + 127) // 128)]
NTILES = len(TILES)
BY_ACT = {"wlal", "k", "r", "v", "ckv", "qd", "mq", "cx"}
ACT_TILES = [t for t, x in enumerate(TILES) if GROUPS[x[0]][0] in BY_ACT]
LAST = [max(t for t, x in enumerate(TILES) if x[0] == g) for g in range(NG)]
DVE_TILES = [t for t, x in enumerate(TILES) if GROUPS[x[0]][0] not in BY_ACT]

VECS = [("pre", 8), ("conv", 6), ("mu", 7), ("w0", 2), ("a0", 2), ("kk", 2), ("ka", 2), ("rk", 2),
        ("lg", 2), ("lb", 2), ("qn", 2), ("kn", 1), ("mn", 8)]
VOFF, _o = {}, 0
for _n, _c in VECS:
    VOFF[_n] = _o
    _o += _c
NVEC = _o

CONSTS = [("ident", 128), ("bones", 128), ("ones", 128), ("mgram", 512), ("m1t", 128), ("mlev", 6 * 128),
          ("id64", 64), ("scan", 256), ("rot", 32), ("rep", 128),
          ("tmask", 4), ("sub", 1)]
COFF, _o = {}, 0
for _n, _c in CONSTS:
    COFF[_n] = _o
    _o += _c
NCONST = _o
FMZ = 15 * 128
FMW = FMZ + KC


def loads_of_slot(g):
    return 16 * sum(2 if GROUPS[q][1] == 0 else 1 for q in range(g % 2, g + 1, 2))


def constants():
    c = np.zeros((P, NCONST), np.float32)
    i = np.arange(P)
    r, q = i[:, None], i[None, :]

    def put(name, a):
        c[:, COFF[name]:COFF[name] + a.shape[1]] = a
    put("ident", (r == q) * 1.0)
    put("bones", (r // 64 == q // 64) * 1.0)
    put("ones", np.ones((P, P)))
    same = r // C == q // C
    put("mgram", np.concatenate([same & (r < q), same & (r <= q)] * 2, 1) * 1.0)
    lev = [(r // (2 * w) == q // (2 * w)) & (r % (2 * w) >= w) & (q % (2 * w) < w) for w in (1, 2, 4, 8, 16, 32)]
    put("m1t", lev[0].T * 1.0)
    put("mlev", np.concatenate(lev, 1) * 1.0)
    put("id64", (r % 64 == np.arange(64)[None, :]) * 1.0)
    put("scan", np.broadcast_to((np.arange(T) % C != 0)[None, :] * 1.0, (P, T)))
    rot = np.zeros((P, 32))
    for a in range(16):
        rot[a + 16, a] = -1.0
        rot[a, a + 16] = 1.0
    put("rot", rot)
    put("rep", (r == q % 32) * 1.0)
    put("tmask", (r // 32 == np.arange(4)[None, :]) * 1.0)
    put("sub", (i // 32)[:, None] * 1.0)
    return c


def rope_tables():
    half = RD // 2
    inv = np.power(np.float32(10000.0), (-np.arange(half, dtype=np.float32) / np.float32(half)))
    pos = np.concatenate([np.arange(S), np.full(NS, PAST)]).astype(np.float32)
    ang = inv.astype(np.float32)[:, None] * pos[None, :]
    ang = np.concatenate([ang, ang], 0)
    return np.stack([np.cos(ang), np.sin(ang)]).astype(np.float32)


class Block:

    def __init__(self, l, block):
        self.l, self.block, self.prompt = l, block, block is not None
        if self.prompt:
            self.it, self.ip, self.tok, self.n, self.tiles = l * IT + block, l * NB + block, block * T, T, 2
        else:
            self.it, self.n, self.tiles = l * IT + NB, NS, 1


class Sig:

    def __init__(self, ctx, nc, name, n, base=0):
        self.h, self.n, self.base = ctx.enter_context(nc.semaphore(name)), n, base

    def wait(self, eng, it, k):
        eng.wait_ge(self.h, it * self.n + (k + self.base))

    def wait_alone(self, eng, it, k):
        eng.wait_ge(self.const, 32)
        eng.wait_ge(self.h, it * self.n + (k + self.base))


def build_program(nc, a):
    ctx = ExitStack()
    with ctx:
        def sb(name, shape, dt=F32):
            return ctx.enter_context(nc.sbuf_tensor(name, shape, dt))

        begun = []

        def sig(name, n, base=0):
            s = Sig(ctx, nc, name, n, base)
            if base:
                begun.append(s)
            return s

        cst = sb("cst", [P, NCONST])
        fmask = sb("fmask", [P, FMW], BF16)
        win = sb("win", [P, 2, KD, 256])
        wout = sb("wout", [P, 2, D])
        hT = sb("hT", [P, KD, T])
        mix = sb("mix", [P, 8, T])
        pr = sb("pr", [P, 7, T + 1])
        halo = sb("halo", [P, 7])
        qd = sb("qd", [P, 2, T])
        ckr = sb("ckr", [P, T])
        krr = sb("krr", [RD, T])
        mq = sb("mq", [P, 2, T])
        cxs = sb("cxs", [P, 2, T])
        u = sb("u", [P, 2, T + 2])
        kv = sb("kv", [P, 6144])
        memKT = sb("memKT", [P, 2, NM])
        memV = sb("memV", [P, 2, 256])
        wuq = sb("wuq", [P, 2, 384])
        wukn = sb("wukn", [P, 256])
        wukT = sb("wukT", [64, NH, R])
        wuv = sb("wuv", [P, 256])
        w2a2 = sb("w2a2", [P, 256])
        vecrow = sb("vecrow", [NVEC, P])
        vec = sb("vec", [P, NVEC])
        postg = sb("postg", [P, D])
        cs = sb("cs", [RD, 2, T])
        xin = sb("xin", [P, 2, D])
        xn = sb("xn", [P, D])
        st = sb("st", [P, 48])
        T1 = sb("T1", [P, 2, T]); T2 = sb("T2", [P, 2, T]); sw = sb("sw", [P, 2, T]); aa = sb("aa", [P, 2, T])
        Ls = sb("Ls", [P, 2, T]); eP = sb("eP", [P, 2, T]); Bp = sb("Bp", [P, 2, T]); Kt = sb("Kt", [P, 2, T])
        bon = sb("bon", [P, 2, T]); yy = sb("yy", [P, 2, T])
        T3 = sb("T3", [P, 2, T])
        KR = sb("KR", [P, 2, 2, 2, P])
        nat = sb("nat", [P, 2, 3, P])
        G = sb("G", [P, NH, 4, P])
        XX = sb("XX", [P, NH, 2, P])
        X0 = sb("X0", [P, 2, P]); SA = sb("SA", [P, 2, P]); BD = sb("BD", [P, 2, P]);
        ql = sb("ql", [P, NH, T]); qr = sb("qr", [RD, NH, T]); qr2 = sb("qr2", [RD, NH, T])
        qnp = sb("qnp", [64, NH, T])
        Sm = sb("Sm", [P, 2, KC]); PT = sb("PT", [P, 2, 4, P]); OO = sb("OO", [P, 8, P]);
        ml = sb("ml", [P, 8, 8])
        shs = sb("shs", [P, 7, NS]); cvs = sb("cvs", [P, 2, NS, 2]); raw = sb("raw", [P, 7, NS])
        sqn = sb("sqn", [P, 3, T]); ge = sb("ge", [P, 2, T]); nvec = sb("nvec", [P, 4])
        cko = sb("cko", [P, 2, P]); kro = sb("kro", [P, 2, RD])
        QR4 = sb("QR4", [P, NS, 16]); sns = sb("sns", [P, NS, NH]); Pb = sb("Pb", [P, P + 4])
        pgi = sb("pgi", [P, NS], I32); pgf = sb("pgf", [P, NS]); idx = sb("idx", [P, NS], I32)
        idc = sb("idc", [P, 1], I32); zero = sb("zero", [P, 1], I32); zerof = sb("zerof", [P, 16]); mhalf = sb("mhalf", [P, 1])
        PP = [ctx.enter_context(nc.psum_tensor(f"bank{i}", [P, 512], F32)) for i in range(8)]

        ckvT = kv[:, 0:2048]
        ckvN = kv[:, 2048:4096].rearrange("p (t r) -> p t r", r=R)
        krT = kv[0:RD, 4096:6144]
        An, Om = OO[:, 0:4, :], OO[:, 4:8, :]
        Qs, BT = PT[:, 0, :, :], PT[:, 1, 0:2, :]
        eN, eK = ql[:, 0:2, :], ql[:, 2:4, :]
        OT = XX[:, :, :, :].rearrange("p h a t -> p h (a t)")
        junk = G[:, :, :, :].rearrange("p h a t -> p (h a t)")
        fst = KR[:, :, :, :, :].rearrange("p a j k t -> p (a j k t)")[:, 0:5 * P]
        shn = qnp[0:NS, :, :].rearrange("p h t -> p (h t)")[:, 0:896]
        cvn = qr[0:2 * NS, 0, :]
        kvg = kv[:, 0:4096].rearrange("p (c r) -> p c r", r=R)
        krg = kv[:, 4096:5120]
        dmk = kv[:, 0:2048].rearrange("p (b t c) -> p b t c", b=4, t=2)
        dmv = kv[:, 2048:4096].rearrange("p (b t c) -> p b t c", b=4, t=2)
        dmp = kv[:, 4096:6144].rearrange("p (b t c) -> p b t c", b=4, t=2)
        S0 = Sm[:, :, :].rearrange("p a (b j) -> p (a b) j", j=64)
        SD = OO[:, :, :].rearrange("p a (b j) -> p (a b) j", j=64)
        SW = XX[:, :, :, :].rearrange("p a c (b j) -> p (a c b) j", j=64)
        qB = G[:, :, :, :].rearrange("p h a t -> p (h a t)").rearrange("p (b a c) -> p b a c", b=NS, a=2)
        T1f, T2f, T3f = (t[:, :, :].rearrange("p a t -> p (a t)") for t in (T1, T2, T3))
        Sm4 = Sm[:, :, :].rearrange("p a (b t) -> p (a b) t", b=2)

        def K(name, n=None, m=P):
            w = dict(CONSTS)[name] if n is None else n
            return cst[0:m, COFF[name]:COFF[name] + w]

        def V(name, i=0, n=1):
            return vec[:, VOFF[name] + i:VOFF[name] + i + n]
        ident, bones, ones = K("ident"), K("bones"), K("ones")
        mgram = K("mgram").rearrange("p (a q) -> p a q", a=4)
        mlev = K("mlev").rearrange("p (a q) -> p a q", a=6)

        def bc(ap, shape):
            return ap.broadcast_to(shape)

        s_const = sig("const_loaded", 0)
        Sig.const = s_const.h
        s_xcopy = sig("residual_copied", 0)
        s_lw = sig("layer_weights_loaded", 16 * (len(VECS) + 8))
        s_mw = sig("memory_loaded", 48)
        s_vt = sig("vectors_transposed", 1)
        s_vr = sig("vectors_ready", 1)
        s_mem = {n: sig("mem_" + n, c, int(n == "out")) for n, c in dict(ss=2, xn=2, tp=2, hT=1, kv=2, kvr=1, kt=1, ktr=1, out=64, pw=2, pr=2).items()}
        s_state = sig("states_stored", 16 * (2 + NH + NS + 3), base=1)
        s_fp = sig("prompt_states_turned", 1)
        s_fpr = sig("prompt_states_read", 1)
        s_x = sig("x_loaded", 16)
        s_cs = sig("rope_tables_loaded", 16)
        s_ss = sig("x_squares_summed", 2)
        s_xn = sig("x_normalised", 2)
        s_xt = sig("x_transposed", 2)
        s_hT = sig("h_ready", 1)
        s_wi = [sig(f"w_in_loaded{i}", loads_of_slot(NG - 2 + i)) for i in range(2)]
        s_pj = sig("projected", NTILES, base=1)
        s_pa = sig("projection_read_by_act", len(ACT_TILES))
        s_pv = sig("projection_read_by_dve", len(DVE_TILES))
        s_shift = sig("token_shift_done", 4)
        s_th = sig("tanh_ready", 1)
        s_lo = sig("lora_done", 1)
        s_lor = sig("lora_read", 1)
        s_sg = sig("decay_summed", 1)
        s_dec = sig("decay_factors_ready", 1)
        s_sq = sig("key_squares_ready", 1)
        s_sqd = sig("key_norms_done", 1)
        s_bo = sig("bonus_products_ready", 1)
        s_bod = sig("bonus_summed", 1)
        s_bor = sig("bonus_read", 1)
        s_nq = sig("latent_squares_ready", 1)
        s_nqd = sig("latent_norms_done", 1)
        s_qn = sig("latents_normalised", 1)
        s_qp = sig("queries_projected", 2)
        s_qpr = sig("queries_read", 2)
        s_ql = sig("latent_queries_done", 2)
        s_qla = sig("latent_queries_read", 1)
        s_qlr = sig("queries_rotated", 1)
        s_kr = sig("key_partner_and_latents_turned", 2)
        s_krr = sig("keys_rotated", 1)
        s_kn = sig("rotary_rows_done", 1)
        s_kvd = sig("latents_cached", 1, base=1)
        s_coe = sig("latent_rows_read", 1, base=1)
        s_ge = sig("gate_exponentials", 8)
        s_an = sig("running_max_ready", STEPS)
        s_co = sig("latents_written", 32, base=1)
        s_rt = sig("rwkv_operands_ready", 1)
        s_nt = sig("rwkv_transposed", 4)
        s_ntr = sig("rwkv_natural_ready", 4)
        s_gr = sig("grams_done", 4)
        s_grr = sig("grams_masked", 2)
        s_om = sig("level_block_ready", 10)
        s_q = sig("inverse_first_product", 20)
        s_qrd = sig("inverse_first_read", 20)
        s_xx = sig("inverse_second_product", 20)
        s_xxr = sig("inverse_updated", 20)
        s_x0 = sig("chunk_rhs_done", 8)
        s_x0r = sig("chunk_rhs_read", 8)
        s_sa = sig("chunk_solved", 8)
        s_sar = sig("chunk_solution_read", 8)
        s_su = sig("state_increment_done", 8)
        s_sur = sig("state_updated", 8)
        s_y = sig("rwkv_out_done", 4)
        s_yr = sig("rwkv_out_read", 4)
        s_lm = sig("mean_summed", 1)
        s_lc = sig("centred_squares_ready", 1)
        s_lv = sig("variance_summed", 1)
        s_lvr = sig("rwkv_group_done", 1)
        s_as = sig("scores_done", STEPS)
        s_am = sig("scores_masked", STEPS)
        s_ae = sig("probs_ready", STEPS)
        s_at = sig("probs_transposed", STEPS, base=1)
        s_ar = sig("probs_transposed_read", STEPS)
        s_av = sig("values_summed", STEPS, base=1)
        s_ao = sig("values_read", STEPS, base=1)
        s_ai = sig("attention_begun", 1)
        s_on = sig("attention_normalised", 1)
        s_ot = sig("attention_transposed", 1)
        s_otr = sig("attention_transposed_read", 1)
        s_uv = sig("attention_projected", 1)
        s_uvr = sig("attention_gated", 1)
        s_ms = sig("mem_scores_done", 2)
        s_mx = sig("mem_max_ready", 2)
        s_me = sig("mem_exp_done", 2)
        s_mn = sig("mem_probs_ready", 2)
        s_mt = sig("mem_probs_transposed", 2)
        s_mtr = sig("mem_probs_read", 2)
        s_mo = sig("mem_values_done", 1)
        s_mix = sig("mixed_ready", 1)
        s_wo = [sig(f"w_out_loaded{i}", 16 * 4) for i in range(2)]
        s_wou = sig("w_out_used", KD, base=1)
        s_o = sig("out_projected", 1)
        s_os = sig("out_squares_summed", 1)
        s_of = sig("residual_added", 1)
        s_od = sig("residual_stored", 16, base=1)
        s_pw = sig("root_wanted", 4)
        s_pr = sig("root_done", 4)
        s_rw = sig("square_root_wanted", 2)
        s_rd = sig("square_root_done", 2)
        s_pg = sig("pages_loaded", 0)
        s_se = sig("spread_operand_ready", 5)
        s_sb = sig("rows_spread", 5)
        s_sl = sig("decode_states_loaded", 16 * NS)
        s_sst2 = sig("decode_states_updated", 1)
        s_sy = sig("decode_rwkv_out", 1)
        s_sr = sig("decode_rows_turned", 1)
        s_srr = sig("decode_rows_read", 1)
        s_dp = sig("own_score_products", 1)
        s_dq = sig("own_scores_and_spread_queries", 1)
        s_dqr = sig("decode_queries_ready", 1)
        s_dg = sig("pages_gathered", 32 * NS)
        s_dt = sig("decode_keys_turned", 8 * NS)
        s_dtr = sig("decode_latents_read", 8 * NS, base=1)
        s_dtv = sig("decode_rotary_keys_read", 8 * NS, base=1)
        s_ds = sig("decode_scores_done", 8 * NS)
        s_dm1 = sig("decode_partition_max", NS)
        s_dm2 = sig("decode_max", NS)
        s_dx = sig("decode_scores_shifted", NS)
        s_dxe = sig("decode_exponentials", NS)
        s_de = sig("decode_probs_summed", NS)
        s_dv = sig("decode_values_done", NS)
        s_da = sig("decode_attention_done", NS)
        s_qe = sig("memory_query_operand", 2)
        s_qb = sig("memory_queries_spread", 2)
        s_dml = sig("decode_memory_loaded", 16 * 16)
        s_dmx = sig("memory_partition_max", 2)
        s_dmr = sig("memory_max", 2)
        s_dms = sig("memory_scores_shifted", 2)
        s_dme = sig("memory_exponentials", 2)
        s_dmo = sig("memory_values_done", 2)
        s_dm = sig("memory_half_done", 2)

        xres, csd = a["xres"], a["cs"]
        blk = ctx.enter_context(nc.Block())

        def prompt_loop(eng, body, l):
            with eng().Fori(0, NB // 2) as m:
                with eng().Fori(0, 2) as e:
                    body(Block(l, m * 2 + e), m, e)

        def steps_before(l, m, e):
            return l * STEPS + (m + e) * (m + 1) * 8

        @blk.sync
        def _(sp):
            for s in begun:
                sp.sem_inc(s.h, 1)
            sp.dma_start(cst[:, :], a["cst"]).then_inc(s_const.h, 16)
            sp.dma_start(fmask[:, :], a["fm"]).then_inc(s_const.h, 16)
            sp.wait_ge(s_const.h, 32)
            sp.dma_start(xres[0, 0:S, :], a["x_prompt"][0]).then_inc(s_xcopy.h, 16)
            sp.dma_start(xres[0, S:S + NS, :], a["x_sample"][:, 0, :]).then_inc(s_xcopy.h, 16)
            sp.wait_ge(s_xcopy.h, 32)
            with sp.Fori(0, L) as l:
                s_od.wait_alone(sp, l * IT, 0)
                sl = bass.ds(l, 1)
                count = [0]

                def put(dst, src):
                    sp.dma_start(dst, src).then_inc(s_lw.h, 16)
                    count[0] += 16

                def rows(name, src):
                    n = dict(VECS)[name]
                    put(vecrow[VOFF[name]:VOFF[name] + n, :], src.rearrange("a (n p) -> (a n) p", p=P))
                sp.dma_start(xin[:, :, :], a["mem_prompt"][0].rearrange("(t p) d -> p t d", p=P)).then_inc(s_mw.h, 16)
                wm = kv[:, 0:4096].rearrange("p (k n) -> p k n", k=KD)
                sp.dma_start(wm[:, :, 0:256], a["w_mem_k"][sl].rearrange("a (k p) n -> p (a k) n", p=P)).then_inc(s_mw.h, 16)
                sp.dma_start(wm[:, :, 256:512], a["w_mem_v"][sl].rearrange("a (k p) n -> p (a k) n", p=P)).then_inc(s_mw.h, 16)
                s_mem["out"].wait_alone(sp, l, 0)
                rows("pre", a["pre_norm_g"][sl, :])
                rows("conv", a["conv_w"][sl].rearrange("a k c -> a (k c)"))
                rows("mu", a["rwkv_mu"][sl, :])
                rows("w0", a["rwkv_w0"][sl, :])
                rows("a0", a["rwkv_a0"][sl, :])
                rows("kk", a["rwkv_k_k"][sl, :])
                rows("ka", a["rwkv_k_a"][sl, :])
                rows("rk", a["rwkv_r_k"][sl].rearrange("a h d -> a (h d)"))
                rows("lg", a["rwkv_lnx_g"][sl, :])
                rows("lb", a["rwkv_lnx_b"][sl, :])
                rows("qn", a["mla_q_norm_g"][sl, :])
                rows("kn", a["mla_kv_norm_g"][sl, :])
                rows("mn", a["mem_norm_g"][sl, :])
                put(postg[:, :], a["post_norm_g"][sl, :].broadcast_to([P, D]))
                put(wuq[:, :, :], a["mla_w_uq"][sl].rearrange("a (t p) n -> p (a t) n", p=P))
                put(wukn[:, :], a["mla_w_uk"][sl].rearrange("a r h d -> (a r) (h d)"))
                put(wuv[:, :], a["mla_w_uv"][sl].rearrange("a r h d -> (a r) (h d)"))
                put(w2a2[0:64, :], a["rwkv_w2"][sl].rearrange("a r c -> (a r) c"))
                put(w2a2[64:128, :], a["rwkv_a2"][sl].rearrange("a r c -> (a r) c"))
                s_state.wait_alone(sp, l, 0)
                put(shn[:, :], a["state_rwkv_shift"][sl].rearrange("a b c -> (a b) c"))
                put(cvn[:, :], a["state_conv"][sl].rearrange("a b k c -> (a b k) c"))
                assert count[0] == s_lw.n

                def block(it, tok, n):
                    s_kvd.wait_alone(sp, it, 0)
                    s_od.wait_alone(sp, it, 0)
                    s_mem["xn"].wait_alone(sp, l, 2)
                    if n == T:
                        src = xres[sl, bass.ds(tok, n), :].rearrange("a (t p) d -> p (a t) d", p=P)
                        sp.dma_start(xin[:, :, :], src).then_inc(s_x.h, 16)
                    else:
                        sp.dma_start(xin[0:n, 0, :], xres[sl, tok:tok + n, :].rearrange("a p d -> p (a d)")).then_inc(s_x.h, 16)
                    dst = cs[:, :, 0:n]
                    sp.dma_start(dst, csd[:, :, bass.ds(tok, n)].rearrange("c p t -> p c t")).then_inc(s_cs.h, 16)
                    for g, (_, c0, w) in enumerate(GROUPS):
                        s_pj.wait_alone(sp, it, 0 if g < 2 else LAST[g - 2] + 1)
                        src = a["w_in"][sl, :, c0:c0 + w].rearrange("a (k p) n -> p (a k) n", p=P)
                        for k0, k1 in ([(0, KD)] if c0 else [(1, KD), (0, 1)]):
                            sp.dma_start(win[:, g % 2, k0:k1, 0:w], src[:, k0:k1, :]).then_inc(s_wi[g % 2].h, 16)
                def output_weights(it, k0, k1):
                    for k in range(k0, k1):
                        s_wou.wait_alone(sp, it, max(k - 1, 0))
                        src = a["w_out"][sl, k * P:(k + 1) * P, :].rearrange("a p n -> (a p) n")
                        sp.dma_start(wout[:, k % 2, :], src).then_inc(s_wo[k % 2].h, 16)

                def prompt_block(B, m, e):
                    block(B.it, B.tok, T)
                    output_weights(B.it, 0, KD)
                prompt_loop(lambda: sp, prompt_block, l)
                block(l * IT + NB, S, NS)
                output_weights(l * IT + NB, 0, 2)
                s_rt.wait_alone(sp, l * IT + NB, 1)
                for b in range(NS):
                    sp.dma_start(S0[:, 2 * b:2 * b + 2, :],
                                 a["state_rwkv"][sl, b].rearrange("a (p h) i j -> (h i) (a p) j", p=2)).then_inc(s_sl.h, 16)
                for q in range(2):
                    if q == 0:
                        s_da.wait_alone(sp, l, NS)
                    else:
                        s_dm.wait_alone(sp, l, 1)
                    for b in range(4):
                        sp.dma_start(dmk[:, b, :, :], a["cache_mem_k"][sl, 4 * q + b].rearrange("a (t p) h d -> p (a t) (h d)", p=P)).then_inc(s_dml.h, 16)
                        sp.dma_start(dmv[:, b, :, :], a["cache_mem_v"][sl, 4 * q + b].rearrange("a (t p) h d -> p (a t) (h d)", p=P)).then_inc(s_dml.h, 16)
                output_weights(l * IT + NB, 2, KD)
            sp.wait_ge(s_od.h, L * IT * s_od.n + 1)
            sp.wait_ge(s_state.h, L * s_state.n + 1)
            sp.wait_ge(s_co.h, L * IT * s_co.n + 1)
            sp.wait_ge(s_mem["out"].h, L * s_mem["out"].n + 1)

        @blk.tensor
        def _(pe):
            def mm(out, lhsT, rhs, start=True, stop=True):
                return pe.matmul(out, lhsT, rhs, start=start, stop=stop, skip_group_check=True)

            def tr(out, in_, w):
                return pe.transpose(out, in_, ident[0:w, 0:w])

            def transpose_rows(sig_in, sig_out, it, tiles, w, k):
                for j in range(tiles):
                    sig_in.wait_alone(pe, it, j + 1)
                    for dt in range(KD):
                        c = (dt % 2) * T + j * P
                        rows, out = xn[0:w, dt * P:(dt + 1) * P], PP[dt // 2][:, c:c + w]
                        last = tr(out, rows, w) if w == P else mm(out, rows, ident[0:w, 0:w])
                    last.then_inc(sig_out.h, k)

            def halves(bank, n, parts=P):
                return PP[bank][0:parts, :].rearrange("p (a t) -> p a t", a=2)[:, :, 0:n]

            def project(B):
                it, n, w = B.it, B.n, min(B.n, P)
                for t, (g, i, c, f) in enumerate(TILES):
                    if i == 0:
                        s_wi[g % 2].wait(pe, it, loads_of_slot(g))
                    if t >= 4:
                        q = t - 4
                        if q in ACT_TILES:
                            s_pa.wait(pe, it, ACT_TILES.index(q) + 1)
                        else:
                            s_pv.wait(pe, it, DVE_TILES.index(q) + 1)
                    for k in range(KD):
                        last = mm(PP[t % 4][0:f, 0:n], win[:, g % 2, k, c:c + f], hT[:, k, 0:n], k == 0, k == KD - 1)
                    last.then_inc(s_pj.h, 1)
                    if (t + 1 == NTILES) or TILES[t + 1][0] != g:
                        side = SIDE.get(GROUPS[g][0])
                        if side:
                            side(B)

            def lora(B):
                s_th.wait(pe, B.it, 1)
                for r0, bank in ((0, 4), (64, 5)):
                    for p in range(2):
                        last = mm(halves(bank, B.n)[:, p, :], w2a2[r0:r0 + 64, p * P:(p + 1) * P],
                                  pr[r0:r0 + 64, 6, 1:1 + B.n])
                last.then_inc(s_lo.h, 1)

            def key_norms(B):
                s_sq.wait(pe, B.it, 1)
                mm(halves(6, B.n), bones, T2[:, :, 0:B.n]).then_inc(s_sqd.h, 1)

            def latent_norms(B):
                s_nq.wait(pe, B.it, 1)
                mm(PP[7][:, 0:B.n], ones, sqn[:, 0, 0:B.n])
                mm(PP[7][:, T:T + B.n], ones, sqn[:, 1, 0:B.n], True, False)
                mm(PP[7][:, T:T + B.n], ones, sqn[:, 2, 0:B.n], False, True).then_inc(s_nqd.h, 1)

            def bonus(B):
                s_bo.wait(pe, B.it, 1)
                mm(halves(6, B.n), bones, T2[:, :, 0:B.n]).then_inc(s_bod.h, 1)

            def queries(B):
                n = B.n
                s_qn.wait(pe, B.it, 1)
                s_lor.wait(pe, B.it, 1)
                for c0, m, bank in ((NOPE, RD, 4), (0, NOPE, 6)):
                    if bank == 6:
                        s_bor.wait(pe, B.it, 1)
                    for h in range(NH):
                        for t in range(2):
                            last = mm(PP[bank + h // 2][0:m, (h % 2) * T:(h % 2) * T + n],
                                      wuq[:, t, h * 96 + c0:h * 96 + c0 + m], qd[:, t, 0:n], t == 0, t == 1)
                    last.then_inc(s_qp.h, 1)

            def latent_queries(B):
                n = B.n
                s_qpr.wait(pe, B.it, 2)
                for h in range(NH):
                    last = mm(PP[4 + h // 2][:, (h % 2) * T:(h % 2) * T + n], wukT[:, h, :], qnp[:, h, 0:n])
                last.then_inc(s_ql.h, 1)
                for i in range(2):
                    last = mm(halves(6 + i, n, RD), K("rot", m=RD), qr[:, 2 * i:2 * i + 2, 0:n])
                last.then_inc(s_ql.h, 1)

            def latents(B):
                w = min(B.n, P)
                s_qla.wait_alone(pe, B.it, 1)
                mm(PP[4][0:RD, 0:B.n], K("rot", m=RD), krr[:, 0:B.n]).then_inc(s_kr.h, 1)
                for j in range(B.tiles):
                    last = tr(PP[5][0:w, j * P:j * P + P], ckr[:, j * P:j * P + w], P)
                last.then_inc(s_kr.h, 1)

            def rotary_rows(B):
                w = min(B.n, P)
                s_qlr.wait_alone(pe, B.it, 1)
                s_krr.wait(pe, B.it, 1)
                for j in range(B.tiles):
                    last = tr(PP[6][0:w, j * RD:(j + 1) * RD], krr[:, j * P:j * P + w], RD)
                last.then_inc(s_kn.h, 1)

            SIDE = dict(ckv=lora, qd=key_norms, mq=latent_norms, cx=bonus, cc=queries, cb=latent_queries,
                        cg=latents, rg=rotary_rows)

            def rwkv_chunks(B):
                ip = B.ip
                s_rt.wait(pe, B.it, 1)
                s_pv.wait(pe, B.it, len(DVE_TILES))
                s_kvd.wait(pe, B.it, 1)
                s_coe.wait(pe, B.it, 1)
                for j in range(2):
                    J = slice(j * P, (j + 1) * P)
                    for p in range(2):
                        if j:
                            s_yr.wait(pe, ip, p + 1)
                        tr(PP[4 + p][:, 0:P], pr[:, 4 + p, 1 + j * P:1 + (j + 1) * P], P)
                        tr(PP[4 + p][:, P:2 * P], Kt[:, p, J], P)
                        tr(PP[4 + p][:, 2 * P:3 * P], Bp[:, p, J], P).then_inc(s_nt.h, 1)
                    for p in range(2):
                        for h in range(2):
                            q = slice(64 * h, 64 * h + 64)
                            mm(PP[2 * p + h][:, 0:T], Bp[q, p, J], KR[q, p, j, :, :])
                            mm(PP[2 * p + h][:, T:2 * T], Kt[q, p, J], KR[q, p, j, :, :])
                            last = mm(PP[6 + h][:, p * P:(p + 1) * P], KR[q, p, j, 0, :], Bp[q, p, J])
                        last.then_inc(s_gr.h, 1)
                    for lev in range(5):
                        for p in range(2):
                            s_om.wait(pe, ip, j * 5 + lev + 1)
                            if lev == 0:
                                s_grr.wait(pe, ip, j + 1)
                            else:
                                s_xxr.wait(pe, ip, (j * 5 + lev - 1) * 2 + p + 1)
                            for h in range(2):
                                last = mm(PP[p][:, h * P:(h + 1) * P], Om[:, 2 * p + h, :], XX[:, 2 * p + h, 0, :])
                            last.then_inc(s_q.h, 1)
                        for p in range(2):
                            s_qrd.wait(pe, ip, (j * 5 + lev) * 2 + p + 1)
                            for h in range(2):
                                q = 2 * p + h
                                last = mm(PP[2 + p][:, h * T:h * T + P], XX[:, q, 1, :], Qs[:, q, :])
                                if lev < 4:
                                    last = mm(PP[2 + p][:, h * T + P:(h + 1) * T], Qs[:, q, :], XX[:, q, 1, :])
                            last.then_inc(s_xx.h, 1)
                    for c in range(2):
                        n0 = (j * 2 + c) * 2
                        Q = slice(64 * c, 64 * c + 64)
                        for p in range(2):
                            if n0:
                                s_sur.wait(pe, ip, n0 - 2 + p + 1)
                            if c == 0:
                                s_ntr.wait(pe, ip, j * 2 + p + 1)
                                s_xxr.wait(pe, ip, (j * 5 + 4) * 2 + p + 1)
                            mm(PP[p][Q, 0:P], KR[:, p, j, 0, Q], BD[:, p, :], True, False)
                            for h in range(2):
                                last = mm(PP[p][Q, 64 * h:64 * h + 64], G[:, 2 * p + h, 2, Q],
                                          nat[:, p, 0, 64 * h:64 * h + 64], False, h == 1)
                            last.then_inc(s_x0.h, 1)
                        for p in range(2):
                            mm(PP[4 + p][:, Q], BD[:, p, :], KR[:, p, j, 1, Q], c == 0, False)
                        for p in range(2):
                            s_x0r.wait(pe, ip, n0 + p + 1)
                            for h in range(2):
                                last = mm(PP[p][Q, P + 64 * h:P + 64 * h + 64], XX[:, 2 * p + h, 0, Q],
                                          X0[:, p, 64 * h:64 * h + 64])
                            last.then_inc(s_sa.h, 1)
                        for p in range(2):
                            s_sar.wait(pe, ip, n0 + p + 1)
                            mm(PP[2 + p][:, 0:P], nat[Q, p, 1, :], nat[Q, p, 0, :], True, False)
                            mm(PP[2 + p][:, 0:P], nat[Q, p, 2, :], SA[Q, p, :], False, True)\
                                .then_inc(s_su.h, 1)
                    for p in range(2):
                        for h in range(2):
                            q = slice(64 * h, 64 * h + 64)
                            mm(PP[4 + p][q, 0:P], nat[:, p, 0, q], G[:, 2 * p + h, 3, :], False, False)
                            last = mm(PP[4 + p][q, 0:P], SA[:, p, q], G[:, 2 * p + h, 1, :], False, h == 1)
                        last.then_inc(s_y.h, 1)

            def attention(B, l, m, e):
                s_lvr.wait_alone(pe, B.it, 1)
                with pe.Fori(0, m + 1) as kc:
                    n0 = pe.snap(steps_before(l, m, e) + kc * 8)

                    def scores(s):
                        j, h = s // NH, s % NH
                        if s >= 2:
                            pe.wait_ge(s_am.h, n0 + (s - 1))
                        mm(PP[s % 2][:, :], ql[:, h, j * P:(j + 1) * P], ckvT[:, bass.ds(kc * KC, KC)], True, False)
                        mm(PP[s % 2][:, :], qr2[:, h, j * P:(j + 1) * P], krT[:, bass.ds(kc * KC, KC)], False, True)\
                            .then_inc(s_as.h, 1)

                    def turn(s):
                        pe.wait_ge(s_ae.h, n0 + (s + 1))
                        if s >= 2:
                            pe.wait_ge(s_ar.h, n0 + (s - 1))
                        for i in range(4):
                            last = tr(PP[2 + s % 2][:, i * P:(i + 1) * P], Sm[:, s % 2, i * P:(i + 1) * P], P)
                        last.then_inc(s_at.h, 1)

                    def values(s):
                        pe.wait_ge(s_ar.h, n0 + (s + 1))
                        pe.wait_ge(s_ao.h, n0 + max(s - 1, 0) + s_ao.base)
                        for i in range(4):
                            last = mm(PP[4 + s % 2][:, 0:R], PT[:, s % 2, i, :], ckvN[:, bass.ds(kc * 4 + i, 1), :],
                                      i == 0, i == 3)
                        last.then_inc(s_av.h, 1)
                    scores(0)
                    for s in range(8):
                        if s < 7:
                            scores(s + 1)
                        turn(s)
                        if s:
                            values(s - 1)
                    values(7)

            def attention_out(B):
                if B.prompt:
                    s_on.wait(pe, B.ip, 1)
                    for j in range(2):
                        for h in range(NH):
                            last = tr(PP[6 + j][:, h * P:(h + 1) * P], OO[:, j * NH + h, :], P)
                    last.then_inc(s_ot.h, 1)
                s_otr.wait(pe, B.it, 1)
                for h in range(NH):
                    last = mm(PP[4 + h // 2][64 * (h % 2):64 * (h % 2) + 64, 0:B.n], wuv[:, 64 * h:64 * h + 64],
                              OT[:, h, 0:B.n])
                last.then_inc(s_uv.h, 1)

            def memory(B):
                for j in range(2):
                    J = slice(j * P, (j + 1) * P)
                    if j:
                        s_mn.wait(pe, B.ip, j)
                    for h in range(2):
                        q = slice(64 * h, 64 * h + 64)
                        for p in range(2):
                            last = mm(PP[h][:, p * NM:(p + 1) * NM], mq[q, p, J], memKT[q, p, :])
                    last.then_inc(s_ms.h, 1)
                    s_mn.wait(pe, B.ip, j + 1)
                    for q in range(4):
                        for t in range(2):
                            last = tr(PP[2 + q // 2][:, (q % 2) * T + t * P:(q % 2) * T + (t + 1) * P],
                                      Sm4[:, q, t * P:(t + 1) * P], P)
                    last.then_inc(s_mt.h, 1)
                    s_mtr.wait(pe, B.ip, j + 1)
                    for h in range(2):
                        for p in range(2):
                            for t in range(2):
                                last = mm(PP[6][64 * h:64 * h + 64, p * T + j * P:p * T + (j + 1) * P],
                                          memV[:, t, (2 * p + h) * 64:(2 * p + h) * 64 + 64],
                                          PT[:, h, 2 * p + t, :], t == 0, t == 1)
                last.then_inc(s_mo.h, 1)

            def group_norm(B, part):
                if part == 0:
                    if B.prompt:
                        s_yr.wait(pe, B.ip, 4)
                    else:
                        s_sy.wait(pe, B.l, 1)
                    mm(halves(6, B.n), bones, yy[:, :, 0:B.n]).then_inc(s_lm.h, 1)
                else:
                    s_lc.wait(pe, B.it, 1)
                    mm(halves(0, B.n), bones, T2[:, :, 0:B.n]).then_inc(s_lv.h, 1)

            def project_out(B):
                w = min(B.n, P)
                s_mix.wait(pe, B.it, 1)
                for k in range(KD):
                    s_wo[k % 2].wait(pe, B.it, 16 * (k // 2 + 1))
                    for j in range(B.tiles):
                        for i in range(2):
                            last = mm(PP[2 * j + i][0:w, :], mix[:, k, j * P:j * P + w], wout[:, k % 2, i * 512:(i + 1) * 512],
                                      k == 0, k == KD - 1)
                    last.then_inc(s_wou.h, 1)

            def prompt_states(l):
                tr(PP[4][0:7, 0:P], halo[:, :], P)
                for p in range(2):
                    tr(PP[4][0:2, P + p * P:P + (p + 1) * P], u[:, p, 0:2], P)
                    last = tr(PP[5][:, p * P:(p + 1) * P], BD[:, p, :], P)
                last.then_inc(s_fp.h, 1)

            def sample_rwkv(l):
                s_pv.wait(pe, l * IT + NB, len(DVE_TILES))
                for i in range(5):
                    s_se.wait(pe, l, i + 1)
                    for q in range(2):
                        last = mm(PP[2 * (i % 2) + q][:, :], bones, xn[:, q * 512:(q + 1) * 512])
                    last.then_inc(s_sb.h, 1)
                for i in range(7):
                    tr(PP[4 + i // 4][0:NS, (i % 4) * P:(i % 4 + 1) * P], raw[:, i, :], P)
                for p in range(2):
                    last = tr(PP[7][0:NS, p * P:(p + 1) * P], u[:, p, 2:2 + NS], P)
                last.then_inc(s_sr.h, 1)

            def sample_attention(l):
                s_dp.wait(pe, l, 1)
                s_lvr.wait(pe, l * IT + NB, 1)
                mm(PP[4][:, 0:32], K("rep", m=RD), qr2[:, :, 0:NS])
                mm(PP[4][:, 64:96], ones, T1f[:, 0:32], True, False)
                mm(PP[4][:, 64:96], ones[0:RD, :], T3f[0:RD, 0:32], False, True).then_inc(s_dq.h, 1)
                s_dqr.wait_alone(pe, l, 1)
                with pe.Fori(0, NS) as b:
                    n = pe.snap(l * NS + b)
                    pe.wait_ge(s_dg.h, n * 32 + 32)

                    def keys(g):
                        if g >= 2:
                            pe.wait_ge(s_dtr.h, n * 8 + (g - 1) + s_dtr.base)
                            pe.wait_ge(s_dtv.h, n * 8 + (g - 1) + s_dtv.base)
                        else:
                            pe.wait_ge(s_dtr.h, n * 8 + s_dtr.base)
                            pe.wait_ge(s_dtv.h, n * 8 + s_dtv.base)
                        for i in range(4):
                            tr(PP[g % 2][:, i * P:(i + 1) * P], kvg[:, 4 * g + i, :], P)
                        tr(PP[2 + g % 2][:, 0:P], krg[:, g * P:(g + 1) * P], P).then_inc(s_dt.h, 1)

                    def score(g):
                        pe.wait_ge(s_dtr.h, n * 8 + (g + 1) + s_dtr.base)
                        pe.wait_ge(s_dtv.h, n * 8 + (g + 1) + s_dtv.base)
                        mm(PP[5][:, 16 * g:16 * g + 16], T2f[:, (g % 2) * P:(g % 2) * P + P], QR4[:, bass.ds(b, 1), :], True, False)
                        for i in range(4):
                            last = mm(PP[5][:, 16 * g + 4 * i:16 * g + 4 * i + 4], PT[:, g % 2, i, :],
                                      ql[:, :, bass.ds(b, 1)], False, i == 3)
                        last.then_inc(s_ds.h, 1)
                    keys(0)
                    for g in range(8):
                        if g < 7:
                            keys(g + 1)
                        score(g)
                    pe.wait_ge(s_de.h, n + 1)
                    mm(PP[6][:, 64:68], ones, st[:, 16:20])
                    for i in range(32):
                        last = mm(PP[6][:, 0:4], kvg[:, i, :], Pb[:, 4 * i:4 * i + 4], i == 0, i == 31)
                    last.then_inc(s_dv.h, 1)
                    pe.wait_ge(s_da.h, n + 1)

            def sample_memory(l):
                for p in range(2):
                    s_qe.wait(pe, l, p + 1)
                    for q in range(2):
                        last = mm(PP[2 * p + q][:, :], ones, xn[:, q * 512:(q + 1) * 512])
                    last.then_inc(s_qb.h, 1)
                for q in range(2):
                    s_dme.wait(pe, l, q + 1)
                    mm(PP[7][:, 0:32], ones, Pb[:, 0:32])
                    for b in range(4):
                        for p in range(2):
                            for t in range(2):
                                c = (b * 2 + p) * 2
                                last = mm(PP[6][:, c:c + 2], dmv[:, b, t, p * P:(p + 1) * P],
                                          Pb[:, (b * 2 + t) * 4 + 2 * p:(b * 2 + t) * 4 + 2 * p + 2], t == 0, t == 1)
                    last.then_inc(s_dmo.h, 1)
                    s_dm.wait(pe, l, q + 1)

            pe.wait_ge(s_const.h, 32)
            with pe.Fori(0, L) as l:
                s_lw.wait_alone(pe, l, s_lw.n)
                mm(PP[7][:, 0:NVEC], vecrow[:, :], ident[0:NVEC, 0:NVEC])
                for h in range(NH):
                    tr(PP[6][0:64, h * P:(h + 1) * P], wukn[:, h * 64:(h + 1) * 64], P)
                for i in range(7):
                    tr(PP[5][:, i * NS:(i + 1) * NS], shn[:, i * P:(i + 1) * P], NS)
                for p in range(2):
                    last = tr(PP[5][:, 64 + 16 * p:80 + 16 * p], cvn[:, p * P:(p + 1) * P], 16)
                last.then_inc(s_vt.h, 1)
                transpose_rows(s_mem["xn"], s_mem["tp"], l, 2, P, 1)
                s_mw.wait(pe, l, s_mw.n)
                s_mem["hT"].wait(pe, l, 1)
                wm = kv[:, 0:4096].rearrange("p (k n) -> p k n", k=KD)
                for j in range(2):
                    for k in range(KD):
                        last = mm(PP[4 + j][:, :], hT[:, k, j * P:(j + 1) * P], wm[:, k, :], k == 0, k == KD - 1)
                    last.then_inc(s_mem["kv"].h, 1)
                s_mem["kvr"].wait(pe, l, 1)
                for p in range(2):
                    for j in range(2):
                        last = tr(PP[6][:, p * T + j * P:p * T + (j + 1) * P], T1[:, j, p * P:(p + 1) * P], P)
                last.then_inc(s_mem["kt"].h, 1)

                def block(B, m, e):
                    transpose_rows(s_xn, s_xt, B.it, 2, P, 1)
                    s_hT.wait(pe, B.it, 1)
                    project(B)
                    rwkv_chunks(B)
                    group_norm(B, 0)
                    group_norm(B, 1)
                    attention(B, l, m, e)
                    attention_out(B)
                    memory(B)
                    project_out(B)
                prompt_loop(lambda: pe, block, l)
                B = Block(l, None)
                prompt_states(l)
                s_fpr.wait_alone(pe, l, 1)
                transpose_rows(s_xn, s_xt, B.it, 1, NS, 2)
                s_hT.wait(pe, B.it, 1)
                project(B)
                sample_rwkv(l)
                group_norm(B, 0)
                group_norm(B, 1)
                sample_attention(l)
                attention_out(B)
                sample_memory(l)
                project_out(B)

        @blk.vector
        def _(v):
            def drain():
                v.drain()

            def scalars(ap, n):
                return ap.unsqueeze(2).broadcast_to([ap.shape[0], ap.shape[1], n])

            def inverse_roots(want, done, last, it, upto, k=1):
                last.then_inc(want.h, k)
                done.wait(v, it, upto)

            def normalise_rows(sums, ready, turned, want, done, it, tiles, w, k):
                for j in range(tiles):
                    sums.wait(v, it, (j + 1) if tiles == 2 else 2)
                    if j:
                        turned.wait(v, it, j)
                    last = v.tensor_scalar(st[0:w, 4 + j:5 + j], st[0:w, j:j + 1], 1.0 / D, EPS, MULT, ADD)
                    inverse_roots(want, done, last, it, (j + 1) * k, k)
                    v.tensor_scalar(xn[0:w, :], xin[0:w, j, :], st[0:w, 4 + j:5 + j], None, MULT).then_inc(ready.h, k)

            def halves(bank, n, parts=P):
                return PP[bank][0:parts, :].rearrange("p (a t) -> p a t", a=2)[:, :, 0:n]

            def take_h(turned, ready, it, gain, n):
                turned.wait(v, it, 2)
                for i in range(4):
                    last = v.tensor_tensor(hT[:, 2 * i:2 * i + 2, 0:n], halves(i, n), scalars(V(gain, 2 * i, 2), n), MULT)
                last.then_inc(ready.h, 1)

            def shift(B, a0, a1, seen):
                n = B.n
                s_pa.wait(v, B.it, seen)
                cur = pr[:, a0:a1, 1:1 + n]
                d = T3[:, 0:a1 - a0, 0:n]
                if B.prompt:
                    v.tensor_copy(halo[:, a0:a1], pr[:, a0:a1, n:n + 1].rearrange("p a o -> p (a o)"))
                    v.tensor_tensor(d, pr[:, a0:a1, 0:n], cur, SUB)
                else:
                    v.tensor_copy(raw[:, a0:a1, :], cur)
                    v.tensor_tensor(d, shs[:, a0:a1, 0:n], cur, SUB)
                drain()
                v.tensor_tensor(d, d, scalars(V("mu", a0, a1 - a0), n), MULT)
                drain()
                last = v.tensor_tensor(cur, cur, d, ADD)
                if B.prompt:
                    last = v.tensor_copy(pr[:, a0:a1, 0:1], halo[:, a0:a1].unsqueeze(2))
                last.then_inc(s_shift.h, 1)
                drain()

            def rwkv_prepare(B):
                it, n = B.it, B.n
                kx, rx, vx = (pr[:, i:i + 2, 1:1 + n] for i in (2, 0, 4))
                t1, t2, t3, s_, a_ = (t[:, :, 0:n] for t in (T1, T2, T3, sw, aa))
                shift(B, 6, 7, 1)
                shift(B, 2, 4, 3)
                v.tensor_tensor(t1, kx, scalars(V("kk", 0, 2), n), MULT)
                drain()
                v.tensor_tensor(t2, t1, t1, MULT).then_inc(s_sq.h, 1)
                shift(B, 0, 2, 5)
                shift(B, 4, 6, 7)
                s_lor.wait(v, it, 1)
                v.tensor_scalar(s_, s_, 1.0, None, ADD)
                v.tensor_scalar(a_, a_, 1.0, None, ADD)
                drain()
                v.reciprocal(s_, s_)
                last = v.reciprocal(a_, a_)
                drain()
                if B.prompt:
                    for p in range(2):
                        v.tensor_tensor_scan(Ls[:, p, :], K("scan"), sw[:, p, :], 0.0, MULT, ADD)
                    drain()
                    last = v.tensor_tensor(T3[:, :, :], Ls[:, :, :], sw[:, :, :], SUB)
                    last.then_inc(s_sg.h, 1)
                else:
                    v.tensor_copy(Ls[:, :, 0:n], s_).then_inc(s_sg.h, 1)
                s_pa.wait(v, it, 11)
                v.tensor_tensor(sqn[:, 0, 0:n], ckr[:, 0:n], ckr[:, 0:n], MULT)
                v.tensor_tensor(sqn[:, 1:3, 0:n], qd[:, :, 0:n], qd[:, :, 0:n], MULT).then_inc(s_nq.h, 1)
                s_sqd.wait(v, it, 1)
                v.tensor_scalar(t2, halves(6, n), 1e-12, None, ADD)
                s_nqd.wait(v, B.it, 1)
                v.tensor_scalar(sqn[:, 0, 0:n], PP[7][:, 0:n], 1.0 / R, EPS, MULT, ADD)
                v.tensor_scalar(sqn[:, 1, 0:n], PP[7][:, T:T + n], 1.0 / 256, EPS, MULT, ADD).then_inc(s_rw.h, 1)
                s_rd.wait(v, it, 1)
                v.reciprocal(t2, t2)
                v.reciprocal(sqn[:, 0:2, 0:n], sqn[:, 0:2, 0:n])
                drain()
                v.tensor_tensor(t1, t1, t2, MULT)
                drain()
                for p in range(2):
                    v.tensor_scalar(T2[:, p, 0:n], aa[:, p, 0:n], -1.0, V("ka", p), ADD, MULT)
                drain()
                v.scalar_tensor_tensor(kx, t2, 1.0, kx, ADD, MULT)
                drain()
                v.tensor_tensor(t2, rx, kx, MULT)
                drain()
                v.tensor_tensor(t2, t2, scalars(V("rk", 0, 2), n), MULT).then_inc(s_bo.h, 1)
                b_ = Bp[:, :, 0:n]
                v.tensor_tensor(b_, t1, a_, MULT)
                s_dec.wait_alone(v, it, 1)
                if B.prompt:
                    drain()
                    v.tensor_tensor(b_, b_, eN[:, :, :], MULT)
                    v.tensor_tensor(Kt[:, :, :], kx, eN[:, :, :], MULT)
                    tt = lambda t: t.rearrange("p a (j t) -> p a j t", j=2)
                    v.tensor_tensor(KR[:, :, :, 0, :], tt(T1[:, :, :]), tt(eK[:, :, :]), MULT)
                    last = v.tensor_tensor(KR[:, :, :, 1, :], tt(rx), tt(eP[:, :, :]), MULT)
                else:
                    drain()
                    last = v.tensor_copy(Ls[:, :, 0:n], t1)
                last.then_inc(s_rt.h, 1)
                drain()

            def latents(B):
                n = B.n
                v.scalar_tensor_tensor(ckr[:, 0:n], ckr[:, 0:n], V("kn"), sqn[:, 0, 0:n], MULT, MULT)
                for t in range(2):
                    last = v.scalar_tensor_tensor(qd[:, t, 0:n], qd[:, t, 0:n], V("qn", t), sqn[:, 1, 0:n], MULT, MULT)
                last.then_inc(s_qn.h, 1)
                drain()
                if B.prompt:
                    v.tensor_scalar(ckvT[:, bass.ds(B.tok, n)], ckr[:, 0:n], 1.0, None, MULT)
                s_bod.wait(v, B.it, 1)
                v.tensor_tensor(bon[:, :, 0:n], halves(6, n), pr[:, 4:6, 1:1 + n], MULT).then_inc(s_bor.h, 1)

            def convolution(B):
                n, it = B.n, B.it
                t0 = DVE_TILES[0]
                s_pa.wait(v, it, 15)
                for p in range(2):
                    s_pj.wait(v, it, t0 + p + 1)
                    v.tensor_tensor(u[:, p, 2:2 + n], PP[(t0 + p) % 4][:, 0:n], cxs[:, p, 0:n], MULT).then_inc(s_pv.h, 1)
                drain()
                for p in range(2):
                    taps = [u[:, p, 0:n], u[:, p, 1:1 + n]] if B.prompt else [cvs[:, p, :, 0], cvs[:, p, :, 1]]
                    v.tensor_scalar(T3[:, p, 0:n], taps[0], V("conv", p), None, MULT)
                    drain()
                    v.scalar_tensor_tensor(T3[:, p, 0:n], taps[1], V("conv", 2 + p), T3[:, p, 0:n], MULT, ADD)
                    drain()
                    v.scalar_tensor_tensor(T3[:, p, 0:n], u[:, p, 2:2 + n], V("conv", 4 + p), T3[:, p, 0:n], MULT, ADD)
                if B.prompt:
                    drain()
                    v.tensor_copy(u[:, :, 0:2], u[:, :, n:n + 2])
                drain()
                for p in range(2):
                    t = DVE_TILES[2 + p]
                    s_pj.wait(v, it, t + 1)
                    v.tensor_tensor(mix[:, p, 0:n], PP[t % 4][:, 0:n], T3[:, p, 0:n], MULT).then_inc(s_pv.h, 1)

            def gates(B, which, dst):
                n = B.n
                for p in range(2):
                    i = 2 * which + p
                    t = DVE_TILES[4 + i]
                    g = ge[:, i % 2, 0:n]
                    s_ge.wait(v, B.it, i + 1)
                    v.tensor_scalar(g, g, 1.0, None, ADD)
                    drain()
                    v.reciprocal(g, g)
                    drain()
                    if which == 0:
                        v.tensor_tensor(g, g, PP[t % 4][:, 0:n], MULT)
                        drain()
                        v.tensor_tensor(mix[:, p, 0:n], mix[:, p, 0:n], g, MULT).then_inc(s_pv.h, 1)
                    else:
                        v.tensor_tensor(mix[:, dst + p, 0:n], g, PP[t % 4][:, 0:n], MULT).then_inc(s_pv.h, 1)

            def rotate_queries(B):
                n = B.n
                cos, sin = (cs[:, i:i + 1, 0:n].broadcast_to([RD, NH, n]) for i in range(2))
                s_cs.wait(v, B.it, 16)
                s_ql.wait(v, B.it, 2)
                s_qpr.wait(v, B.it, 2)
                tmp = OT[0:RD, :, 0:n]
                for i in range(2):
                    v.tensor_tensor(OT[0:RD, 2 * i:2 * i + 2, 0:n], halves(6 + i, n, RD),
                                    cs[:, 1:2, 0:n].broadcast_to([RD, 2, n]), MULT)
                v.tensor_tensor(qr2[:, :, 0:n], qr[:, :, 0:n], cos, MULT)
                drain()
                v.tensor_tensor(qr2[:, :, 0:n], qr2[:, :, 0:n], tmp, ADD).then_inc(s_qlr.h, 1)

            def store_latents(B):
                n = B.n
                s_kr.wait(v, B.it, 1)
                v.tensor_tensor(T3[0:RD, 0, 0:n], PP[4][0:RD, 0:n], cs[:, 1, 0:n], MULT)
                v.tensor_tensor(krr[:, 0:n], krr[:, 0:n], cs[:, 0, 0:n], MULT)
                drain()
                v.tensor_tensor(krr[:, 0:n], krr[:, 0:n], T3[0:RD, 0, 0:n], ADD).then_inc(s_krr.h, 1)
                drain()
                s_kr.wait(v, B.it, 2)
                if B.prompt:
                    v.tensor_scalar(ckvN[:, bass.ds(B.block * 2, 2), :], PP[5][:, 0:T].rearrange("p (a t) -> p a t", a=2), 1.0, None, MULT)
                    v.tensor_scalar(krT[:, bass.ds(B.tok, n)], krr[:, 0:n], 1.0, None, MULT)
                v.tensor_copy(st[:, 47:48], st[:, 46:47]).then_inc(s_kvd.h, 1)
                drain()

            def rwkv_chunks(B):
                ip = B.ip
                for j in range(2):
                    J = slice(j * P, (j + 1) * P)
                    for p in range(2):
                        s_gr.wait(v, ip, 2 * j + p + 1)
                        for h in range(2):
                            v.tensor_tensor(G[:, 2 * p + h, :, :], PP[2 * p + h][:, :].rearrange("p (a t) -> p a t", a=4), mgram, MULT)
                    for h in range(2):
                        v.tensor_copy(An[:, h:h + 3:2, :], PP[6 + h][:, 0:2 * P].rearrange("p (a t) -> p a t", a=2))
                    drain()
                    v.tensor_tensor(XX[:, :, 0, :], G[:, :, 0, :], K("m1t").unsqueeze(1).broadcast_to([P, NH, P]), MULT)
                    v.tensor_tensor(XX[:, :, 1, :], An[:, :, :], mlev[:, 0:1, :].broadcast_to([P, NH, P]), MULT)
                    drain()
                    xf = XX[:, :, :, :].rearrange("p a b t -> p (a b) t")
                    v.tensor_tensor(xf, ident.unsqueeze(1).broadcast_to([P, 8, P]), xf, SUB).then_inc(s_grr.h, 1)
                    drain()
                    for lev in range(5):
                        n0 = j * 5 + lev
                        if lev:
                            s_q.wait(v, ip, n0 * 2)
                        v.tensor_tensor(Om[:, :, :], An[:, :, :], mlev[:, lev + 1:lev + 2, :].broadcast_to([P, NH, P]), MULT)\
                            .then_inc(s_om.h, 1)
                        for p in range(2):
                            s_xx.wait(v, ip, n0 * 2 + p + 1)
                            k = 2 if lev < 4 else 1
                            x = XX[:, 2 * p:2 * p + 2, 0:k, :]
                            d = PP[2 + p][:, :].rearrange("p (h k t) -> p h k t", h=2, k=2)[:, :, 0:k, :]
                            v.tensor_tensor(x, x, d, SUB).then_inc(s_xxr.h, 1)
                            drain()
                    for c in range(2):
                        Q = slice(64 * c, 64 * c + 64)
                        n0 = (j * 2 + c) * 2
                        for p in range(2):
                            s_x0.wait(v, ip, n0 + p + 1)
                            v.tensor_copy(X0[Q, p, :], PP[p][Q, 0:P]).then_inc(s_x0r.h, 1)
                        for p in range(2):
                            s_sa.wait(v, ip, n0 + p + 1)
                            v.tensor_scalar(SA[Q, p, :], PP[p][Q, P:2 * P], -1.0, None, MULT).then_inc(s_sar.h, 1)
                        for p in range(2):
                            dec = eP[:, p, j * P + c * 64 + 63:j * P + c * 64 + 64]
                            s_su.wait(v, ip, n0 + p + 1)
                            v.scalar_tensor_tensor(BT[:, p, :], PP[2 + p][:, 0:P], dec, bones, MULT, MULT)
                            drain()
                            v.scalar_tensor_tensor(BD[:, p, :], BD[:, p, :], dec, BT[:, p, :], MULT, ADD).then_inc(s_sur.h, 1)
                            drain()
                    for p in range(2):
                        s_y.wait(v, ip, 2 * j + p + 1)
                        v.tensor_copy(yy[:, p, J], PP[4 + p][:, 0:P]).then_inc(s_yr.h, 1)
                drain()

            def centre(B):
                n = B.n
                y = yy[:, :, 0:n]
                s_lm.wait(v, B.it, 1)
                v.scalar_tensor_tensor(y, halves(6, n), -1.0 / HD, y, MULT, ADD)
                drain()
                v.tensor_tensor(T2[:, :, 0:n], y, y, MULT).then_inc(s_lc.h, 1)

            def rwkv_finish(B):
                n = B.n
                y, t = yy[:, :, 0:n], T1[:, :, 0:n]
                s_lv.wait(v, B.it, 1)
                v.tensor_scalar(t, halves(0, n), 1.0 / HD, LN_EPS, MULT, ADD).then_inc(s_rw.h, 1)
                s_rd.wait(v, B.it, 2)
                v.reciprocal(t, t)
                drain()
                v.tensor_tensor(y, y, t, MULT)
                drain()
                for p in range(2):
                    v.tensor_scalar(yy[:, p, 0:n], yy[:, p, 0:n], V("lg", p), V("lb", p), MULT, ADD)
                drain()
                v.tensor_tensor(y, y, bon[:, :, 0:n], ADD)
                drain()
                v.tensor_tensor(mix[:, 2:4, 0:n], mix[:, 2:4, 0:n], y, MULT).then_inc(s_lvr.h, 1)

            def attention_begin(B):
                v.memset(ml[:, 0, :], NEG)
                v.memset(ml[:, 1, :], 0.0)
                v.memset(OO[:, :, :], 0.0).then_inc(s_ai.h, 1)
                drain()

            def attention(B, l, m, e):
                with v.Fori(0, m + 1) as kc:
                    n0 = v.snap(steps_before(l, m, e) + kc * 8)

                    def masked_max(s):
                        j = s // NH
                        o = nc.s_assert_within(FMZ - 128 * j + (kc - m) * KC - e * T, 0, FMZ,
                                               skip_runtime_bounds_check_because="kc is at most m")
                        v.wait_ge(s_at.h, n0 + max(s - 1, 0) + s_at.base)
                        v.wait_ge(s_as.h, n0 + (s + 1))
                        v.tensor_tensor(Sm[:, s % 2, :], PP[s % 2][:, :], fmask[:, bass.ds(o, KC)], ADD).then_inc(s_am.h, 1)
                        drain()
                        v.tensor_reduce(ml[:, 2, s:s + 1], Sm[:, s % 2, :], AX, MAX)
                        drain()
                        v.tensor_tensor(ml[:, 3, s:s + 1], ml[:, 2, s:s + 1], ml[:, 0, s:s + 1], MAX)
                        drain()
                        v.tensor_scalar(ml[:, 4, s:s + 1], ml[:, 3, s:s + 1], -MLA_SCALE, None, MULT)
                        v.tensor_tensor(ml[:, 5, s:s + 1], ml[:, 0, s:s + 1], ml[:, 3, s:s + 1], SUB).then_inc(s_an.h, 1)

                    def sums(s):
                        v.wait_ge(s_ae.h, n0 + (s + 1))
                        v.scalar_tensor_tensor(ml[:, 1, s:s + 1], ml[:, 1, s:s + 1], ml[:, 6, s:s + 1], ml[:, 7, s:s + 1], MULT, ADD)
                        v.tensor_copy(ml[:, 0, s:s + 1], ml[:, 3, s:s + 1])

                    def accumulate(s):
                        v.wait_ge(s_av.h, n0 + (s + 1) + s_av.base)
                        v.scalar_tensor_tensor(OO[:, s, :], OO[:, s, :], ml[:, 6, s:s + 1], PP[4 + s % 2][:, 0:R], MULT, ADD)\
                            .then_inc(s_ao.h, 1)
                    for s in range(8):
                        masked_max(s)
                        if s >= 1:
                            sums(s - 1)
                        if s >= 2:
                            accumulate(s - 2)
                    sums(7)
                    accumulate(6)
                    accumulate(7)
                    drain()
                v.reciprocal(ml[:, 2, :], ml[:, 1, :])
                drain()
                v.tensor_tensor(OO[:, :, :], OO[:, :, :], scalars(ml[:, 2, :], P), MULT).then_inc(s_on.h, 1)

            def gate_attention(B):
                n = B.n
                s_uv.wait(v, B.it, 1)
                for p in range(2):
                    v.tensor_tensor(mix[:, 4 + p, 0:n], mix[:, 4 + p, 0:n], PP[4 + p][:, 0:n], MULT)

            def memory(B):
                for j in range(2):
                    s_ms.wait(v, B.ip, j + 1)
                    for h in range(2):
                        v.tensor_reduce(st[:, 16 + 2 * h:18 + 2 * h], halves(h, T), AX, MAX)
                    drain()
                    v.tensor_scalar(st[:, 20:24], st[:, 16:20], -MEM_SCALE, None, MULT).then_inc(s_mx.h, 1)
                    s_me.wait(v, B.ip, j + 1)
                    v.reciprocal(st[:, 28:32], st[:, 24:28])
                    drain()
                    v.tensor_tensor(Sm4, Sm4, scalars(st[:, 28:32], T), MULT).then_inc(s_mn.h, 1)
                s_mo.wait(v, B.ip, 1)
                v.tensor_tensor(mix[:, 6:8, :], mix[:, 6:8, :], halves(6, T), MULT).then_inc(s_mix.h, 1)

            def residual(B):
                w, it = min(B.n, P), B.it
                s_os.wait(v, it, 1)
                for j in range(B.tiles):
                    r = st[0:w, 32 + j:33 + j]
                    v.tensor_tensor(r, st[0:w, 8 + 2 * j:9 + 2 * j], st[0:w, 9 + 2 * j:10 + 2 * j], ADD)
                    drain()
                    last = v.tensor_scalar(r, r, 1.0 / D, EPS, MULT, ADD)
                    k = 2 // B.tiles
                    inverse_roots(s_pw, s_pr, last, it, 2 + (j + 1) * k, k)
                    for i in range(2):
                        q = slice(i * 512, (i + 1) * 512)
                        v.scalar_tensor_tensor(xn[0:w, q], PP[2 * j + i][0:w, :], r, postg[0:w, q], MULT, MULT)
                    drain()
                    last = v.tensor_tensor(xin[0:w, j, :], xin[0:w, j, :], xn[0:w, :], ADD)
                    if j == B.tiles - 1:
                        last.then_inc(s_of.h, 1)
                    drain()

            def spread(vec3, sig_out, l, i):
                if i >= 1:
                    s_sb.wait(v, l, i)
                e4 = xn[:, :].rearrange("p (b a j) -> p b a j", b=NS, a=2)
                for a_ in range(2):
                    last = v.tensor_tensor(e4[:, :, a_, :], vec3[:, a_, :].unsqueeze(2).broadcast_to([P, NS, 64]),
                                           K("id64").unsqueeze(1).broadcast_to([P, NS, 64]), MULT)
                last.then_inc(sig_out.h, 1)

            def sample_rwkv(l):
                n = NS
                vecs = [eP[:, :, 0:n], Ls[:, :, 0:n], Bp[:, :, 0:n], pr[:, 2:4, 1:1 + n], pr[:, 0:2, 1:1 + n]]
                s_sl.wait(v, l, s_sl.n)
                spread(vecs[0], s_se, l, 0)
                sab = st[:, 0:16]
                for i in range(5):
                    if i < 4:
                        spread(vecs[i + 1], s_se, l, i + 1)
                    s_sb.wait(v, l, i + 1)
                    for q in range(2):
                        rows = PP[2 * (i % 2) + q][:, :].rearrange("p (a j) -> p a j", j=64)
                        s_ = S0[:, 8 * q:8 * q + 8, :]
                        w_ = SW[:, 8 * q:8 * q + 8, :]
                        if i == 0:
                            v.tensor_tensor(SD[:, 8 * q:8 * q + 8, :], s_, rows, MULT)
                        elif i == 1:
                            v.tensor_tensor(w_, s_, rows, MULT)
                            drain()
                            v.tensor_reduce(sab[:, 8 * q:8 * q + 8], w_, AX, ADD)
                            drain()
                        elif i == 2:
                            v.tensor_tensor(w_, rows, scalars(sab[:, 8 * q:8 * q + 8], 64), MULT)
                            drain()
                            v.tensor_tensor(SD[:, 8 * q:8 * q + 8, :], SD[:, 8 * q:8 * q + 8, :], w_, SUB)
                        elif i == 3:
                            for b in range(4):
                                vb = pr[:, 4:6, 1 + 4 * q + b:2 + 4 * q + b].broadcast_to([P, 2, 64])
                                v.tensor_tensor(w_[:, 2 * b:2 * b + 2, :], rows[:, 2 * b:2 * b + 2, :], vb, MULT)
                            drain()
                            v.tensor_tensor(SD[:, 8 * q:8 * q + 8, :], SD[:, 8 * q:8 * q + 8, :], w_, ADD)
                        else:
                            v.tensor_tensor(w_, SD[:, 8 * q:8 * q + 8, :], rows, MULT)
                            drain()
                            v.tensor_reduce(sab[:, 8 * q:8 * q + 8], w_, AX, ADD)
                    if i == 3:
                        drain()
                        v.tensor_copy(st[:, 47:48], st[:, 46:47]).then_inc(s_sst2.h, 1)
                drain()
                v.tensor_copy(yy[:, :, 0:n], sab.rearrange("p (b a) -> p a b", a=2)).then_inc(s_sy.h, 1)
                drain()

            def sample_attention(l):
                n = NS
                f = lambda t: t.rearrange("p (h b) -> p h b", h=NH)
                v.tensor_tensor(f(T1f[:, 0:32]), ql[:, :, 0:n], ckr[:, 0:n].unsqueeze(1).broadcast_to([P, NH, n]), MULT)
                v.tensor_tensor(f(T3f[0:RD, 0:32]), qr2[:, :, 0:n], krr[:, 0:n].unsqueeze(1).broadcast_to([RD, NH, n]), MULT)\
                    .then_inc(s_dp.h, 1)
                s_dq.wait(v, l, 1)
                src = PP[4][:, 0:32].rearrange("p (h b) -> p b h", h=NH)
                for t in range(4):
                    v.tensor_scalar(QR4[:, :, 4 * t:4 * t + 4], src, K("tmask")[:, t:t + 1], None, MULT)
                v.tensor_copy(sns[:, :, :], PP[4][:, 64:96].rearrange("p (h b) -> p b h", h=NH)).then_inc(s_dqr.h, 1)
                drain()
                with v.Fori(0, NS) as b:
                    k = v.snap(l * NS + b)
                    for g in range(8):
                        v.wait_ge(s_dt.h, k * 8 + (g + 1))
                        if g >= 2:
                            v.wait_ge(s_ds.h, k * 8 + (g - 1))
                        v.tensor_copy(T2f[:, (g % 2) * P:(g % 2) * P + P], PP[2 + g % 2][:, 0:P]).then_inc(s_dtv.h, 1)
                    v.wait_ge(s_ds.h, k * 8 + 8)
                    sc = PP[5][:, 0:P].rearrange("p (c h) -> p h c", h=NH)
                    v.tensor_reduce(st[:, 0:4], sc, AX, MAX).then_inc(s_dm1.h, 1)
                    v.wait_ge(s_dm2.h, k + 1)
                    sn = sns[:, bass.ds(b, 1), :].rearrange("p o h -> p (o h)")
                    v.tensor_copy(st[:, 47:48], st[:, 46:47])
                    v.tensor_tensor(st[:, 8:12], st[:, 4:8], sn, MAX)
                    drain()
                    v.tensor_tensor(T1f[:, 0:P].rearrange("p (c h) -> p c h", h=NH), PP[5][:, 0:P].rearrange("p (c h) -> p c h", h=NH),
                                    st[:, 8:12].unsqueeze(1).broadcast_to([P, 32, NH]), SUB)
                    v.tensor_tensor(T1f[:, P:P + 4], sn, st[:, 8:12], SUB).then_inc(s_dx.h, 1)
                    v.wait_ge(s_dxe.h, k + 1)
                    v.tensor_reduce(st[:, 16:20], Pb[:, 0:P].rearrange("p (c h) -> p h c", h=NH), AX, ADD).then_inc(s_de.h, 1)
                    v.wait_ge(s_dv.h, k + 1)
                    v.tensor_tensor(st[:, 20:24], PP[6][:, 64:68], Pb[:, P:P + 4], ADD)
                    drain()
                    v.reciprocal(st[:, 20:24], st[:, 20:24])
                    cn = ckr[:, bass.ds(b, 1)].broadcast_to([P, NH])
                    v.tensor_tensor(st[:, 24:28], Pb[:, P:P + 4], cn, MULT)
                    drain()
                    v.tensor_tensor(st[:, 24:28], st[:, 24:28], PP[6][:, 0:4], ADD)
                    drain()
                    v.tensor_tensor(OT[:, :, bass.ds(b, 1)], st[:, 24:28].unsqueeze(2), st[:, 20:24].unsqueeze(2), MULT).then_inc(s_da.h, 1)
                drain()
                v.tensor_copy(st[:, 47:48], st[:, 46:47]).then_inc(s_otr.h, 1)

            def sample_memory(l):
                for p in range(2):
                    if p:
                        s_qb.wait(v, l, 1)
                    v.tensor_tensor(xn[:, :].rearrange("p (b c) -> p b c", b=NS), mq[:, p, 0:NS].unsqueeze(2).broadcast_to([P, NS, P]),
                                    ident.unsqueeze(1).broadcast_to([P, NS, P]), MULT).then_inc(s_qe.h, 1)
                    s_qb.wait(v, l, p + 1)
                    for q in range(2):
                        v.tensor_copy(qB[:, 4 * q:4 * q + 4, p, :], PP[2 * p + q][:, :].rearrange("p (b c) -> p b c", b=4))
                drain()
                for q in range(2):
                    s_dml.wait(v, l, 128 * (q + 1))
                    qb = qB[:, 4 * q:4 * q + 4, :, :].rearrange("p b a c -> p b (a c)")
                    for t in range(2):
                        v.tensor_tensor(dmp[:, :, t, :], dmk[:, :, t, :], qb, MULT)
                    drain()
                    v.tensor_reduce(st[:, 0:32], dmp[:, :, :, :].rearrange("p b t (h d) -> p (b t h) d", d=HD), AX, ADD)
                    drain()
                    s3 = st[:, 0:32].rearrange("p (b t h) -> p b t h", b=4, t=2)
                    m3 = T1f[:, 0:16].rearrange("p (b h) -> p b h", b=4)
                    v.tensor_tensor(m3, s3[:, :, 0, :], s3[:, :, 1, :], MAX).then_inc(s_dmx.h, 1)
                    s_dmr.wait(v, l, q + 1)
                    g3 = T1f[:, 16:32].rearrange("p (b h) -> p b h", b=4)
                    for t in range(2):
                        last = v.tensor_tensor(s3[:, :, t, :], s3[:, :, t, :], g3, SUB)
                    last.then_inc(s_dms.h, 1)
                    s_dmo.wait(v, l, q + 1)
                    d3 = PP[7][:, 0:32].rearrange("p (b t h) -> p b t h", b=4, t=2)
                    r3 = T1f[:, 32:48].rearrange("p (b h) -> p b h", b=4)
                    v.tensor_copy(r3, d3[:, :, 0, :])
                    drain()
                    v.tensor_tensor(r3, r3, d3[:, :, 1, :], ADD)
                    drain()
                    v.reciprocal(r3, r3)
                    drain()
                    o3 = PP[6][:, 0:16].rearrange("p (b a h) -> p b a h", b=4, a=2)
                    for h in range(2):
                        H = slice(64 * h, 64 * h + 64)
                        rr = T1f[H, 32:48].rearrange("p (b a h) -> p b a h", b=4, a=2)[:, :, :, h]
                        t4 = T1f[H, 48:56].rearrange("p (b a) -> p b a", b=4)
                        v.tensor_tensor(t4, o3[H, :, :, h], rr, MULT)
                        drain()
                        mx = mix[H, 6:8, 4 * q:4 * q + 4].rearrange("p a b -> p b a")
                        v.tensor_tensor(mx, mx, t4, MULT)
                        drain()
                    v.tensor_copy(st[:, 47:48], st[:, 46:47]).then_inc(s_dm.h, 1)
                drain()
                v.tensor_copy(st[:, 47:48], st[:, 46:47]).then_inc(s_mix.h, 1)

            v.memset(st[:, 40:48], 0.0)
            v.memset(krT, 0.0)
            v.memset(X0[:, :, :], 0.0)
            v.memset(SA[:, :, :], 0.0)
            drain()
            v.wait_ge(s_const.h, 32)
            with v.Fori(0, L) as l:
                s_vt.wait(v, l, 1)
                v.tensor_copy(vec[:, :], PP[7][:, 0:NVEC])
                v.tensor_copy(wukT[:, :, :], PP[6][0:64, :].rearrange("p (h r) -> p h r", h=NH))
                v.tensor_copy(shs[:, :, :], PP[5][:, 0:56].rearrange("p (a b) -> p a b", a=7))
                v.tensor_copy(cvs[:, :, :, :], PP[5][:, 64:96].rearrange("p (a b k) -> p a b k", a=2, b=NS))
                v.memset(pr[:, :, 0:1], 0.0)
                v.memset(u[:, :, 0:2], 0.0)
                v.memset(BD[:, :, :], 0.0).then_inc(s_vr.h, 1)
                drain()
                normalise_rows(s_mem["ss"], s_mem["xn"], s_mem["tp"], s_mem["pw"], s_mem["pr"], l, 2, P, 1)
                take_h(s_mem["tp"], s_mem["hT"], l, "mn", T)
                s_mem["kv"].wait(v, l, 2)
                for j in range(2):
                    v.tensor_copy(T1[:, j, :], PP[4 + j][:, 0:256])
                    last = v.tensor_copy(memV[:, j, :], PP[4 + j][:, 256:512])
                last.then_inc(s_mem["kvr"].h, 1)
                s_mem["kt"].wait(v, l, 1)
                v.tensor_copy(memKT[:, :, :], PP[6][:, :].rearrange("p (a m) -> p a m", a=2)).then_inc(s_mem["ktr"].h, 1)
                s_mem["out"].wait(v, l, 64)
                v.tensor_copy(st[:, 47:48], st[:, 46:47])
                drain()

                def begin(B):
                    normalise_rows(s_ss, s_xn, s_xt, s_pw, s_pr, B.it, B.tiles, min(B.n, P), 2 // B.tiles)
                    take_h(s_xt, s_hT, B.it, "pre", B.n)
                    rwkv_prepare(B)
                    latents(B)
                    convolution(B)
                    rotate_queries(B)
                    gates(B, 0, 0)
                    store_latents(B)
                    gates(B, 1, 2)
                    gates(B, 2, 4)
                    gates(B, 3, 6)
                    drain()

                def block(B, m, e):
                    begin(B)
                    rwkv_chunks(B)
                    centre(B)
                    attention_begin(B)
                    rwkv_finish(B)
                    attention(B, l, m, e)
                    gate_attention(B)
                    memory(B)
                    residual(B)
                prompt_loop(lambda: v, block, l)
                B = Block(l, None)
                s_fp.wait(v, l, 1)
                v.tensor_copy(fst[0:7, 0:P], PP[4][0:7, 0:P])
                v.tensor_copy(fst[0:2, P:3 * P], PP[4][0:2, P:3 * P])
                v.tensor_copy(fst[:, 3 * P:5 * P], PP[5][:, 0:2 * P]).then_inc(s_fpr.h, 1)
                begin(B)
                sample_rwkv(l)
                s_sr.wait(v, l, 1)
                for i in range(2):
                    w = 512 if i == 0 else 384
                    v.tensor_copy(shn[:, i * 512:i * 512 + w], PP[4 + i][0:NS, 0:w])
                v.tensor_copy(cvn[0:NS, :], PP[7][0:NS, 0:256]).then_inc(s_srr.h, 1)
                centre(B)
                drain()
                rwkv_finish(B)
                drain()
                sample_attention(l)
                gate_attention(B)
                drain()
                sample_memory(l)
                residual(B)

        @blk.scalar
        def _(act):
            act.wait_ge(s_const.h, 32)
            with nc.allow_non_contiguous_dma(reason="rows of small states"), act.Fori(0, L) as l:
                sl, sn = bass.ds(l, 1), bass.ds(l + 1, 1)

                def squares(sums, it, tiles, w, k):
                    for j in range(tiles):
                        act.activation(junk[0:w, j * D:(j + 1) * D], xin[0:w, j, :], ACT.Square, accum_out=st[0:w, j:j + 1]).then_inc(sums.h, k)
                s_mw.wait(act, l, s_mw.n)
                squares(s_mem["ss"], l, 2, P, 1)
                s_mem["kvr"].wait(act, l, 1)
                for j in range(2):
                    act.dma_start(a["mem_k"][sl, j * P:(j + 1) * P, :].rearrange("a m c -> (a m) c"), T1[:, j, :]).then_inc(s_mem["out"].h, 16)
                    act.dma_start(a["mem_v"][sl, j * P:(j + 1) * P, :].rearrange("a m c -> (a m) c"), memV[:, j, :]).then_inc(s_mem["out"].h, 16)

                def begin(B):
                    it, n, w = B.it, B.n, min(B.n, P)
                    s_x.wait(act, it, 16)
                    squares(s_ss, it, B.tiles, w, 2 // B.tiles)
                    dst = {"wlal": pr[:, 6:7], "k": pr[:, 2:4], "r": pr[:, 0:2], "v": pr[:, 4:6], "qd": qd, "mq": mq, "cx": cxs}

                    def take(name):
                        for t, (g, i, c, f) in enumerate(TILES):
                            if GROUPS[g][0] != name:
                                continue
                            s_pj.wait(act, it, t + 1)
                            if name == "ckv":
                                if i == 0:
                                    s_coe.wait(act, it, 0)
                                o = ckr[:, 0:n] if i == 0 else krr[:, 0:n]
                            elif name in ("wlal", "k", "r", "v"):
                                o = dst[name][:, i, 1:1 + n]
                            else:
                                o = dst[name][:, i, 0:n]
                            act.activation(o, PP[t % 4][0:f, 0:n], ACT.Copy).then_inc(s_pa.h, 1)

                    def halves(bank, m, parts=P):
                        return PP[bank][0:parts, :].rearrange("p (a t) -> p a t", a=2)[:, :, 0:m]
                    take("wlal")
                    s_shift.wait(act, it, 1)
                    act.activation(pr[0:64, 6, 1:1 + n], pr[0:64, 6, 1:1 + n], ACT.Tanh).then_inc(s_th.h, 1)
                    take("k")
                    take("r")
                    take("v")
                    take("ckv")
                    s_lo.wait(act, it, 1)
                    for p in range(2):
                        act.activation(sw[:, p, 0:n], halves(4, n)[:, p, :], ACT.Exp, bias=nvec[:, p:p + 1], scale=-1.0)
                        last = act.activation(aa[:, p, 0:n], halves(5, n)[:, p, :], ACT.Exp, bias=nvec[:, 2 + p:3 + p], scale=-1.0)
                    last.then_inc(s_lor.h, 1)
                    take("qd")
                    s_sg.wait(act, it, 1)
                    act.activation(eP[:, :, 0:n], Ls[:, :, 0:n], ACT.Exp, scale=-DECAY)
                    if B.prompt:
                        act.activation(eN[:, :, :], Ls[:, :, :], ACT.Exp, scale=DECAY)
                        last = act.activation(eK[:, :, :], T3[:, :, :], ACT.Exp, scale=-DECAY)
                    else:
                        last = act.activation(eN[:, :, 0:n], Ls[:, :, 0:n], ACT.Copy)
                    last.then_inc(s_dec.h, 1)
                    take("mq")
                    s_rw.wait(act, it, 1)
                    act.activation(T2[:, :, 0:n], T2[:, :, 0:n], ACT.Sqrt)
                    act.activation(sqn[:, 0:2, 0:n], sqn[:, 0:2, 0:n], ACT.Sqrt).then_inc(s_rd.h, 1)
                    take("cx")
                    s_qp.wait(act, it, 1)
                    for i in range(2):
                        last = act.activation(qr[:, 2 * i:2 * i + 2, 0:n], halves(4 + i, n, RD), ACT.Copy)
                    last.then_inc(s_qpr.h, 1)
                    s_qp.wait(act, it, 2)
                    for i in range(2):
                        last = act.activation(qnp[:, 2 * i:2 * i + 2, 0:n], halves(6 + i, n, 64), ACT.Copy)
                    last.then_inc(s_qpr.h, 1)

                    def gate(i):
                        t = DVE_TILES[4 + i]
                        s_pj.wait(act, it, t + 1)
                        s_pv.wait(act, it, i + 3)
                        act.activation(ge[:, i % 2, 0:n], PP[t % 4][:, 0:n], ACT.Exp, scale=-1.0).then_inc(s_ge.h, 1)
                    s_ql.wait(act, it, 1)
                    for i in range(2):
                        last = act.activation(ql[:, 2 * i:2 * i + 2, 0:n], halves(4 + i, n), ACT.Copy)
                    last.then_inc(s_qla.h, 1)
                    gate(0)
                    gate(1)
                    s_co.wait(act, it, 0)
                    s_kvd.wait(act, it, 1)
                    act.activation(cko[0:w, 0:B.tiles, :], PP[5][0:w, 0:B.tiles * P].rearrange("p (a t) -> p a t", t=P), ACT.Copy)
                    gate(2)
                    gate(3)
                    s_kn.wait(act, it, 1)
                    act.activation(kro[0:w, 0:B.tiles, :], PP[6][0:w, 0:B.tiles * RD].rearrange("p (a t) -> p a t", t=RD), ACT.Copy).then_inc(s_coe.h, 1)
                    s_coe.wait(act, it, 1)
                    for out, src in ((a["ckv"], cko), (a["krope"], kro)):
                        if B.prompt:
                            o = out[sl, bass.ds(B.tok, T), :].rearrange("a (t p) c -> p (a t) c", p=P)
                            act.dma_start(o, src[:, :, :]).then_inc(s_co.h, 16)
                        else:
                            act.dma_start(out[sl, S:S + NS, :].rearrange("a p c -> p (a c)"), src[0:NS, 0, :]).then_inc(s_co.h, 16)
                    for i in range(4, 8):
                        gate(i)

                def finish(B):
                    it, w = B.it, min(B.n, P)
                    s_wou.wait(act, it, KD)
                    for j in range(B.tiles):
                        for i in range(2):
                            last = act.activation(junk[0:w, (2 * j + i) * 512:(2 * j + i + 1) * 512], PP[2 * j + i][0:w, :], ACT.Square,
                                                  accum_out=st[0:w, 8 + 2 * j + i:9 + 2 * j + i])
                    last.then_inc(s_os.h, 1)
                    s_of.wait(act, it, 1)
                    if B.prompt:
                        o = xres[sn, bass.ds(B.tok, T), :].rearrange("a (t p) d -> p (a t) d", p=P)
                        act.dma_start(o, xin[:, :, :]).then_inc(s_od.h, 16)
                    else:
                        act.dma_start(xres[sn, S:S + NS, :].rearrange("a p d -> p (a d)"), xin[0:NS, 0, :]).then_inc(s_od.h, 16)

                def variance_root(B):
                    s_rw.wait(act, B.it, 2)
                    act.activation(T1[:, :, 0:B.n], T1[:, :, 0:B.n], ACT.Sqrt).then_inc(s_rd.h, 1)

                def block(B, m, e):
                    ip = B.ip
                    begin(B)
                    for j in range(2):
                        for p in range(2):
                            s_nt.wait(act, ip, 2 * j + p + 1)
                            act.activation(nat[:, p, :, :], PP[4 + p][:, 0:3 * P].rearrange("p (a t) -> p a t", t=P), ACT.Copy).then_inc(s_ntr.h, 1)
                        for lev in range(5):
                            for p in range(2):
                                k = (j * 5 + lev) * 2 + p + 1
                                s_q.wait(act, ip, k)
                                if k > 2:
                                    s_xx.wait(act, ip, k - 2)
                                act.activation(Qs[:, 2 * p:2 * p + 2, :], PP[p][:, 0:T].rearrange("p (a t) -> p a t", t=P), ACT.Copy).then_inc(s_qrd.h, 1)
                    variance_root(B)
                    with act.Fori(0, m + 1) as kc:
                        n0 = act.snap(steps_before(l, m, e) + kc * 8)

                        def probs(s):
                            act.wait_ge(s_an.h, n0 + (s + 1))
                            act.activation(Sm[:, s % 2, :], Sm[:, s % 2, :], ACT.Exp, bias=ml[:, 4, s:s + 1],
                                           scale=MLA_SCALE, accum_out=ml[:, 7, s:s + 1])
                            act.activation(ml[:, 6, s:s + 1], ml[:, 5, s:s + 1], ACT.Exp, scale=MLA_SCALE).then_inc(s_ae.h, 1)

                        def take(s):
                            act.wait_ge(s_at.h, n0 + (s + 1) + s_at.base)
                            act.wait_ge(s_av.h, n0 + max(s - 1, 0) + s_av.base)
                            act.activation(PT[:, s % 2, :, :], PP[2 + s % 2][:, :].rearrange("p (a t) -> p a t", a=4), ACT.Copy).then_inc(s_ar.h, 1)
                        probs(0)
                        for s in range(8):
                            if s < 7:
                                probs(s + 1)
                            take(s)
                    s_ot.wait(act, ip, 1)
                    for j in range(2):
                        last = act.activation(OT[:, :, j * P:(j + 1) * P], PP[6 + j][:, :].rearrange("p (h t) -> p h t", h=NH), ACT.Copy)
                    last.then_inc(s_otr.h, 1)
                    for j in range(2):
                        s_mx.wait(act, ip, j + 1)
                        for q in range(4):
                            last = act.activation(Sm4[:, q, :], PP[q // 2][:, (q % 2) * T:(q % 2) * T + T], ACT.Exp,
                                                  bias=st[:, 20 + q:21 + q], scale=MEM_SCALE, accum_out=st[:, 24 + q:25 + q])
                        last.then_inc(s_me.h, 1)
                        s_mt.wait(act, ip, j + 1)
                        for q in range(2):
                            last = act.activation(PT[:, q, :, :], PP[2 + q][:, :].rearrange("p (a t) -> p a t", a=4), ACT.Copy)
                        last.then_inc(s_mtr.h, 1)
                    finish(B)
                s_vr.wait(act, l, 1)
                act.mul(nvec[:, 0:2], V("w0", 0, 2), -1.0)
                act.mul(nvec[:, 2:4], V("a0", 0, 2), -1.0)
                act.drain()
                prompt_loop(lambda: act, block, l)
                s_fpr.wait(act, l, 1)
                act.dma_start(a["shift_p"][sl, :].rearrange("a (n p) -> (a n) p", p=P), fst[0:7, 0:P]).then_inc(s_state.h, 16)
                act.dma_start(a["conv_p"][sl].rearrange("a k c -> (a k) c"), fst[0:2, P:3 * P]).then_inc(s_state.h, 16)
                for h in range(NH):
                    q, c = slice(64 * (h % 2), 64 * (h % 2) + 64), 3 * P + (h // 2) * P + 64 * (h % 2)
                    act.dma_start(a["st_p"][sl, h].rearrange("a i j -> (a i) j"), fst[q, c:c + 64]).then_inc(s_state.h, 16)
                B = Block(l, None)
                begin(B)
                variance_root(B)
                s_sst2.wait(act, l, 1)
                for b in range(NS):
                    act.dma_start(a["st_s"][sl, b].rearrange("a (p h) i j -> (h i) (a p) j", p=2), SD[:, 2 * b:2 * b + 2, :]).then_inc(s_state.h, 16)
                s_srr.wait(act, l, 1)
                act.dma_start(a["shift_s"][sl].rearrange("a b c -> (a b) c"), shn[:, :]).then_inc(s_state.h, 16)
                act.dma_start(a["conv_s"][sl, :, 1, :].rearrange("a b c -> (a b) c"), cvn[0:NS, :]).then_inc(s_state.h, 16)
                act.dma_start(a["conv_s"][sl, :, 0, :].rearrange("a b c -> (a b) c"), a["state_conv"][sl, :, 1, :].rearrange("a b c -> (a b) c")).then_inc(s_state.h, 16)
                with act.Fori(0, NS) as b:
                    k = act.snap(l * NS + b)
                    for g in range(8):
                        act.wait_ge(s_dt.h, k * 8 + (g + 1))
                        if g >= 2:
                            act.wait_ge(s_ds.h, k * 8 + (g - 1))
                        act.activation(PT[:, g % 2, :, :], PP[g % 2][:, :].rearrange("p (a t) -> p a t", a=4), ACT.Copy).then_inc(s_dtr.h, 1)
                    act.wait_ge(s_dx.h, k + 1)
                    act.activation(Pb[:, 0:P + 4], T1f[:, 0:P + 4], ACT.Exp, scale=MLA_SCALE).then_inc(s_dxe.h, 1)
                for q in range(2):
                    s_dms.wait(act, l, q + 1)
                    act.activation(Pb[:, 0:32], st[:, 0:32], ACT.Exp, scale=MEM_SCALE).then_inc(s_dme.h, 1)
                finish(B)

        @blk.gpsimd
        def _(pool):
            pool.memset(zero[:, :], 0)
            pool.memset(zerof[:, :], 0.0)
            pool.memset(mhalf[:, :], -0.5)
            pool.drain()
            pool.wait_ge(s_const.h, 32)
            with nc.allow_non_contiguous_dma(reason="page numbers"):
                for b in range(NS):
                    src = a["page_table"][b:b + 1, :].rearrange("a (n o) -> (a n) o", o=1)
                    for s in range(4):
                        pool.dma_start(pgi[s * 32:(s + 1) * 32, b:b + 1], src).then_inc(s_pg.h, 16)
            pool.wait_ge(s_pg.h, 16 * 4 * NS)
            pool.tensor_copy(pgf[:, :], pgi[:, :])
            pool.drain()
            pool.tensor_scalar(pgf[:, :], pgf[:, :], 4.0, K("sub"), MULT, ADD)
            pool.drain()

            def root(want, done, it, n, ap, k=1):
                want.wait_alone(pool, it, n)
                half = mhalf[0:ap.shape[0], :]
                if len(ap.shape) == 3:
                    half = half.unsqueeze(2)
                pool.tensor_tensor(ap, ap, half.broadcast_to(list(ap.shape)), POW).then_inc(done.h, k)

            def norms(B, part):
                w, k = min(B.n, P), 2 // B.tiles
                if part == 0:
                    for j in range(B.tiles):
                        root(s_pw, s_pr, B.it, (j + 1) * k, st[0:w, 4 + j:5 + j], k)
                else:
                    for j in range(B.tiles):
                        root(s_pw, s_pr, B.it, 2 + (j + 1) * k, st[0:w, 32 + j:33 + j], k)
            with pool.Fori(0, L) as l:
                for j in range(2):
                    root(s_mem["pw"], s_mem["pr"], l, j + 1, st[:, 4 + j:5 + j])

                def block(B, m, e):
                    norms(B, 0)
                    norms(B, 1)
                prompt_loop(lambda: pool, block, l)
                B = Block(l, None)
                norms(B, 0)
                pool.tensor_copy(idx[:, :], pgf[:, :])
                pool.drain()
                pool.tensor_scalar(pgf[:, :], pgf[:, :], float(NPHYS * 4), None, ADD)
                pool.drain()
                for b in range(NS):
                    k = l * NS + b
                    if b == 0:
                        s_rt.wait(pool, l * IT + NB, 1)
                    else:
                        pool.wait_ge(s_da.h, k)
                    pool.tensor_tensor(idc[:, 0:1], idx[:, b:b + 1], zero[:, :], ADD)
                    pool.drain()
                    pool.indirect_dma_start(kv[:, 0:4096], None, a["cache_ckv"].rearrange("l n (g k) r -> (l n g) (k r)", g=4),
                                            bass.IndirectOffsetOnAxis(ap=idc[:, 0:1], axis=0)).then_inc(s_dg.h, 16)
                    pool.indirect_dma_start(kv[:, 4096:5120], None, a["cache_krope"].rearrange("l n (g k) r -> (l n g) (k r)", g=4),
                                            bass.IndirectOffsetOnAxis(ap=idc[:, 0:1], axis=0)).then_inc(s_dg.h, 16)
                    pool.wait_ge(s_dm1.h, k + 1)
                    pool.tensor_tensor(st[:, 12:16], st[:, 0:4], zerof[:, 0:4], ADD)
                    pool.drain()
                    pool.partition_all_reduce(st[:, 4:8], st[:, 12:16], P, bass.bass_isa.ReduceOp.max).then_inc(s_dm2.h, 1)
                for q in range(2):
                    s_dmx.wait(pool, l, q + 1)
                    pool.tensor_tensor(T1f[:, 56:72], T1f[:, 0:16], zerof[:, :], ADD)
                    pool.drain()
                    pool.partition_all_reduce(T1f[:, 16:32], T1f[:, 56:72], P, bass.bass_isa.ReduceOp.max).then_inc(s_dmr.h, 1)
                norms(B, 1)
    return nc


_OUTS = [("xres", (L + 1, S + NS, D)), ("ckv", (L, S + NS, R)), ("krope", (L, S + NS, RD)),
         ("mem_k", (L, NM, 256)), ("mem_v", (L, NM, 256)), ("conv_p", (L, 2, 256)), ("conv_s", (L, NS, 2, 256)),
         ("shift_p", (L, 896)), ("shift_s", (L, NS, 896)), ("st_p", (L, NH, HD, HD)), ("st_s", (L, NS, NH, HD, HD))]


def kernel(**inputs):
    import concourse.bacc as bacc
    import ml_dtypes
    from concourse.bass_utils import run_bass_kernel_spmd

    nc = bacc.Bacc("TRN2", target_bir_lowering=False, num_devices=1)
    arrays = {k: np.ascontiguousarray(x) for k, x in inputs.items()}
    arrays["cst"] = constants()
    arrays["cs"] = rope_tables()
    q, c = np.arange(P)[:, None], np.arange(FMW)[None, :]
    arrays["fm"] = np.where(c <= q + FMZ, 0.0, NEG).astype(ml_dtypes.bfloat16)
    args = {k: nc.dram_tensor(f"in_{k}", x.shape, mybir.dt.from_np(x.dtype), kind="ExternalInput").ap()
            for k, x in arrays.items()}
    for k, shape in _OUTS:
        args[k] = nc.dram_tensor(f"out_{k}", shape, F32, kind="ExternalOutput").ap()
    build_program(nc, args)
    r = run_bass_kernel_spmd(nc, [{f"in_{k}": x for k, x in arrays.items()}], core_ids=[0])
    g = {k: r.results[0][f"out_{k}"] for k, _ in _OUTS}
    return (g["xres"][L, :S][None], g["xres"][L, S:][:, None],
            g["ckv"][:, :S][:, None], g["ckv"][:, S:][:, :, None],
            g["krope"][:, :S][:, None], g["krope"][:, S:][:, :, None],
            g["mem_k"].reshape(L, 1, NM, NH, HD), g["mem_v"].reshape(L, 1, NM, NH, HD),
            g["conv_p"][:, None], g["conv_s"], g["shift_p"][:, None], g["shift_s"],
            g["st_p"][:, None], g["st_s"])
```

```python
from contextlib import ExitStack

import concourse.bass as bass
import numpy as np
from concourse import mybir

F32 = mybir.dt.float32
BF16 = mybir.dt.bfloat16
I32 = mybir.dt.int32
ALU = mybir.AluOpType
ACT = mybir.ActivationFunctionType
AX = mybir.AxisListType.X
MULT, ADD, SUB, POW, MAX = ALU.mult, ALU.add, ALU.subtract, ALU.pow, ALU.max

P = 128
D = 1024
KD = D // P
L = 2
S = 2048
NS = 8
T = 256
NB = S // T
IT = NB + 1
C = 64
HD = 64
NH = 4
PAST, PAGE, NPHYS = 4096, 128, 320
NPG = PAST // PAGE
R, RD, NOPE = 128, 32, 64
NM = 256
KC = 512
DECAY = 0.6065306597
EPS, LN_EPS = 1e-6, 64e-5
MLA_SCALE = (NOPE + RD) ** -0.5
MEM_SCALE = HD ** -0.5
NEG = -1e30
STEPS = sum((b // 2 + 1) * 8 for b in range(NB))

GROUPS = [("wlal", 1792, 128), ("k", 1280, 256), ("r", 1024, 256), ("v", 1536, 256), ("ckv", 2432, 160),
          ("qd", 2176, 256), ("mq", 2848, 256), ("cx", 512, 256), ("cc", 256, 256), ("cb", 0, 256),
          ("cg", 768, 256), ("rg", 1920, 256), ("ag", 2592, 256), ("mg", 3104, 256)]
NG = len(GROUPS)
TILES = [(g, i, 128 * i, min(128, w - 128 * i)) for g, (_, _, w) in enumerate(GROUPS) for i in range((w + 127) // 128)]
NTILES = len(TILES)
BY_ACT = {"wlal", "k", "r", "v", "ckv", "qd", "mq", "cx"}
ACT_TILES = [t for t, x in enumerate(TILES) if GROUPS[x[0]][0] in BY_ACT]
LAST = [max(t for t, x in enumerate(TILES) if x[0] == g) for g in range(NG)]
DVE_TILES = [t for t, x in enumerate(TILES) if GROUPS[x[0]][0] not in BY_ACT]

VECS = [("pre", 8), ("conv", 6), ("mu", 7), ("w0", 2), ("a0", 2), ("kk", 2), ("ka", 2), ("rk", 2),
        ("lg", 2), ("lb", 2), ("qn", 2), ("kn", 1), ("mn", 8)]
VOFF, _o = {}, 0
for _n, _c in VECS:
    VOFF[_n] = _o
    _o += _c
NVEC = _o

CONSTS = [("ident", 128), ("bones", 128), ("ones", 128), ("mgram", 512), ("m1t", 128), ("mlev", 6 * 128),
          ("id64", 64), ("scan", 256), ("rot", 32), ("rep", 128),
          ("tmask", 4), ("sub", 1)]
COFF, _o = {}, 0
for _n, _c in CONSTS:
    COFF[_n] = _o
    _o += _c
NCONST = _o
FMZ = 15 * 128
FMW = FMZ + KC


def loads_of_slot(g):
    return 16 * sum(2 if GROUPS[q][1] == 0 else 1 for q in range(g % 2, g + 1, 2))


def constants():
    c = np.zeros((P, NCONST), np.float32)
    i = np.arange(P)
    r, q = i[:, None], i[None, :]

    def put(name, a):
        c[:, COFF[name]:COFF[name] + a.shape[1]] = a
    put("ident", (r == q) * 1.0)
    put("bones", (r // 64 == q // 64) * 1.0)
    put("ones", np.ones((P, P)))
    same = r // C == q // C
    put("mgram", np.concatenate([same & (r < q), same & (r <= q)] * 2, 1) * 1.0)
    lev = [(r // (2 * w) == q // (2 * w)) & (r % (2 * w) >= w) & (q % (2 * w) < w) for w in (1, 2, 4, 8, 16, 32)]
    put("m1t", lev[0].T * 1.0)
    put("mlev", np.concatenate(lev, 1) * 1.0)
    put("id64", (r % 64 == np.arange(64)[None, :]) * 1.0)
    put("scan", np.broadcast_to((np.arange(T) % C != 0)[None, :] * 1.0, (P, T)))
    rot = np.zeros((P, 32))
    for a in range(16):
        rot[a + 16, a] = -1.0
        rot[a, a + 16] = 1.0
    put("rot", rot)
    put("rep", (r == q % 32) * 1.0)
    put("tmask", (r // 32 == np.arange(4)[None, :]) * 1.0)
    put("sub", (i // 32)[:, None] * 1.0)
    return c


def rope_tables():
    half = RD // 2
    inv = np.power(np.float32(10000.0), (-np.arange(half, dtype=np.float32) / np.float32(half)))
    pos = np.concatenate([np.arange(S), np.full(NS, PAST)]).astype(np.float32)
    ang = inv.astype(np.float32)[:, None] * pos[None, :]
    ang = np.concatenate([ang, ang], 0)
    return np.stack([np.cos(ang), np.sin(ang)]).astype(np.float32)


class Block:

    def __init__(self, l, block):
        self.l, self.block, self.prompt = l, block, block is not None
        if self.prompt:
            self.it, self.ip, self.tok, self.n, self.tiles = l * IT + block, l * NB + block, block * T, T, 2
        else:
            self.it, self.n, self.tiles = l * IT + NB, NS, 1


class Sig:

    def __init__(self, ctx, nc, name, n, base=0):
        self.h, self.n, self.base = ctx.enter_context(nc.semaphore(name)), n, base

    def at(self, it, k):
        return it * self.n + (k + self.base)


def build_program(nc, a):
    ctx = ExitStack()
    with ctx:
        def sb(name, shape, dt=F32):
            return ctx.enter_context(nc.sbuf_tensor(name, shape, dt))

        begun = []

        def sig(name, n, base=0):
            s = Sig(ctx, nc, name, n, base)
            if base:
                begun.append(s)
            return s

        cst = sb("cst", [P, NCONST])
        fmask = sb("fmask", [P, FMW], BF16)
        win = sb("win", [P, 2, KD, 256])
        wout = sb("wout", [P, 2, D])
        hT = sb("hT", [P, KD, T])
        mix = sb("mix", [P, 8, T])
        pr = sb("pr", [P, 7, T + 1])
        halo = sb("halo", [P, 7])
        qd = sb("qd", [P, 2, T])
        ckr = sb("ckr", [P, T])
        krr = sb("krr", [RD, T])
        mq = sb("mq", [P, 2, T])
        cxs = sb("cxs", [P, 2, T])
        u = sb("u", [P, 2, T + 2])
        kv = sb("kv", [P, 8192 + 2048])
        memKT = sb("memKT", [P, 2, NM])
        memV = sb("memV", [P, 2, 256])
        wuq = sb("wuq", [P, 2, 384])
        wukn = sb("wukn", [P, 256])
        wukT = sb("wukT", [64, NH, R])
        wuv = sb("wuv", [P, 256])
        w2a2 = sb("w2a2", [P, 256])
        vecrow = sb("vecrow", [NVEC, P])
        vec = sb("vec", [P, NVEC])
        postg = sb("postg", [P, D])
        cs = sb("cs", [RD, 2, T])
        xin = sb("xin", [P, 2, D])
        xn = sb("xn", [P, D])
        st = sb("st", [P, 48])
        T12 = sb("T12", [P, 4, T]); T1, T2 = T12[:, 0:2, :], T12[:, 2:4, :]
        sw = sb("sw", [P, 2, T]); aa = sb("aa", [P, 2, T])
        Ls = sb("Ls", [P, 2, T]); eP = sb("eP", [P, 2, T]); Bp = sb("Bp", [P, 2, T]); Kt = sb("Kt", [P, 2, T])
        bon = sb("bon", [P, 2, T])
        T3 = sb("T3", [P, 2, T])
        KR = sb("KR", [P, 2, 2, 2, P])
        nat = sb("nat", [P, 2, 3, P])
        G = sb("G", [P, NH, 4, P])
        XX = sb("XX", [P, NH, 2, P])
        X0 = sb("X0", [P, 2, P]); SA = sb("SA", [P, 2, P]); BD = sb("BD", [P, 2, P]);
        qr = sb("qr", [RD, NH, T])
        Q96 = sb("Q96", [NOPE + RD, NH, T])
        ql = sb("ql", [P, NH, NS]); qr2 = sb("qr2", [RD, NH, NS])
        Sm = sb("Sm", [P, 2, KC]); PT = sb("PT", [P, 2, 4, P]); OO = sb("OO", [P, 8, P]);
        ml = sb("ml", [P, 8, 8])
        shs = sb("shs", [P, 7, NS]); cvs = sb("cvs", [P, 2, NS, 2]); raw = sb("raw", [P, 7, NS])
        nvec = sb("nvec", [P, 4])
        cko = sb("cko", [P, 2, P]); kro = sb("kro", [P, 2, RD])
        QR4 = sb("QR4", [P, NS, 16]); sns = sb("sns", [P, NS, NH]); Pb = sb("Pb", [P, P + 4])
        pgi = sb("pgi", [P, NS], I32); pgf = sb("pgf", [P, NS]); idx = sb("idx", [P, NS], I32)
        idc = sb("idc", [P, NS], I32); zero = sb("zero", [P, 1], I32); zerof = sb("zerof", [P, 16]); mhalf = sb("mhalf", [P, 1])
        PP = [ctx.enter_context(nc.psum_tensor(f"bank{i}", [P, 512], F32)) for i in range(8)]

        keysT = kv[0:NOPE + RD, 0:8192].rearrange("p (h s) -> p h s", h=NH)
        ckvN = kv[:, 8192:10240].rearrange("p (t r) -> p t r", r=R)
        heads = lambda t: t[:, :, :].rearrange("p a t -> p (a t)").rearrange("p (h t) -> p h t", t=P)
        An, Om = [OO[:, 0:4, :], heads(sw)], [OO[:, 4:8, :], heads(aa)]
        ge = OO[:, 0:4, :].rearrange("p a t -> p (a t)").rearrange("p (i t) -> p i t", i=2)
        sqn = nat[:, :, :, :].rearrange("p a b t -> p (a b t)").rearrange("p (i t) -> p i t", i=3)
        yy = cxs
        Pm = [Sm[:, :, :].rearrange("p a (b t) -> p (a b) t", b=2), OO[:, :, :].rearrange("p (q b) t -> p q (b t)", b=2)]
        PTm = [PT, XX[:, :, :, :].rearrange("p h a t -> p (h a t)").rearrange("p (q i t) -> p q i t", q=2, i=4)]
        mst = [[st[:, 16 + 4 * i:20 + 4 * i] for i in range(4)], [ml[:, i, 0:4] for i in range(4)]]
        Qs, BT = [PT[:, 0, :, :], heads(Ls)], PT[:, 1, 0:2, :]
        XI = [XX[:, :, :, :].rearrange("p h k t -> p k h t"),
              T12[:, :, :].rearrange("p a t -> p (a t)").rearrange("p (k h t) -> p k h t", k=2, h=NH)]
        Smg = Sm[:, :, :].rearrange("p a k -> p (a k)").rearrange("p (h k t) -> p h k t", h=NH, k=2)
        gram2 = [G[:, :, 1:3, :], Smg]
        gramF = [G[:, :, 3, :], heads(T3)]
        eN, eK = (OO[:, 4 * i:4 * i + 4, :].rearrange("p a t -> p (a t)").rearrange("p (i t) -> p i t", i=2) for i in range(2))
        OT = XX[:, :, :, :].rearrange("p h a t -> p h (a t)")
        junk = G[:, :, :, :].rearrange("p h a t -> p (h a t)")
        fst = KR[:, :, :, :, :].rearrange("p a j k t -> p (a j k t)")[:, 0:5 * P]
        shn = Q96[0:NS, :, :].rearrange("p h t -> p (h t)")[:, 0:896]
        cvn = qr[0:2 * NS, 0, :]
        memx = hT[:, :, :].rearrange("p k t -> p (k t)").rearrange("p (j d) -> p j d", j=2)
        winf = win[:, :, :, :].rearrange("p s k n -> p (s k n)")
        gat = [kv[:, 0:4096], winf]
        krg = [kv[:, 4096:5120], hT[:, :, :].rearrange("p k t -> p (k t)")[:, 0:1024]]
        kvg = [x.rearrange("p (c r) -> p c r", r=R) for x in gat]
        dmk = [x[:, 0:2048].rearrange("p (b t c) -> p b t c", b=4, t=2) for x in gat]
        dmv = [x[:, 2048:4096].rearrange("p (b t c) -> p b t c", b=4, t=2) for x in gat]
        dmp = kv[:, 4096:6144].rearrange("p (b t c) -> p b t c", b=4, t=2)
        S0 = Sm[:, :, :].rearrange("p a (b j) -> p (a b) j", j=64)
        SD = OO[:, :, :].rearrange("p a (b j) -> p (a b) j", j=64)
        SW = XX[:, :, :, :].rearrange("p a c (b j) -> p (a c b) j", j=64)
        qB = G[:, :, :, :].rearrange("p h a t -> p (h a t)").rearrange("p (b a c) -> p b a c", b=NS, a=2)
        T1f, T2f, T3f = (t[:, :, :].rearrange("p a t -> p (a t)") for t in (T1, T2, T3))

        def K(name, n=None, m=P):
            w = dict(CONSTS)[name] if n is None else n
            return cst[0:m, COFF[name]:COFF[name] + w]

        def V(name, i=0, n=1):
            return vec[:, VOFF[name] + i:VOFF[name] + i + n]
        ident, bones, ones = K("ident"), K("bones"), K("ones")
        mgram = K("mgram").rearrange("p (a q) -> p a q", a=4)
        mlev = K("mlev").rearrange("p (a q) -> p a q", a=6)

        def bc(ap, shape):
            return ap.broadcast_to(shape)

        s_const = sig("const_loaded", 0)
        s_xcopy = sig("residual_copied", 0)
        s_lvl = sig("layer_vectors_loaded", 16 * len(VECS))
        s_lw = sig("layer_weights_loaded", 16 * 8)
        s_mtl = sig("memory_tokens_loaded", 16)
        s_mw = sig("memory_weights_loaded", 32)
        s_vt = sig("vectors_transposed", 1)
        s_vr = sig("vectors_ready", 1, base=1)
        s_wr = sig("small_weights_read", 1)
        s_wt = sig("small_weights_transposed", 1)
        s_mem = {n: sig("mem_" + n, c, int(n == "out")) for n, c in dict(ss=2, xn=2, tp=2, hT=1, kv=2, kvr=1, kt=1, ktr=1, out=64, pw=2, pr=2).items()}
        s_state = sig("states_stored", 16 * (2 + NH + NS + 3), base=1)
        s_fp = sig("prompt_states_turned", 1)
        s_fpr = sig("prompt_states_read", 1)
        s_x = sig("x_loaded", 16)
        s_xl = sig("residual_loaded", 16)
        s_cs = sig("rope_tables_loaded", 16)
        s_ss = sig("x_squares_summed", 2)
        s_xr = sig("x_root_done", 2)
        s_xn = sig("x_normalised", 2, base=1)
        s_xt = sig("x_transposed", 2)
        s_hT = sig("h_ready", 2)
        s_wi = [sig(f"w_in_loaded{i}", loads_of_slot(NG - 2 + i)) for i in range(2)]
        s_pj = sig("projected", NTILES, base=1)
        s_pa = sig("projection_read_by_act", len(ACT_TILES))
        s_pv = sig("projection_read_by_dve", len(DVE_TILES))
        s_shift = sig("token_shift_done", 4)
        s_th = sig("tanh_ready", 1)
        s_lo = sig("lora_done", 1)
        s_lor = sig("lora_read", 1)
        s_sg = sig("decay_summed", 1)
        s_dec = sig("decay_factors_ready", 1)
        s_sq = sig("key_squares_ready", 1)
        s_sqd = sig("key_norms_done", 1)
        s_bo = sig("bonus_products_ready", 1)
        s_bod = sig("bonus_summed", 1)
        s_bor = sig("bonus_read", 1)
        s_nq = sig("latent_squares_ready", 1)
        s_nqd = sig("latent_norms_done", 1)
        s_qn = sig("latents_normalised", 1)
        s_qp = sig("queries_projected", 1)
        s_qpr = sig("queries_read", 2)
        s_ql = sig("latent_queries_done", 2)
        s_qla = sig("latent_queries_read", 1)
        s_qlr = sig("queries_rotated", 1)
        s_kr = sig("key_partner_and_latents_turned", 2)
        s_krr = sig("keys_rotated", 1)
        s_kn = sig("rotary_rows_done", 1)
        s_kvd = sig("latents_cached", 1, base=1)
        s_coe = sig("latent_rows_read", 1, base=1)
        s_ge = sig("gate_tanh_ready", 8)
        s_an = sig("running_max_ready", STEPS)
        s_co = sig("latents_written", 32, base=1)
        s_rt = sig("rwkv_operands_ready", 1)
        s_nt = sig("rwkv_transposed", 4)
        s_ntr = sig("rwkv_natural_ready", 4)
        s_gr = sig("grams_done", 4)
        s_gm = sig("grams_read", 4)
        s_ga = sig("natural_grams_done", 2)
        s_anr = sig("natural_grams_read", 2)
        s_grr = sig("grams_masked", 2)
        s_om = sig("level_block_ready", 10)
        s_q = sig("inverse_first_product", 20)
        s_qrd = sig("inverse_first_read", 20)
        s_xx = sig("inverse_second_product", 20)
        s_xxr = sig("inverse_updated", 20)
        s_x0 = sig("chunk_rhs_done", 8)
        s_x0r = sig("chunk_rhs_read", 8)
        s_sa = sig("chunk_solved", 8)
        s_sar = sig("chunk_solution_read", 8)
        s_su = sig("state_increment_done", 8)
        s_sur = sig("state_updated", 8)
        s_y = sig("rwkv_out_done", 4)
        s_yr = sig("rwkv_out_read", 4)
        s_lm = sig("mean_summed", 1)
        s_lc = sig("centred_squares_ready", 1)
        s_lv = sig("variance_summed", 1)
        s_lvr = sig("rwkv_group_done", 1)
        s_as = sig("scores_done", STEPS)
        s_am = sig("scores_masked", STEPS)
        s_ae = sig("probs_ready", STEPS)
        s_at = sig("probs_transposed", STEPS, base=1)
        s_ar = sig("probs_transposed_read", STEPS)
        s_av = sig("values_summed", STEPS, base=1)
        s_ao = sig("values_read", STEPS, base=1)
        s_ai = sig("attention_begun", 1)
        s_on = sig("attention_normalised", 1)
        s_ot = sig("attention_transposed", 1)
        s_otr = sig("attention_transposed_read", 1)
        s_uv = sig("attention_projected", 1)
        s_uvr = sig("attention_gated", 1)
        s_ms = sig("mem_scores_done", 2)
        s_mx = sig("mem_max_ready", 2)
        s_me = sig("mem_exp_done", 2)
        s_mn = sig("mem_probs_ready", 2)
        s_mt = sig("mem_probs_transposed", 2)
        s_mtr = sig("mem_probs_read", 2)
        s_mo = sig("mem_values_done", 1)
        s_mix = sig("mixed_ready", 1)
        s_wo = [sig(f"w_out_loaded{i}", 16 * 4) for i in range(2)]
        s_wou = sig("w_out_used", KD, base=1)
        s_o = sig("out_projected", 1)
        s_os = sig("out_squares_summed", 1)
        s_of = sig("residual_added", 1, base=1)
        s_od = sig("residual_stored", 16, base=1)
        s_pw = sig("root_wanted", 2)
        s_pr = sig("root_done", 2)
        s_rw = sig("square_root_wanted", 2)
        s_rd = sig("square_root_done", 2)
        s_pg = sig("pages_loaded", 0)
        s_se = sig("spread_operand_ready", 5)
        s_sb = sig("rows_spread", 5)
        s_sl = sig("decode_states_loaded", 16 * NS)
        s_sst2 = sig("decode_states_updated", 1)
        s_sy = sig("decode_rwkv_out", 1)
        s_sr = sig("decode_rows_turned", 1)
        s_srr = sig("decode_rows_read", 1)
        s_dp = sig("own_score_products", 1)
        s_dq = sig("own_scores_and_spread_queries", 1)
        s_dqr = sig("decode_queries_ready", 1)
        s_dg = [sig(f"pages_gathered{i}", 32 * NS // 2) for i in range(2)]
        s_dt = sig("decode_keys_turned", 8 * NS)
        s_dtr = sig("decode_latents_read", 8 * NS, base=1)
        s_ds = sig("decode_scores_done", 8 * NS, base=1)
        s_dm1 = sig("decode_partition_max", NS)
        s_dm2 = sig("decode_max", NS)
        s_dx = sig("decode_scores_shifted", NS)
        s_dxe = sig("decode_exponentials", NS)
        s_de = sig("decode_probs_summed", NS)
        s_dv = sig("decode_values_done", NS, base=1)
        s_da = sig("decode_attention_done", NS)
        s_qe = sig("memory_query_operand", 2)
        s_qb = sig("memory_queries_spread", 2)
        s_dml = [sig(f"decode_memory_loaded{i}", 16 * 8) for i in range(2)]
        s_dmx = sig("memory_partition_max", 2)
        s_dmr = sig("memory_max", 2)
        s_dms = sig("memory_scores_shifted", 2)
        s_dme = sig("memory_exponentials", 2)
        s_dmo = sig("memory_values_done", 2)
        s_dm = sig("memory_half_done", 2, base=1)

        xres, csd = a["xres"], a["cs"]
        blk = ctx.enter_context(nc.Block())

        def prompt_loop(eng, body, l):
            with eng().Fori(0, NB // 2) as m:
                with eng().Fori(0, 2) as e:
                    body(Block(l, m * 2 + e), m, e)

        def steps_before(l, m, e):
            return l * STEPS + (m + e) * (m + 1) * 8

        @blk.sync
        def _(sp):
            for s in begun:
                sp.sem_inc(s.h, 1)
            sp.dma_start(cst[:, :], a["cst"]).then_inc(s_const.h, 16)
            sp.dma_start(fmask[:, :], a["fm"]).then_inc(s_const.h, 16)
            sp.wait_ge(s_const.h, 32)
            with sp.Fori(0, L) as l:
                sl = bass.ds(l, 1)
                count = [0]

                def put(dst, src):
                    sp.dma_start(dst, src).then_inc(s_lw.h, 16)
                    count[0] += 16

                sp.wait_ge(s_const.h, 32)
                sp.wait_ge(s_dv.h, s_dv.at(l, 0))
                sp.dma_start(memx, a["mem_prompt"][0].rearrange("(t p) d -> p t d", p=P)).then_inc(s_mtl.h, 16)

                def rows(name, src):
                    n = dict(VECS)[name]
                    sp.dma_start(vecrow[VOFF[name]:VOFF[name] + n, :], src.rearrange("a (n p) -> (a n) p", p=P)).then_inc(s_lvl.h, 16)
                sp.wait_ge(s_const.h, 32)
                sp.wait_ge(s_vr.h, s_vr.at(l, 0))
                rows("pre", a["pre_norm_g"][sl, :])
                rows("conv", a["conv_w"][sl].rearrange("a k c -> a (k c)"))
                rows("mu", a["rwkv_mu"][sl, :])
                rows("w0", a["rwkv_w0"][sl, :])
                rows("a0", a["rwkv_a0"][sl, :])
                rows("kk", a["rwkv_k_k"][sl, :])
                rows("ka", a["rwkv_k_a"][sl, :])
                rows("rk", a["rwkv_r_k"][sl].rearrange("a h d -> a (h d)"))
                rows("lg", a["rwkv_lnx_g"][sl, :])
                rows("lb", a["rwkv_lnx_b"][sl, :])
                rows("qn", a["mla_q_norm_g"][sl, :])
                rows("kn", a["mla_kv_norm_g"][sl, :])
                rows("mn", a["mem_norm_g"][sl, :])
                wm = kv[:, 0:4096].rearrange("p (k n) -> p k n", k=KD)
                sp.wait_ge(s_const.h, 32)
                sp.wait_ge(s_dm.h, s_dm.at(l, 0))
                sp.dma_start(wm[:, :, 0:256], a["w_mem_k"][sl].rearrange("a (k p) n -> p (a k) n", p=P)).then_inc(s_mw.h, 16)
                sp.dma_start(wm[:, :, 256:512], a["w_mem_v"][sl].rearrange("a (k p) n -> p (a k) n", p=P)).then_inc(s_mw.h, 16)
                sp.wait_ge(s_const.h, 32)
                sp.wait_ge(s_od.h, s_od.at(l * IT, 0))
                put(postg[:, :], a["post_norm_g"][sl, :].broadcast_to([P, D]))
                put(wuq[:, :, :], a["mla_w_uq"][sl].rearrange("a (t p) n -> p (a t) n", p=P))
                put(wukn[:, :], a["mla_w_uk"][sl].rearrange("a r h d -> (a r) (h d)"))
                put(wuv[:, :], a["mla_w_uv"][sl].rearrange("a r h d -> (a r) (h d)"))
                put(w2a2[0:64, :], a["rwkv_w2"][sl].rearrange("a r c -> (a r) c"))
                put(w2a2[64:128, :], a["rwkv_a2"][sl].rearrange("a r c -> (a r) c"))
                sp.wait_ge(s_const.h, 32)
                sp.wait_ge(s_state.h, s_state.at(l, 0))
                put(shn[:, :], a["state_rwkv_shift"][sl].rearrange("a b c -> (a b) c"))
                put(cvn[:, :], a["state_conv"][sl].rearrange("a b k c -> (a b k) c"))
                assert count[0] == s_lw.n

                def load_x(it, tok):
                    sp.wait_ge(s_const.h, 32)
                    sp.wait_ge(s_xn.h, s_xn.at(it, 0))
                    src = xres[sl, bass.ds(tok, T), :].rearrange("a (t p) d -> p (a t) d", p=P)
                    sp.dma_start(xin[:, :, :], src).then_inc(s_x.h, 16)

                sp.wait_ge(s_xcopy.h, 32 + 16 * L)
                load_x(l * IT, 0)

                def block(it, tok, n):
                    sp.wait_ge(s_const.h, 32)
                    sp.wait_ge(s_kvd.h, s_kvd.at(it, 0))
                    dst = cs[:, :, 0:n]
                    sp.dma_start(dst, csd[:, :, bass.ds(tok, n)].rearrange("c p t -> p c t")).then_inc(s_cs.h, 16)
                    for g, (_, c0, w) in enumerate(GROUPS):
                        if g == 6:
                            sp.wait_ge(s_const.h, 32)
                            sp.wait_ge(s_od.h, s_od.at(it, 0))
                            if n == T:
                                load_x(it + 1, tok + T)
                            else:
                                sp.dma_start(xin[0:n, 0, :], xres[sl, tok:tok + n, :].rearrange("a p d -> p (a d)")).then_inc(s_xl.h, 16)
                        sp.wait_ge(s_const.h, 32)
                        sp.wait_ge(s_pj.h, s_pj.at(it, 0 if g < 2 else LAST[g - 2] + 1))
                        src = a["w_in"][sl, :, c0:c0 + w].rearrange("a (k p) n -> p (a k) n", p=P)
                        for k0, k1 in ([(0, KD)] if c0 else [(1, KD), (0, 1)]):
                            sp.dma_start(win[:, g % 2, k0:k1, 0:w], src[:, k0:k1, :]).then_inc(s_wi[g % 2].h, 16)
                def prompt_block(B, m, e):
                    block(B.it, B.tok, T)
                    sp.wait_ge(s_const.h, 32)
                    sp.wait_ge(s_xn.h, s_xn.at(B.it + 1, 2))
                    src = xres[sl, bass.ds(B.tok, T), :].rearrange("a (t p) d -> p (a t) d", p=P)
                    sp.dma_start(xin[:, :, :], src).then_inc(s_xl.h, 16)
                prompt_loop(lambda: sp, prompt_block, l)
                block(l * IT + NB, S, NS)
                sp.wait_ge(s_const.h, 32)
                sp.wait_ge(s_rt.h, s_rt.at(l * IT + NB, 1))
                for b in range(NS):
                    sp.dma_start(S0[:, 2 * b:2 * b + 2, :],
                                 a["state_rwkv"][sl, b].rearrange("a (p h) i j -> (h i) (a p) j", p=2)).then_inc(s_sl.h, 16)
                for q in range(2):
                    sp.wait_ge(s_const.h, 32)
                    sp.wait_ge(s_dv.h, s_dv.at(l, NS - 1 + q))
                    for b in range(4):
                        sp.dma_start(dmk[q][:, b, :, :], a["cache_mem_k"][sl, 4 * q + b].rearrange("a (t p) h d -> p (a t) (h d)", p=P)).then_inc(s_dml[q].h, 16)
                        sp.dma_start(dmv[q][:, b, :, :], a["cache_mem_v"][sl, 4 * q + b].rearrange("a (t p) h d -> p (a t) (h d)", p=P)).then_inc(s_dml[q].h, 16)
            sp.wait_ge(s_od.h, L * IT * s_od.n + 1)
            sp.wait_ge(s_state.h, L * s_state.n + 1)
            sp.wait_ge(s_co.h, L * IT * s_co.n + 1)
            sp.wait_ge(s_mem["out"].h, L * s_mem["out"].n + 1)

        @blk.tensor
        def _(pe):
            def mm(out, lhsT, rhs, start=True, stop=True):
                return pe.matmul(out, lhsT, rhs, start=start, stop=stop, skip_group_check=True)

            def tr(out, in_, w):
                return pe.transpose(out, in_, ident[0:w, 0:w])

            def transpose_rows(sig_in, sig_out, it, tiles, w, k):
                for j in range(tiles):
                    pe.wait_ge(s_const.h, 32)
                    pe.wait_ge(sig_in.h, sig_in.at(it, j + 1))
                    for dt in range(KD):
                        c = (dt % 2) * T + j * P
                        last = tr(PP[dt // 2][:, c:c + w], xn[0:w, dt * P:(dt + 1) * P], w)
                    last.then_inc(sig_out.h, k)

            def turn_x(it, j):
                if j:
                    pe.wait_ge(s_hT.h, s_hT.at(it, j))
                pe.wait_ge(s_const.h, 32)
                pe.wait_ge(s_xn.h, s_xn.at(it, j + 1))
                for dt in range(KD):
                    last = tr(PP[6 + dt // 4][:, (dt % 4) * P:(dt % 4 + 1) * P], xn[:, dt * P:(dt + 1) * P], P)
                last.then_inc(s_xt.h, 1)

            def halves(bank, n, parts=P):
                return PP[bank][0:parts, :].rearrange("p (a t) -> p a t", a=2)[:, :, 0:n]

            def project(B):
                it, n, w = B.it, B.n, min(B.n, P)
                for t, (g, i, c, f) in enumerate(TILES):
                    if i == 0:
                        pe.wait_ge(s_wi[g % 2].h, s_wi[g % 2].at(it, loads_of_slot(g)))
                    if t >= 4:
                        q = t - 4
                        if q in ACT_TILES:
                            pe.wait_ge(s_pa.h, s_pa.at(it, ACT_TILES.index(q) + 1))
                        else:
                            pe.wait_ge(s_pv.h, s_pv.at(it, DVE_TILES.index(q) + 1))
                    for k in range(KD):
                        last = mm(PP[t % 4][0:f, 0:n], win[:, g % 2, k, c:c + f], hT[:, k, 0:n], k == 0, k == KD - 1)
                    last.then_inc(s_pj.h, 1)
                    if (t + 1 == NTILES) or TILES[t + 1][0] != g:
                        side = SIDE.get(GROUPS[g][0])
                        if side:
                            side(B)

            def lora(B):
                pe.wait_ge(s_const.h, 32)
                pe.wait_ge(s_of.h, s_of.at(B.it, 0))
                pe.wait_ge(s_th.h, s_th.at(B.it, 1))
                for r0, bank in ((0, 4), (64, 5)):
                    for p in range(2):
                        last = mm(halves(bank, B.n)[:, p, :], w2a2[r0:r0 + 64, p * P:(p + 1) * P],
                                  pr[r0:r0 + 64, 6, 1:1 + B.n])
                last.then_inc(s_lo.h, 1)

            def key_norms(B):
                pe.wait_ge(s_sq.h, s_sq.at(B.it, 1))
                mm(halves(6, B.n), bones, T2[:, :, 0:B.n]).then_inc(s_sqd.h, 1)

            def latent_norms(B):
                pe.wait_ge(s_nq.h, s_nq.at(B.it, 1))
                mm(PP[7][:, 0:B.n], ones, sqn[:, 0, 0:B.n])
                mm(PP[7][:, T:T + B.n], ones, sqn[:, 1, 0:B.n], True, False)
                mm(PP[7][:, T:T + B.n], ones, sqn[:, 2, 0:B.n], False, True).then_inc(s_nqd.h, 1)

            def bonus(B):
                pe.wait_ge(s_bo.h, s_bo.at(B.it, 1))
                mm(halves(6, B.n), bones, T2[:, :, 0:B.n]).then_inc(s_bod.h, 1)

            def queries(B):
                n = B.n
                pe.wait_ge(s_qn.h, s_qn.at(B.it, 1))
                pe.wait_ge(s_lor.h, s_lor.at(B.it, 1))
                for h in range(NH):
                    for t in range(2):
                        last = mm(PP[4 + h // 2][0:96, (h % 2) * T:(h % 2) * T + n], wuq[:, t, h * 96:h * 96 + 96],
                                  qd[:, t, 0:n], t == 0, t == 1)
                last.then_inc(s_qp.h, 1)

            def latent_queries(B):
                n = B.n
                pe.wait_ge(s_bor.h, s_bor.at(B.it, 1))
                pe.wait_ge(s_qpr.h, s_qpr.at(B.it, 2))
                for h in range(NH):
                    cols = slice((h % 2) * T, (h % 2) * T + n)
                    if B.prompt:
                        last = mm(PP[4 + h // 2][0:NOPE, cols], wukn[:, h * NOPE:(h + 1) * NOPE], ckr[:, 0:n])
                    else:
                        last = mm(PP[4 + h // 2][:, cols], wukT[:, h, :], Q96[0:NOPE, h, 0:n])
                last.then_inc(s_ql.h, 1)
                for i in range(2):
                    last = mm(halves(6 + i, n, RD), K("rot", m=RD), qr[:, 2 * i:2 * i + 2, 0:n])
                last.then_inc(s_ql.h, 1)

            def latents(B):
                w = min(B.n, P)
                pe.wait_ge(s_const.h, 32)
                pe.wait_ge(s_qla.h, s_qla.at(B.it, 1))
                mm(PP[4][0:RD, 0:B.n], K("rot", m=RD), krr[:, 0:B.n]).then_inc(s_kr.h, 1)
                for j in range(B.tiles):
                    last = tr(PP[5][0:w, j * P:j * P + P], ckr[:, j * P:j * P + w], P)
                last.then_inc(s_kr.h, 1)

            def rotary_rows(B):
                w = min(B.n, P)
                pe.wait_ge(s_const.h, 32)
                pe.wait_ge(s_qlr.h, s_qlr.at(B.it, 1))
                pe.wait_ge(s_krr.h, s_krr.at(B.it, 1))
                for j in range(B.tiles):
                    last = tr(PP[6][0:w, j * RD:(j + 1) * RD], krr[:, j * P:j * P + w], RD)
                last.then_inc(s_kn.h, 1)

            SIDE = dict(ckv=lora, qd=key_norms, mq=latent_norms, cc=bonus, cb=queries, cg=latent_queries,
                        rg=latents, ag=rotary_rows)

            def rwkv_chunks(B):
                ip = B.ip
                pe.wait_ge(s_rt.h, s_rt.at(B.it, 1))
                pe.wait_ge(s_kvd.h, s_kvd.at(B.it, 1))
                pe.wait_ge(s_coe.h, s_coe.at(B.it, 1))
                def natural(j, bank, c0):
                    for p in range(2):
                        if j:
                            pe.wait_ge(s_sur.h, s_sur.at(ip, 2 + p + 1))
                        for i, src in enumerate((pr[:, 4 + p, 1 + j * P:1 + (j + 1) * P], Kt[:, p, j * P:(j + 1) * P],
                                                 Bp[:, p, j * P:(j + 1) * P])):
                            last = tr(PP[bank + p][:, c0 + i * P:c0 + (i + 1) * P], src, P)
                        last.then_inc(s_nt.h, 1)

                natural(0, 4, 0)
                pe.wait_ge(s_pv.h, s_pv.at(B.it, len(DVE_TILES)))
                for j in range(2):
                    J = slice(j * P, (j + 1) * P)
                    for p in range(2):
                        if j:
                            pe.wait_ge(s_gm.h, s_gm.at(ip, p + 1))
                        for h in range(2):
                            q = slice(64 * h, 64 * h + 64)
                            mm(PP[2 * p + h][:, 0:T], Bp[q, p, J], KR[q, p, j, :, :])
                            last = mm(PP[2 * p + h][:, T:2 * T], Kt[q, p, J], KR[q, p, j, :, :])
                        last.then_inc(s_gr.h, 1)
                    if j:
                        pe.wait_ge(s_anr.h, s_anr.at(ip, 1))
                    for p in range(2):
                        for h in range(2):
                            q = slice(64 * h, 64 * h + 64)
                            last = mm(PP[6 + h][:, p * P:(p + 1) * P], KR[q, p, j, 0, :], Bp[q, p, J])
                    last.then_inc(s_ga.h, 1)
                for lev in range(5):
                    for j in range(2):
                        pe.wait_ge(s_om.h, s_om.at(ip, lev * 2 + j + 1))
                        if lev == 0:
                            pe.wait_ge(s_gm.h, s_gm.at(ip, 4))
                            pe.wait_ge(s_grr.h, s_grr.at(ip, j + 1))
                        for p in range(2):
                            if lev:
                                pe.wait_ge(s_xxr.h, s_xxr.at(ip, (lev - 1) * 4 + 2 * j + p + 1))
                            for h in range(2):
                                last = mm(PP[2 * j + p][:, h * P:(h + 1) * P], Om[j][:, 2 * p + h, :], XI[j][:, 0, 2 * p + h, :])
                            last.then_inc(s_q.h, 1)
                    if lev == 0:
                        pe.wait_ge(s_ntr.h, s_ntr.at(ip, 2))
                        pe.wait_ge(s_anr.h, s_anr.at(ip, 2))
                    for j in range(2):
                        for p in range(2):
                            pe.wait_ge(s_qrd.h, s_qrd.at(ip, lev * 4 + 2 * j + p + 1))
                            for h in range(2):
                                q, o = 2 * p + h, PP[4 + 2 * j + p]
                                last = mm(o[:, h * T:h * T + P], XI[j][:, 1, q, :], Qs[j][:, q, :])
                                if lev < 4:
                                    last = mm(o[:, h * T + P:(h + 1) * T], Qs[j][:, q, :], XI[j][:, 1, q, :])
                            last.then_inc(s_xx.h, 1)
                for j in range(2):
                    if j:
                        natural(1, 2, P)
                    for c in range(2):
                        n0 = (j * 2 + c) * 2
                        Q = slice(64 * c, 64 * c + 64)
                        for p in range(2):
                            if n0:
                                pe.wait_ge(s_sur.h, s_sur.at(ip, n0 - 2 + p + 1))
                            if c == 0:
                                pe.wait_ge(s_ntr.h, s_ntr.at(ip, j * 2 + p + 1))
                                pe.wait_ge(s_xxr.h, s_xxr.at(ip, 16 + 2 * j + p + 1))
                            mm(PP[p][Q, 0:P], KR[:, p, j, 0, Q], BD[:, p, :], True, False)
                            for h in range(2):
                                last = mm(PP[p][Q, 64 * h:64 * h + 64], gram2[j][:, 2 * p + h, 1, Q],
                                          nat[:, p, 0, 64 * h:64 * h + 64], False, h == 1)
                            last.then_inc(s_x0.h, 1)
                        for p in range(2):
                            if j and c == 0:
                                pe.wait_ge(s_yr.h, s_yr.at(ip, p + 1))
                            mm(PP[4 + p][:, Q], BD[:, p, :], KR[:, p, j, 1, Q], c == 0, False)
                        for p in range(2):
                            pe.wait_ge(s_x0r.h, s_x0r.at(ip, n0 + p + 1))
                            for h in range(2):
                                last = mm(PP[p][Q, P + 64 * h:P + 64 * h + 64], XI[j][:, 0, 2 * p + h, Q],
                                          X0[:, p, 64 * h:64 * h + 64])
                            last.then_inc(s_sa.h, 1)
                        for p in range(2):
                            pe.wait_ge(s_sar.h, s_sar.at(ip, n0 + p + 1))
                            mm(PP[2 + p][:, 0:P], nat[Q, p, 1, :], nat[Q, p, 0, :], True, False)
                            mm(PP[2 + p][:, 0:P], nat[Q, p, 2, :], SA[Q, p, :], False, True)\
                                .then_inc(s_su.h, 1)
                        if c == 0:
                            if j == 0:
                                pe.wait_ge(s_xxr.h, s_xxr.at(ip, 20))
                            turn_x(B.it + 1, j)
                    for p in range(2):
                        for h in range(2):
                            q = slice(64 * h, 64 * h + 64)
                            mm(PP[4 + p][q, 0:P], nat[:, p, 0, q], gramF[j][:, 2 * p + h, :], False, False)
                            last = mm(PP[4 + p][q, 0:P], SA[:, p, q], gram2[j][:, 2 * p + h, 0, :], False, h == 1)
                        last.then_inc(s_y.h, 1)

            def attention(B, l, m, e):
                with pe.Fori(0, m + 1) as kc:
                    n0 = pe.snap(steps_before(l, m, e) + kc * 8)

                    def scores(s):
                        j, h = s // NH, s % NH
                        if s >= 2:
                            pe.wait_ge(s_am.h, n0 + (s - 1))
                        mm(PP[s % 2][:, :], Q96[:, h, j * P:(j + 1) * P], keysT[:, h, bass.ds(kc * KC, KC)]).then_inc(s_as.h, 1)

                    def turn(s):
                        pe.wait_ge(s_ae.h, n0 + (s + 1))
                        if s >= 2:
                            pe.wait_ge(s_ar.h, n0 + (s - 1))
                        for i in range(4):
                            last = tr(PP[2 + s % 2][:, i * P:(i + 1) * P], Sm[:, s % 2, i * P:(i + 1) * P], P)
                        last.then_inc(s_at.h, 1)

                    def values(s):
                        pe.wait_ge(s_ar.h, n0 + (s + 1))
                        pe.wait_ge(s_ao.h, n0 + max(s - 1, 0) + s_ao.base)
                        for i in range(4):
                            last = mm(PP[4 + s % 2][:, 0:R], PT[:, s % 2, i, :], ckvN[:, bass.ds(kc * 4 + i, 1), :],
                                      i == 0, i == 3)
                        last.then_inc(s_av.h, 1)
                    scores(0)
                    for s in range(8):
                        if s < 7:
                            scores(s + 1)
                        turn(s)
                        if s:
                            values(s - 1)
                    values(7)

            def attention_out(B):
                if B.prompt:
                    pe.wait_ge(s_on.h, s_on.at(B.ip, 1))
                    for j in range(2):
                        for h in range(NH):
                            last = tr(PP[6 + j][:, h * P:(h + 1) * P], OO[:, j * NH + h, :], P)
                    last.then_inc(s_ot.h, 1)
                pe.wait_ge(s_otr.h, s_otr.at(B.it, 1))
                for h in range(NH):
                    last = mm(PP[4 + h // 2][64 * (h % 2):64 * (h % 2) + 64, 0:B.n], wuv[:, 64 * h:64 * h + 64],
                              OT[:, h, 0:B.n])
                last.then_inc(s_uv.h, 1)

            def memory(B):
                def scores(j):
                    J = slice(j * P, (j + 1) * P)
                    for h in range(2):
                        q = slice(64 * h, 64 * h + 64)
                        for p in range(2):
                            last = mm(PP[4 * j + h][:, p * NM:(p + 1) * NM], mq[q, p, J], memKT[q, p, :])
                    last.then_inc(s_ms.h, 1)

                def turn(j):
                    pe.wait_ge(s_mn.h, s_mn.at(B.ip, j + 1))
                    b0 = 2 - 2 * j
                    for q in range(4):
                        for t in range(2):
                            last = tr(PP[b0 + q // 2][:, (q % 2) * T + t * P:(q % 2) * T + (t + 1) * P],
                                      Pm[j][:, q, t * P:(t + 1) * P], P)
                    last.then_inc(s_mt.h, 1)

                def values(j):
                    pe.wait_ge(s_mtr.h, s_mtr.at(B.ip, j + 1))
                    for h in range(2):
                        for p in range(2):
                            for t in range(2):
                                last = mm(PP[6][64 * h:64 * h + 64, p * T + j * P:p * T + (j + 1) * P],
                                          memV[:, t, (2 * p + h) * 64:(2 * p + h) * 64 + 64],
                                          PTm[j][:, h, 2 * p + t, :], t == 0, t == 1)
                    return last
                scores(0)
                pe.wait_ge(s_uvr.h, s_uvr.at(B.ip, 1))
                scores(1)
                turn(0)
                turn(1)
                values(0)
                values(1).then_inc(s_mo.h, 1)

            def group_norm(B, part):
                if part == 0:
                    if B.prompt:
                        pe.wait_ge(s_yr.h, s_yr.at(B.ip, 4))
                    else:
                        pe.wait_ge(s_sy.h, s_sy.at(B.l, 1))
                    mm(halves(1, B.n), bones, yy[:, :, 0:B.n]).then_inc(s_lm.h, 1)
                else:
                    pe.wait_ge(s_lc.h, s_lc.at(B.it, 1))
                    if B.prompt:
                        pe.wait_ge(s_hT.h, s_hT.at(B.it + 1, 2))
                    mm(halves(7, B.n), bones, T2[:, :, 0:B.n]).then_inc(s_lv.h, 1)

            def project_out(B):
                w = min(B.n, P)
                pe.wait_ge(s_mix.h, s_mix.at(B.it, 1))
                for k in range(KD):
                    pe.wait_ge(s_wo[k % 2].h, s_wo[k % 2].at(B.it, 16 * (k // 2 + 1)))
                    for j in range(B.tiles):
                        for i in range(2):
                            last = mm(PP[4 + 2 * j + i][0:w, :], mix[:, k, j * P:j * P + w], wout[:, k % 2, i * 512:(i + 1) * 512],
                                      k == 0, k == KD - 1)
                    last.then_inc(s_wou.h, 1)

            def prompt_states(l):
                tr(PP[0][0:7, 0:P], halo[:, :], P)
                for p in range(2):
                    tr(PP[0][0:2, P + p * P:P + (p + 1) * P], u[:, p, 0:2], P)
                    last = tr(PP[1][:, p * P:(p + 1) * P], BD[:, p, :], P)
                last.then_inc(s_fp.h, 1)

            def sample_rwkv(l):
                pe.wait_ge(s_pv.h, s_pv.at(l * IT + NB, len(DVE_TILES)))
                for i in range(5):
                    pe.wait_ge(s_se.h, s_se.at(l, i + 1))
                    for q in range(2):
                        last = mm(PP[2 * (i % 2) + q][:, :], bones, xn[:, q * 512:(q + 1) * 512])
                    last.then_inc(s_sb.h, 1)
                for i in range(7):
                    tr(PP[4 + i // 4][0:NS, (i % 4) * P:(i % 4 + 1) * P], raw[:, i, :], P)
                for p in range(2):
                    last = tr(PP[7][0:NS, p * P:(p + 1) * P], u[:, p, 2:2 + NS], P)
                last.then_inc(s_sr.h, 1)

            def sample_attention(l):
                pe.wait_ge(s_dp.h, s_dp.at(l, 1))
                mm(PP[4][:, 0:32], K("rep", m=RD), qr2[:, :, 0:NS])
                mm(PP[4][:, 64:96], ones, T1f[:, 0:32], True, False)
                mm(PP[4][:, 64:96], ones[0:RD, :], T3f[0:RD, 0:32], False, True).then_inc(s_dq.h, 1)
                pe.wait_ge(s_const.h, 32)
                pe.wait_ge(s_dqr.h, s_dqr.at(l, 1))

                def keys(n, slot, g):
                    pe.wait_ge(s_dtr.h, n * 8 + (max(g - 1, 0) + s_dtr.base))
                    for i in range(4):
                        tr(PP[g % 2][:, i * P:(i + 1) * P], kvg[slot][:, 4 * g + i, :], P)
                    tr(PP[2 + g % 2][:, 0:P], krg[slot][:, g * P:(g + 1) * P], P).then_inc(s_dt.h, 1)

                def score(n, b, slot, g):
                    pe.wait_ge(s_dtr.h, n * 8 + (g + 1 + s_dtr.base))
                    o = PP[5 - slot]
                    mm(o[:, 16 * g:16 * g + 16], T2f[:, (g % 2) * P:(g % 2) * P + P], QR4[:, bass.ds(b, 1), :], True, False)
                    for i in range(4):
                        last = mm(o[:, 16 * g + 4 * i:16 * g + 4 * i + 4], PT[:, g % 2, i, :],
                                  ql[:, :, bass.ds(b, 1)], False, i == 3)
                    last.then_inc(s_ds.h, 1)

                def values(n, slot):
                    pe.wait_ge(s_de.h, n + 1)
                    mm(PP[6][:, 64:68], ones, st[:, 16:20])
                    for i in range(32):
                        last = mm(PP[6][:, 0:4], kvg[slot][:, i, :], Pb[:, 4 * i:4 * i + 4], i == 0, i == 31)
                    last.then_inc(s_dv.h, 1)

                def turn(i, k, g0, g1):
                    n, b = l * NS + i * 2 + k, i * 2 + k
                    if g0 == 0:
                        pe.wait_ge(s_dg[k].h, l * (16 * NS) + (i * 32 + 32))
                        keys(n, k, 0)
                    for g in range(g0, g1):
                        if g < 7:
                            keys(n, k, g + 1)
                        score(n, b, k, g)

                def step(i, k):
                    nxt = (i, 1) if k == 0 else (i + 1, 0)
                    turn(*nxt, 0, 4)
                    values(l * NS + i * 2 + k, k)
                    turn(*nxt, 4, 8)
                turn(0, 0, 0, 8)
                with pe.Fori(0, NS // 2 - 1) as i:
                    step(i, 0)
                    step(i, 1)
                step(NS // 2 - 1, 0)
                values(l * NS + NS - 1, 1)

            def sample_memory(l):
                for p in range(2):
                    pe.wait_ge(s_qe.h, s_qe.at(l, p + 1))
                    for q in range(2):
                        last = mm(PP[2 * p + q][:, :], ones, xn[:, q * 512:(q + 1) * 512])
                    last.then_inc(s_qb.h, 1)
                for q in range(2):
                    pe.wait_ge(s_dme.h, s_dme.at(l, q + 1))
                    mm(PP[7][:, 0:32], ones, Pb[:, 0:32])
                    for b in range(4):
                        for p in range(2):
                            for t in range(2):
                                c = (b * 2 + p) * 2
                                last = mm(PP[6][:, c:c + 2], dmv[q][:, b, t, p * P:(p + 1) * P],
                                          Pb[:, (b * 2 + t) * 4 + 2 * p:(b * 2 + t) * 4 + 2 * p + 2], t == 0, t == 1)
                    last.then_inc(s_dmo.h, 1)
                    pe.wait_ge(s_dm.h, s_dm.at(l, q + 1))

            pe.wait_ge(s_const.h, 32)
            with pe.Fori(0, L) as l:
                pe.wait_ge(s_const.h, 32)
                pe.wait_ge(s_lvl.h, s_lvl.at(l, s_lvl.n))
                mm(PP[7][:, 0:NVEC], vecrow[:, :], ident[0:NVEC, 0:NVEC]).then_inc(s_vt.h, 1)
                transpose_rows(s_mem["xn"], s_mem["tp"], l, 2, P, 1)
                pe.wait_ge(s_mw.h, s_mw.at(l, s_mw.n))
                pe.wait_ge(s_mem["hT"].h, s_mem["hT"].at(l, 1))
                wm = kv[:, 0:4096].rearrange("p (k n) -> p k n", k=KD)
                for j in range(2):
                    for k in range(KD):
                        last = mm(PP[4 + j][:, :], hT[:, k, j * P:(j + 1) * P], wm[:, k, :], k == 0, k == KD - 1)
                    last.then_inc(s_mem["kv"].h, 1)
                pe.wait_ge(s_mem["kvr"].h, s_mem["kvr"].at(l, 1))
                for p in range(2):
                    for j in range(2):
                        last = tr(PP[6][:, p * T + j * P:p * T + (j + 1) * P], T1[:, j, p * P:(p + 1) * P], P)
                last.then_inc(s_mem["kt"].h, 1)
                pe.wait_ge(s_const.h, 32)
                pe.wait_ge(s_lw.h, s_lw.at(l, s_lw.n))
                mm(PP[0][:, 0:NS], shn[:, 0:P], ident[0:NS, 0:NS])
                for i in range(1, 7):
                    tr(PP[0][:, i * NS:(i + 1) * NS], shn[:, i * P:(i + 1) * P], NS)
                for p in range(2):
                    tr(PP[0][:, 64 + 16 * p:80 + 16 * p], cvn[:, p * P:(p + 1) * P], 16)
                for h in range(NH):
                    last = tr(PP[7][0:64, h * P:(h + 1) * P], wukn[:, h * 64:(h + 1) * 64], P)
                last.then_inc(s_wt.h, 1)
                pe.wait_ge(s_const.h, 32)
                pe.wait_ge(s_wr.h, s_wr.at(l, 1))
                for j in range(2):
                    turn_x(l * IT, j)

                def block(B, m, e):
                    pe.wait_ge(s_hT.h, s_hT.at(B.it, 2))
                    project(B)
                    rwkv_chunks(B)
                    group_norm(B, 0)
                    group_norm(B, 1)
                    attention(B, l, m, e)
                    attention_out(B)
                    memory(B)
                    project_out(B)
                prompt_loop(lambda: pe, block, l)
                B = Block(l, None)
                prompt_states(l)
                pe.wait_ge(s_const.h, 32)
                pe.wait_ge(s_fpr.h, s_fpr.at(l, 1))
                pe.wait_ge(s_hT.h, s_hT.at(B.it, 2))
                project(B)
                sample_rwkv(l)
                group_norm(B, 0)
                group_norm(B, 1)
                sample_attention(l)
                attention_out(B)
                sample_memory(l)
                project_out(B)

        @blk.vector
        def _(v):
            def drain():
                v.drain()

            def scalars(ap, n):
                return ap.unsqueeze(2).broadcast_to([ap.shape[0], ap.shape[1], n])

            def inverse_roots(want, done, last, it, upto, k=1):
                last.then_inc(want.h, k)
                v.wait_ge(done.h, done.at(it, upto))

            def normalise_rows(sums, ready, turned, want, done, it, tiles, w, k):
                for j in range(tiles):
                    v.wait_ge(sums.h, sums.at(it, (j + 1) if tiles == 2 else 2))
                    if j:
                        v.wait_ge(turned.h, turned.at(it, j))
                    last = v.tensor_scalar(st[0:w, 4 + j:5 + j], st[0:w, j:j + 1], 1.0 / D, EPS, MULT, ADD)
                    inverse_roots(want, done, last, it, (j + 1) * k, k)
                    v.tensor_scalar(xn[0:w, :], memx[0:w, j, :], st[0:w, 4 + j:5 + j], None, MULT).then_inc(ready.h, k)

            def halves(bank, n, parts=P):
                return PP[bank][0:parts, :].rearrange("p (a t) -> p a t", a=2)[:, :, 0:n]

            def take_h(turned, ready, it, gain, n):
                v.wait_ge(turned.h, turned.at(it, 2))
                for i in range(4):
                    last = v.tensor_tensor(hT[:, 2 * i:2 * i + 2, 0:n], halves(i, n), scalars(V(gain, 2 * i, 2), n), MULT)
                last.then_inc(ready.h, 1)

            def shift(B, a0, a1, seen):
                n = B.n
                v.wait_ge(s_pa.h, s_pa.at(B.it, seen))
                cur = pr[:, a0:a1, 1:1 + n]
                d = T3[:, 0:a1 - a0, 0:n]
                if B.prompt:
                    v.tensor_copy(halo[:, a0:a1], pr[:, a0:a1, n:n + 1].rearrange("p a o -> p (a o)"))
                    v.tensor_tensor(d, pr[:, a0:a1, 0:n], cur, SUB)
                else:
                    v.tensor_copy(raw[:, a0:a1, :], cur)
                    v.tensor_tensor(d, shs[:, a0:a1, 0:n], cur, SUB)
                drain()
                v.tensor_tensor(d, d, scalars(V("mu", a0, a1 - a0), n), MULT)
                drain()
                last = v.tensor_tensor(cur, cur, d, ADD)
                if B.prompt:
                    last = v.tensor_copy(pr[:, a0:a1, 0:1], halo[:, a0:a1].unsqueeze(2))
                last.then_inc(s_shift.h, 1)
                drain()

            def rwkv_prepare(B):
                it, n = B.it, B.n
                kx, rx, vx = (pr[:, i:i + 2, 1:1 + n] for i in (2, 0, 4))
                t1, t2, t3, s_, a_ = (t[:, :, 0:n] for t in (T1, T2, T3, sw, aa))
                shift(B, 6, 7, 1)
                shift(B, 2, 4, 3)
                v.tensor_tensor(t1, kx, scalars(V("kk", 0, 2), n), MULT)
                drain()
                v.tensor_tensor(t2, t1, t1, MULT).then_inc(s_sq.h, 1)
                shift(B, 0, 2, 5)
                shift(B, 4, 6, 7)
                v.wait_ge(s_lor.h, s_lor.at(it, 1))
                v.tensor_scalar(s_, s_, 0.5, 0.5, MULT, ADD)
                last = v.tensor_scalar(a_, a_, 0.5, 0.5, MULT, ADD)
                drain()
                if B.prompt:
                    for p in range(2):
                        v.tensor_tensor_scan(Ls[:, p, :], K("scan"), sw[:, p, :], 0.0, MULT, ADD)
                    drain()
                    last = v.tensor_tensor(T3[:, :, :], Ls[:, :, :], sw[:, :, :], SUB)
                    last.then_inc(s_sg.h, 1)
                else:
                    v.tensor_copy(Ls[:, :, 0:n], s_).then_inc(s_sg.h, 1)
                v.wait_ge(s_pa.h, s_pa.at(it, 11))
                v.tensor_tensor(sqn[:, 0, 0:n], ckr[:, 0:n], ckr[:, 0:n], MULT)
                v.tensor_tensor(sqn[:, 1:3, 0:n], qd[:, :, 0:n], qd[:, :, 0:n], MULT).then_inc(s_nq.h, 1)
                v.wait_ge(s_sqd.h, s_sqd.at(it, 1))
                v.tensor_scalar(t2, halves(6, n), 1e-12, None, ADD)
                v.wait_ge(s_nqd.h, s_nqd.at(B.it, 1))
                v.tensor_scalar(sqn[:, 0, 0:n], PP[7][:, 0:n], 1.0 / R, EPS, MULT, ADD)
                v.tensor_scalar(sqn[:, 1, 0:n], PP[7][:, T:T + n], 1.0 / 256, EPS, MULT, ADD).then_inc(s_rw.h, 1)
                v.wait_ge(s_rd.h, s_rd.at(it, 1))
                v.reciprocal(t2, t2)
                v.reciprocal(sqn[:, 0:2, 0:n], sqn[:, 0:2, 0:n])
                drain()
                v.tensor_tensor(t1, t1, t2, MULT)
                drain()
                for p in range(2):
                    v.tensor_scalar(T2[:, p, 0:n], aa[:, p, 0:n], -1.0, V("ka", p), ADD, MULT)
                drain()
                v.scalar_tensor_tensor(kx, t2, 1.0, kx, ADD, MULT)
                drain()
                v.tensor_tensor(t2, rx, kx, MULT)
                drain()
                v.tensor_tensor(t2, t2, scalars(V("rk", 0, 2), n), MULT).then_inc(s_bo.h, 1)
                b_ = Bp[:, :, 0:n]
                v.tensor_tensor(b_, t1, a_, MULT)
                v.wait_ge(s_const.h, 32)
                v.wait_ge(s_dec.h, s_dec.at(it, 1))
                if B.prompt:
                    drain()
                    v.tensor_tensor(b_, b_, eN[:, :, :], MULT)
                    v.tensor_tensor(Kt[:, :, :], kx, eN[:, :, :], MULT)
                    tt = lambda t: t.rearrange("p a (j t) -> p a j t", j=2)
                    v.tensor_tensor(KR[:, :, :, 0, :], tt(T1[:, :, :]), tt(eK[:, :, :]), MULT)
                    last = v.tensor_tensor(KR[:, :, :, 1, :], tt(rx), tt(eP[:, :, :]), MULT)
                else:
                    drain()
                    last = v.tensor_copy(Ls[:, :, 0:n], t1)
                last.then_inc(s_rt.h, 1)
                drain()

            def latents(B):
                n = B.n
                v.scalar_tensor_tensor(ckr[:, 0:n], ckr[:, 0:n], V("kn"), sqn[:, 0, 0:n], MULT, MULT)
                for t in range(2):
                    last = v.scalar_tensor_tensor(qd[:, t, 0:n], qd[:, t, 0:n], V("qn", t), sqn[:, 1, 0:n], MULT, MULT)
                last.then_inc(s_qn.h, 1)
                drain()
                v.wait_ge(s_bod.h, s_bod.at(B.it, 1))
                v.tensor_tensor(bon[:, :, 0:n], halves(6, n), pr[:, 4:6, 1:1 + n], MULT).then_inc(s_bor.h, 1)

            def convolution(B):
                n, it = B.n, B.it
                t0 = DVE_TILES[0]
                v.wait_ge(s_pa.h, s_pa.at(it, 15))
                for p in range(2):
                    v.wait_ge(s_pj.h, s_pj.at(it, t0 + p + 1))
                    v.tensor_tensor(u[:, p, 2:2 + n], PP[(t0 + p) % 4][:, 0:n], cxs[:, p, 0:n], MULT).then_inc(s_pv.h, 1)
                drain()
                for p in range(2):
                    taps = [u[:, p, 0:n], u[:, p, 1:1 + n]] if B.prompt else [cvs[:, p, :, 0], cvs[:, p, :, 1]]
                    v.tensor_scalar(T3[:, p, 0:n], taps[0], V("conv", p), None, MULT)
                    drain()
                    v.scalar_tensor_tensor(T3[:, p, 0:n], taps[1], V("conv", 2 + p), T3[:, p, 0:n], MULT, ADD)
                    drain()
                    v.scalar_tensor_tensor(T3[:, p, 0:n], u[:, p, 2:2 + n], V("conv", 4 + p), T3[:, p, 0:n], MULT, ADD)
                if B.prompt:
                    drain()
                    v.tensor_copy(u[:, :, 0:2], u[:, :, n:n + 2])
                drain()
                for p in range(2):
                    t = DVE_TILES[2 + p]
                    v.wait_ge(s_pj.h, s_pj.at(it, t + 1))
                    v.tensor_tensor(mix[:, p, 0:n], PP[t % 4][:, 0:n], T3[:, p, 0:n], MULT).then_inc(s_pv.h, 1)

            def gates(B, which, dst):
                n = B.n
                for p in range(2):
                    i = 2 * which + p
                    t = DVE_TILES[4 + i]
                    g = ge[:, i % 2, 0:n]
                    v.wait_ge(s_ge.h, s_ge.at(B.it, i + 1))
                    if which == 0:
                        v.scalar_tensor_tensor(g, g, 1.0, PP[t % 4][:, 0:n], ADD, MULT)
                        drain()
                        v.scalar_tensor_tensor(mix[:, p, 0:n], mix[:, p, 0:n], 0.5, g, MULT, MULT).then_inc(s_pv.h, 1)
                    else:
                        v.scalar_tensor_tensor(mix[:, dst + p, 0:n], g, 1.0, PP[t % 4][:, 0:n], ADD, MULT).then_inc(s_pv.h, 1)

            def rotate_queries(B):
                n = B.n
                cos, sin = (cs[:, i:i + 1, 0:n].broadcast_to([RD, NH, n]) for i in range(2))
                v.wait_ge(s_cs.h, s_cs.at(B.it, 16))
                v.wait_ge(s_ql.h, s_ql.at(B.it, 2))
                v.wait_ge(s_qpr.h, s_qpr.at(B.it, 2))
                tmp = OT[0:RD, :, 0:n]
                for i in range(2):
                    v.tensor_tensor(OT[0:RD, 2 * i:2 * i + 2, 0:n], halves(6 + i, n, RD),
                                    cs[:, 1:2, 0:n].broadcast_to([RD, 2, n]), MULT)
                v.tensor_tensor(qr[:, :, 0:n], qr[:, :, 0:n], cos, MULT)
                drain()
                out = Q96[NOPE:NOPE + RD, :, :] if B.prompt else qr2[:, :, :]
                v.tensor_tensor(out, qr[:, :, 0:n], tmp, ADD).then_inc(s_qlr.h, 1)

            def store_latents(B):
                n = B.n
                v.wait_ge(s_kr.h, s_kr.at(B.it, 1))
                v.tensor_tensor(T3[0:RD, 0, 0:n], PP[4][0:RD, 0:n], cs[:, 1, 0:n], MULT)
                v.tensor_tensor(krr[:, 0:n], krr[:, 0:n], cs[:, 0, 0:n], MULT)
                drain()
                v.tensor_tensor(krr[:, 0:n], krr[:, 0:n], T3[0:RD, 0, 0:n], ADD).then_inc(s_krr.h, 1)
                drain()
                v.wait_ge(s_kr.h, s_kr.at(B.it, 2))
                if B.prompt:
                    v.tensor_scalar(ckvN[:, bass.ds(B.block * 2, 2), :], PP[5][:, 0:T].rearrange("p (a t) -> p a t", a=2), 1.0, None, MULT)
                    v.tensor_scalar(keysT[NOPE:NOPE + RD, :, bass.ds(B.tok, n)], krr[:, :].unsqueeze(1).broadcast_to([RD, NH, n]), 1.0, None, MULT)
                v.tensor_copy(st[:, 47:48], st[:, 46:47]).then_inc(s_kvd.h, 1)
                drain()

            def rwkv_chunks(B):
                ip = B.ip

                def level_block(lev, j):
                    if lev:
                        v.wait_ge(s_q.h, s_q.at(ip, (lev - 1) * 4 + 2 * j + 2))
                    v.tensor_tensor(Om[j], An[j], mlev[:, lev + 1:lev + 2, :].broadcast_to([P, NH, P]), MULT).then_inc(s_om.h, 1)
                for j in range(2):
                    for p in range(2):
                        v.wait_ge(s_gr.h, s_gr.at(ip, 2 * j + p + 1))
                        for h in range(2):
                            q = 2 * p + h
                            g4 = PP[q][:, :].rearrange("p (a t) -> p a t", a=4)
                            v.tensor_tensor(XI[j][:, 0, q, :], g4[:, 0, :], K("m1t"), MULT)
                            v.tensor_tensor(gram2[j][:, q, :, :], g4[:, 1:3, :], mgram[:, 1:3, :], MULT)
                            last = v.tensor_tensor(gramF[j][:, q, :], g4[:, 3, :], mgram[:, 3, :], MULT)
                        last.then_inc(s_gm.h, 1)
                    v.wait_ge(s_ga.h, s_ga.at(ip, j + 1))
                    for h in range(2):
                        last = v.tensor_copy(An[j][:, h:h + 3:2, :], PP[6 + h][:, 0:2 * P].rearrange("p (a t) -> p a t", a=2))
                    last.then_inc(s_anr.h, 1)
                    drain()
                    v.tensor_tensor(XI[j][:, 1, :, :], An[j], mlev[:, 0:1, :].broadcast_to([P, NH, P]), MULT)
                    drain()
                    for k in range(2):
                        last = v.tensor_tensor(XI[j][:, k, :, :], ident.unsqueeze(1).broadcast_to([P, NH, P]), XI[j][:, k, :, :], SUB)
                    last.then_inc(s_grr.h, 1)
                    level_block(0, j)
                for lev in range(5):
                    if lev < 4:
                        for j in range(2):
                            level_block(lev + 1, j)
                    for j in range(2):
                        for p in range(2):
                            v.wait_ge(s_xx.h, s_xx.at(ip, lev * 4 + 2 * j + p + 1))
                            k = 2 if lev < 4 else 1
                            x = XI[j][:, 0:k, 2 * p:2 * p + 2, :]
                            d = PP[4 + 2 * j + p][:, :].rearrange("p (h k t) -> p k h t", h=2, k=2)[:, 0:k, :, :]
                            v.tensor_tensor(x, x, d, SUB).then_inc(s_xxr.h, 1)
                    drain()
                for j in range(2):
                    J = slice(j * P, (j + 1) * P)
                    for c in range(2):
                        Q = slice(64 * c, 64 * c + 64)
                        n0 = (j * 2 + c) * 2
                        for p in range(2):
                            v.wait_ge(s_x0.h, s_x0.at(ip, n0 + p + 1))
                            v.tensor_copy(X0[Q, p, :], PP[p][Q, 0:P]).then_inc(s_x0r.h, 1)
                        for p in range(2):
                            v.wait_ge(s_sa.h, s_sa.at(ip, n0 + p + 1))
                            v.tensor_scalar(SA[Q, p, :], PP[p][Q, P:2 * P], -1.0, None, MULT).then_inc(s_sar.h, 1)
                        for p in range(2):
                            dec = eP[:, p, j * P + c * 64 + 63:j * P + c * 64 + 64]
                            v.wait_ge(s_su.h, s_su.at(ip, n0 + p + 1))
                            v.scalar_tensor_tensor(BT[:, p, :], PP[2 + p][:, 0:P], dec, bones, MULT, MULT)
                            drain()
                            v.scalar_tensor_tensor(BD[:, p, :], BD[:, p, :], dec, BT[:, p, :], MULT, ADD).then_inc(s_sur.h, 1)
                            drain()
                    for p in range(2):
                        v.wait_ge(s_y.h, s_y.at(ip, 2 * j + p + 1))
                        v.tensor_copy(yy[:, p, J], PP[4 + p][:, 0:P]).then_inc(s_yr.h, 1)
                drain()

            def centre(B):
                n = B.n
                y = yy[:, :, 0:n]
                v.wait_ge(s_lm.h, s_lm.at(B.it, 1))
                v.scalar_tensor_tensor(y, halves(1, n), -1.0 / HD, y, MULT, ADD)
                drain()
                v.tensor_tensor(T2[:, :, 0:n], y, y, MULT).then_inc(s_lc.h, 1)

            def variance(B):
                n = B.n
                v.wait_ge(s_lv.h, s_lv.at(B.it, 1))
                v.tensor_scalar(T1[:, :, 0:n], halves(7, n), 1.0 / HD, LN_EPS, MULT, ADD).then_inc(s_rw.h, 1)

            def rwkv_finish(B):
                n = B.n
                y, t = yy[:, :, 0:n], T1[:, :, 0:n]
                v.wait_ge(s_rd.h, s_rd.at(B.it, 2))
                v.reciprocal(t, t)
                drain()
                v.tensor_tensor(y, y, t, MULT)
                drain()
                for p in range(2):
                    v.tensor_scalar(yy[:, p, 0:n], yy[:, p, 0:n], V("lg", p), V("lb", p), MULT, ADD)
                drain()
                v.tensor_tensor(y, y, bon[:, :, 0:n], ADD)
                drain()
                v.scalar_tensor_tensor(mix[:, 2:4, 0:n], mix[:, 2:4, 0:n], 0.5, y, MULT, MULT).then_inc(s_lvr.h, 1)

            def attention_begin(B):
                v.memset(ml[:, 0, :], NEG)
                v.memset(ml[:, 1, :], 0.0)
                v.memset(OO[:, :, :], 0.0).then_inc(s_ai.h, 1)
                drain()

            def attention(B, l, m, e):
                with v.Fori(0, m + 1) as kc:
                    n0 = v.snap(steps_before(l, m, e) + kc * 8)

                    def masked_max(s):
                        j = s // NH
                        o = nc.s_assert_within(FMZ - 128 * j + (kc - m) * KC - e * T, 0, FMZ,
                                               skip_runtime_bounds_check_because="kc is at most m")
                        v.wait_ge(s_at.h, n0 + max(s - 1, 0) + s_at.base)
                        v.wait_ge(s_as.h, n0 + (s + 1))
                        v.tensor_tensor(Sm[:, s % 2, :], PP[s % 2][:, :], fmask[:, bass.ds(o, KC)], ADD).then_inc(s_am.h, 1)
                        drain()
                        v.tensor_reduce(ml[:, 2, s:s + 1], Sm[:, s % 2, :], AX, MAX)
                        drain()
                        v.tensor_tensor(ml[:, 3, s:s + 1], ml[:, 2, s:s + 1], ml[:, 0, s:s + 1], MAX)
                        drain()
                        v.tensor_scalar(ml[:, 4, s:s + 1], ml[:, 3, s:s + 1], -MLA_SCALE, None, MULT)
                        v.tensor_tensor(ml[:, 5, s:s + 1], ml[:, 0, s:s + 1], ml[:, 3, s:s + 1], SUB).then_inc(s_an.h, 1)

                    def sums(s):
                        v.wait_ge(s_ae.h, n0 + (s + 1))
                        v.scalar_tensor_tensor(ml[:, 1, s:s + 1], ml[:, 1, s:s + 1], ml[:, 6, s:s + 1], ml[:, 7, s:s + 1], MULT, ADD)
                        v.tensor_copy(ml[:, 0, s:s + 1], ml[:, 3, s:s + 1])

                    def accumulate(s):
                        v.wait_ge(s_av.h, n0 + (s + 1) + s_av.base)
                        v.scalar_tensor_tensor(OO[:, s, :], OO[:, s, :], ml[:, 6, s:s + 1], PP[4 + s % 2][:, 0:R], MULT, ADD)\
                            .then_inc(s_ao.h, 1)
                    for s in range(8):
                        masked_max(s)
                        if s >= 1:
                            sums(s - 1)
                        if s >= 2:
                            accumulate(s - 2)
                    sums(7)
                    accumulate(6)
                    accumulate(7)
                    drain()
                v.reciprocal(ml[:, 2, :], ml[:, 1, :])
                drain()
                v.tensor_tensor(OO[:, :, :], OO[:, :, :], scalars(ml[:, 2, :], P), MULT).then_inc(s_on.h, 1)

            def gate_attention(B):
                n = B.n
                v.wait_ge(s_uv.h, s_uv.at(B.it, 1))
                for p in range(2):
                    last = v.scalar_tensor_tensor(mix[:, 4 + p, 0:n], mix[:, 4 + p, 0:n], 0.5, PP[4 + p][:, 0:n], MULT, MULT)
                if B.prompt:
                    last.then_inc(s_uvr.h, 1)

            def memory(B):
                for j in range(2):
                    top, neg, _, _ = mst[j]
                    v.wait_ge(s_ms.h, s_ms.at(B.ip, j + 1))
                    for h in range(2):
                        v.tensor_reduce(top[:, 2 * h:2 * h + 2], halves(4 * j + h, T), AX, MAX)
                    drain()
                    v.tensor_scalar(neg, top, -MEM_SCALE, None, MULT).then_inc(s_mx.h, 1)
                for j in range(2):
                    _, _, total, inv = mst[j]
                    v.wait_ge(s_me.h, s_me.at(B.ip, j + 1))
                    v.reciprocal(inv, total)
                    drain()
                    v.tensor_tensor(Pm[j], Pm[j], scalars(inv, T), MULT).then_inc(s_mn.h, 1)
                v.wait_ge(s_mo.h, s_mo.at(B.ip, 1))
                v.scalar_tensor_tensor(mix[:, 6:8, :], mix[:, 6:8, :], 0.5, halves(6, T), MULT, MULT).then_inc(s_mix.h, 1)

            def residual(B):
                w, it = min(B.n, P), B.it
                v.wait_ge(s_xl.h, s_xl.at(it, 16))
                v.wait_ge(s_os.h, s_os.at(it, 1))
                for j in range(B.tiles):
                    r = st[0:w, 32 + j:33 + j]
                    v.tensor_tensor(r, st[0:w, 8 + 2 * j:9 + 2 * j], st[0:w, 9 + 2 * j:10 + 2 * j], ADD)
                    drain()
                    last = v.tensor_scalar(r, r, 1.0 / D, EPS, MULT, ADD)
                    k = 2 // B.tiles
                    inverse_roots(s_pw, s_pr, last, it, (j + 1) * k, k)
                    for i in range(2):
                        q = slice(i * 512, (i + 1) * 512)
                        v.scalar_tensor_tensor(xn[0:w, q], PP[4 + 2 * j + i][0:w, :], r, postg[0:w, q], MULT, MULT)
                    drain()
                    last = v.tensor_tensor(xin[0:w, j, :], xin[0:w, j, :], xn[0:w, :], ADD)
                    if j == B.tiles - 1:
                        last.then_inc(s_of.h, 1)
                    drain()

            def spread(vec3, sig_out, l, i):
                if i >= 1:
                    v.wait_ge(s_sb.h, s_sb.at(l, i))
                e4 = xn[:, :].rearrange("p (b a j) -> p b a j", b=NS, a=2)
                for a_ in range(2):
                    last = v.tensor_tensor(e4[:, :, a_, :], vec3[:, a_, :].unsqueeze(2).broadcast_to([P, NS, 64]),
                                           K("id64").unsqueeze(1).broadcast_to([P, NS, 64]), MULT)
                last.then_inc(sig_out.h, 1)

            def sample_rwkv(l):
                n = NS
                vecs = [eP[:, :, 0:n], Ls[:, :, 0:n], Bp[:, :, 0:n], pr[:, 2:4, 1:1 + n], pr[:, 0:2, 1:1 + n]]
                v.wait_ge(s_sl.h, s_sl.at(l, s_sl.n))
                spread(vecs[0], s_se, l, 0)
                sab = st[:, 0:16]
                for i in range(5):
                    if i < 4:
                        spread(vecs[i + 1], s_se, l, i + 1)
                    v.wait_ge(s_sb.h, s_sb.at(l, i + 1))
                    for q in range(2):
                        rows = PP[2 * (i % 2) + q][:, :].rearrange("p (a j) -> p a j", j=64)
                        s_ = S0[:, 8 * q:8 * q + 8, :]
                        w_ = SW[:, 8 * q:8 * q + 8, :]
                        if i == 0:
                            v.tensor_tensor(SD[:, 8 * q:8 * q + 8, :], s_, rows, MULT)
                        elif i == 1:
                            v.tensor_tensor(w_, s_, rows, MULT)
                            drain()
                            v.tensor_reduce(sab[:, 8 * q:8 * q + 8], w_, AX, ADD)
                            drain()
                        elif i == 2:
                            v.tensor_tensor(w_, rows, scalars(sab[:, 8 * q:8 * q + 8], 64), MULT)
                            drain()
                            v.tensor_tensor(SD[:, 8 * q:8 * q + 8, :], SD[:, 8 * q:8 * q + 8, :], w_, SUB)
                        elif i == 3:
                            for b in range(4):
                                vb = pr[:, 4:6, 1 + 4 * q + b:2 + 4 * q + b].broadcast_to([P, 2, 64])
                                v.tensor_tensor(w_[:, 2 * b:2 * b + 2, :], rows[:, 2 * b:2 * b + 2, :], vb, MULT)
                            drain()
                            v.tensor_tensor(SD[:, 8 * q:8 * q + 8, :], SD[:, 8 * q:8 * q + 8, :], w_, ADD)
                        else:
                            v.tensor_tensor(w_, SD[:, 8 * q:8 * q + 8, :], rows, MULT)
                            drain()
                            v.tensor_reduce(sab[:, 8 * q:8 * q + 8], w_, AX, ADD)
                    if i == 3:
                        drain()
                        v.tensor_copy(st[:, 47:48], st[:, 46:47]).then_inc(s_sst2.h, 1)
                drain()
                v.tensor_copy(yy[:, :, 0:n], sab.rearrange("p (b a) -> p a b", a=2)).then_inc(s_sy.h, 1)
                drain()

            def sample_attention(l):
                n = NS
                f = lambda t: t.rearrange("p (h b) -> p h b", h=NH)
                v.tensor_tensor(f(T1f[:, 0:32]), ql[:, :, 0:n], ckr[:, 0:n].unsqueeze(1).broadcast_to([P, NH, n]), MULT)
                v.tensor_tensor(f(T3f[0:RD, 0:32]), qr2[:, :, 0:n], krr[:, 0:n].unsqueeze(1).broadcast_to([RD, NH, n]), MULT)\
                    .then_inc(s_dp.h, 1)
                v.wait_ge(s_dq.h, s_dq.at(l, 1))
                src = PP[4][:, 0:32].rearrange("p (h b) -> p b h", h=NH)
                for t in range(4):
                    v.tensor_scalar(QR4[:, :, 4 * t:4 * t + 4], src, K("tmask")[:, t:t + 1], None, MULT)
                v.tensor_copy(sns[:, :, :], PP[4][:, 64:96].rearrange("p (h b) -> p b h", h=NH)).then_inc(s_dqr.h, 1)
                drain()

                def softmax_of(i, slot):
                    b, k = i * 2 + slot, l * NS + i * 2 + slot
                    o = PP[5 - slot][:, 0:P]
                    v.wait_ge(s_ds.h, k * 8 + (8 + s_ds.base))
                    v.tensor_reduce(st[:, 0:4], o.rearrange("p (c h) -> p h c", h=NH), AX, MAX).then_inc(s_dm1.h, 1)
                    v.wait_ge(s_dm2.h, k + 1)
                    sn = sns[:, bass.ds(b, 1), :].rearrange("p o h -> p (o h)")
                    v.tensor_copy(st[:, 47:48], st[:, 46:47])
                    v.tensor_tensor(st[:, 8:12], st[:, 4:8], sn, MAX)
                    drain()
                    v.tensor_tensor(T1f[:, 0:P].rearrange("p (c h) -> p c h", h=NH), o.rearrange("p (c h) -> p c h", h=NH),
                                    st[:, 8:12].unsqueeze(1).broadcast_to([P, 32, NH]), SUB)
                    v.tensor_tensor(T1f[:, P:P + 4], sn, st[:, 8:12], SUB).then_inc(s_dx.h, 1)
                    v.wait_ge(s_dxe.h, k + 1)
                    v.tensor_reduce(st[:, 16:20], Pb[:, 0:P].rearrange("p (c h) -> p h c", h=NH), AX, ADD).then_inc(s_de.h, 1)
                    v.wait_ge(s_dv.h, k + (1 + s_dv.base))
                    v.tensor_tensor(st[:, 20:24], PP[6][:, 64:68], Pb[:, P:P + 4], ADD)
                    drain()
                    v.reciprocal(st[:, 20:24], st[:, 20:24])
                    cn = ckr[:, bass.ds(b, 1)].broadcast_to([P, NH])
                    v.tensor_tensor(st[:, 24:28], Pb[:, P:P + 4], cn, MULT)
                    drain()
                    v.tensor_tensor(st[:, 24:28], st[:, 24:28], PP[6][:, 0:4], ADD)
                    drain()
                    v.tensor_tensor(OT[:, :, bass.ds(b, 1)], st[:, 24:28].unsqueeze(2), st[:, 20:24].unsqueeze(2), MULT).then_inc(s_da.h, 1)
                    drain()
                with v.Fori(0, NS // 2) as i:
                    softmax_of(i, 0)
                    softmax_of(i, 1)
                drain()
                v.tensor_copy(st[:, 47:48], st[:, 46:47]).then_inc(s_otr.h, 1)

            def sample_memory(l):
                for p in range(2):
                    if p:
                        v.wait_ge(s_qb.h, s_qb.at(l, 1))
                    v.tensor_tensor(xn[:, :].rearrange("p (b c) -> p b c", b=NS), mq[:, p, 0:NS].unsqueeze(2).broadcast_to([P, NS, P]),
                                    ident.unsqueeze(1).broadcast_to([P, NS, P]), MULT).then_inc(s_qe.h, 1)
                    v.wait_ge(s_qb.h, s_qb.at(l, p + 1))
                    for q in range(2):
                        v.tensor_copy(qB[:, 4 * q:4 * q + 4, p, :], PP[2 * p + q][:, :].rearrange("p (b c) -> p b c", b=4))
                drain()
                for q in range(2):
                    v.wait_ge(s_dml[q].h, s_dml[q].at(l, 128))
                    qb = qB[:, 4 * q:4 * q + 4, :, :].rearrange("p b a c -> p b (a c)")
                    for t in range(2):
                        v.tensor_tensor(dmp[:, :, t, :], dmk[q][:, :, t, :], qb, MULT)
                    drain()
                    v.tensor_reduce(st[:, 0:32], dmp[:, :, :, :].rearrange("p b t (h d) -> p (b t h) d", d=HD), AX, ADD)
                    drain()
                    s3 = st[:, 0:32].rearrange("p (b t h) -> p b t h", b=4, t=2)
                    m3 = T1f[:, 0:16].rearrange("p (b h) -> p b h", b=4)
                    v.tensor_tensor(m3, s3[:, :, 0, :], s3[:, :, 1, :], MAX).then_inc(s_dmx.h, 1)
                    v.wait_ge(s_dmr.h, s_dmr.at(l, q + 1))
                    g3 = T1f[:, 16:32].rearrange("p (b h) -> p b h", b=4)
                    for t in range(2):
                        last = v.tensor_tensor(s3[:, :, t, :], s3[:, :, t, :], g3, SUB)
                    last.then_inc(s_dms.h, 1)
                    v.wait_ge(s_dmo.h, s_dmo.at(l, q + 1))
                    d3 = PP[7][:, 0:32].rearrange("p (b t h) -> p b t h", b=4, t=2)
                    r3 = T1f[:, 32:48].rearrange("p (b h) -> p b h", b=4)
                    v.tensor_copy(r3, d3[:, :, 0, :])
                    drain()
                    v.tensor_tensor(r3, r3, d3[:, :, 1, :], ADD)
                    drain()
                    v.reciprocal(r3, r3)
                    drain()
                    o3 = PP[6][:, 0:16].rearrange("p (b a h) -> p b a h", b=4, a=2)
                    for h in range(2):
                        H = slice(64 * h, 64 * h + 64)
                        rr = T1f[H, 32:48].rearrange("p (b a h) -> p b a h", b=4, a=2)[:, :, :, h]
                        t4 = T1f[H, 48:56].rearrange("p (b a) -> p b a", b=4)
                        v.tensor_tensor(t4, o3[H, :, :, h], rr, MULT)
                        drain()
                        mx = mix[H, 6:8, 4 * q:4 * q + 4].rearrange("p a b -> p b a")
                        v.scalar_tensor_tensor(mx, mx, 0.5, t4, MULT, MULT)
                        drain()
                    v.tensor_copy(st[:, 47:48], st[:, 46:47]).then_inc(s_dm.h, 1)
                drain()
                v.tensor_copy(st[:, 47:48], st[:, 46:47]).then_inc(s_mix.h, 1)

            v.memset(st[:, 40:48], 0.0)
            v.memset(kv[:, 4096:10240], 0.0)
            v.memset(X0[:, :, :], 0.0)
            v.memset(SA[:, :, :], 0.0)
            drain()
            v.wait_ge(s_const.h, 32)
            with v.Fori(0, L) as l:
                v.wait_ge(s_vt.h, s_vt.at(l, 1))
                v.tensor_copy(vec[:, :], PP[7][:, 0:NVEC]).then_inc(s_vr.h, 1)
                v.memset(pr[:, :, 0:1], 0.0)
                v.memset(u[:, :, 0:2], 0.0)
                v.memset(BD[:, :, :], 0.0)
                drain()
                normalise_rows(s_mem["ss"], s_mem["xn"], s_mem["tp"], s_mem["pw"], s_mem["pr"], l, 2, P, 1)
                take_h(s_mem["tp"], s_mem["hT"], l, "mn", T)
                v.wait_ge(s_mem["kv"].h, s_mem["kv"].at(l, 2))
                for j in range(2):
                    v.tensor_copy(T1[:, j, :], PP[4 + j][:, 0:256])
                    last = v.tensor_copy(memV[:, j, :], PP[4 + j][:, 256:512])
                last.then_inc(s_mem["kvr"].h, 1)
                v.wait_ge(s_mem["kt"].h, s_mem["kt"].at(l, 1))
                v.tensor_copy(memKT[:, :, :], PP[6][:, :].rearrange("p (a m) -> p a m", a=2)).then_inc(s_mem["ktr"].h, 1)
                v.wait_ge(s_wt.h, s_wt.at(l, 1))
                v.tensor_copy(wukT[:, :, :], PP[7][0:64, :].rearrange("p (h r) -> p h r", h=NH))
                v.tensor_copy(shs[:, :, :], PP[0][:, 0:56].rearrange("p (a b) -> p a b", a=7))
                v.tensor_copy(cvs[:, :, :, :], PP[0][:, 64:96].rearrange("p (a b k) -> p a b k", a=2, b=NS)).then_inc(s_wr.h, 1)
                v.wait_ge(s_mem["out"].h, s_mem["out"].at(l, 64))
                v.tensor_copy(st[:, 47:48], st[:, 46:47])
                drain()

                def begin(B):
                    rwkv_prepare(B)
                    latents(B)
                    convolution(B)
                    rotate_queries(B)
                    gates(B, 0, 0)
                    store_latents(B)
                    gates(B, 1, 2)
                    gates(B, 2, 4)
                    gates(B, 3, 6)
                    drain()

                def block(B, m, e):
                    begin(B)
                    rwkv_chunks(B)
                    centre(B)
                    attention_begin(B)
                    variance(B)
                    attention(B, l, m, e)
                    rwkv_finish(B)
                    gate_attention(B)
                    memory(B)
                    residual(B)
                prompt_loop(lambda: v, block, l)
                B = Block(l, None)
                v.wait_ge(s_fp.h, s_fp.at(l, 1))
                v.tensor_copy(fst[0:7, 0:P], PP[0][0:7, 0:P])
                v.tensor_copy(fst[0:2, P:3 * P], PP[0][0:2, P:3 * P])
                v.tensor_copy(fst[:, 3 * P:5 * P], PP[1][:, 0:2 * P]).then_inc(s_fpr.h, 1)
                begin(B)
                sample_rwkv(l)
                v.wait_ge(s_sr.h, s_sr.at(l, 1))
                for i in range(2):
                    w = 512 if i == 0 else 384
                    v.tensor_copy(shn[:, i * 512:i * 512 + w], PP[4 + i][0:NS, 0:w])
                v.tensor_copy(cvn[0:NS, :], PP[7][0:NS, 0:256]).then_inc(s_srr.h, 1)
                centre(B)
                drain()
                variance(B)
                rwkv_finish(B)
                drain()
                sample_attention(l)
                gate_attention(B)
                drain()
                sample_memory(l)
                residual(B)

        @blk.scalar
        def _(act):
            act.wait_ge(s_mw.h, 32)
            act.dma_start(xres[0, 0:S, :], a["x_prompt"][0]).then_inc(s_xcopy.h, 16)
            act.dma_start(xres[0, S:S + NS, :], a["x_sample"][:, 0, :]).then_inc(s_xcopy.h, 16)
            for l in range(L):
                act.dma_start(xres[l, S + NS:S + T, :], a["x_prompt"][0, 0:T - NS, :]).then_inc(s_xcopy.h, 16)
            act.wait_ge(s_const.h, 32)
            with nc.allow_non_contiguous_dma(reason="rows of small states"), act.Fori(0, L) as l:
                sl, sn = bass.ds(l, 1), bass.ds(l + 1, 1)

                def squares(sums, it, tiles, w, k):
                    for j in range(tiles):
                        act.activation(junk[0:w, j * D:(j + 1) * D], memx[0:w, j, :], ACT.Square, accum_out=st[0:w, j:j + 1]).then_inc(sums.h, k)
                act.wait_ge(s_mtl.h, s_mtl.at(l, 16))
                squares(s_mem["ss"], l, 2, P, 1)
                act.wait_ge(s_mem["kvr"].h, s_mem["kvr"].at(l, 1))
                for j in range(2):
                    act.dma_start(a["mem_k"][sl, j * P:(j + 1) * P, :].rearrange("a m c -> (a m) c"), T1[:, j, :]).then_inc(s_mem["out"].h, 16)
                    act.dma_start(a["mem_v"][sl, j * P:(j + 1) * P, :].rearrange("a m c -> (a m) c"), memV[:, j, :]).then_inc(s_mem["out"].h, 16)

                def sum_squares(it):
                    act.wait_ge(s_x.h, s_x.at(it, 16))
                    for j in range(2):
                        if j:
                            act.drain()
                        act.activation(xn[:, :], xin[:, j, :], ACT.Square, accum_out=st[:, j:j + 1]).then_inc(s_ss.h, 1)

                    act.drain()

                def normalise(it, j):
                    if j:
                        act.wait_ge(s_xt.h, s_xt.at(it, j))
                    act.wait_ge(s_xr.h, s_xr.at(it, j + 1))
                    act.mul(xn[:, :], xin[:, j, :], st[:, 4 + j:5 + j]).then_inc(s_xn.h, 1)

                def take_h(it, j, k0, k1):
                    act.wait_ge(s_xt.h, s_xt.at(it, j + 1))
                    for dt in range(k0, k1):
                        last = act.mul(hT[:, dt, j * P:(j + 1) * P], PP[6 + dt // 4][:, (dt % 4) * P:(dt % 4 + 1) * P], V("pre", dt))
                    if k1 == KD:
                        last.then_inc(s_hT.h, 1)

                def begin(B):
                    it, n, w = B.it, B.n, min(B.n, P)
                    output_weights(it, 0, 2)
                    dst = {"wlal": pr[:, 6:7], "k": pr[:, 2:4], "r": pr[:, 0:2], "v": pr[:, 4:6], "qd": qd, "mq": mq, "cx": cxs}

                    def take(name):
                        for t, (g, i, c, f) in enumerate(TILES):
                            if GROUPS[g][0] != name:
                                continue
                            act.wait_ge(s_pj.h, s_pj.at(it, t + 1))
                            if name == "ckv":
                                if i == 0:
                                    act.wait_ge(s_coe.h, s_coe.at(it, 0))
                                o = ckr[:, 0:n] if i == 0 else krr[:, 0:n]
                            elif name in ("wlal", "k", "r", "v"):
                                o = dst[name][:, i, 1:1 + n]
                            else:
                                o = dst[name][:, i, 0:n]
                            act.activation(o, PP[t % 4][0:f, 0:n], ACT.Copy).then_inc(s_pa.h, 1)

                    def halves(bank, m, parts=P):
                        return PP[bank][0:parts, :].rearrange("p (a t) -> p a t", a=2)[:, :, 0:m]
                    take("wlal")
                    act.wait_ge(s_shift.h, s_shift.at(it, 1))
                    act.activation(pr[0:64, 6, 1:1 + n], pr[0:64, 6, 1:1 + n], ACT.Tanh).then_inc(s_th.h, 1)
                    take("k")
                    take("r")
                    take("v")
                    take("ckv")
                    act.wait_ge(s_lo.h, s_lo.at(it, 1))
                    for p in range(2):
                        act.activation(sw[:, p, 0:n], halves(4, n)[:, p, :], ACT.Tanh, bias=nvec[:, p:p + 1], scale=0.5)
                        last = act.activation(aa[:, p, 0:n], halves(5, n)[:, p, :], ACT.Tanh, bias=nvec[:, 2 + p:3 + p], scale=0.5)
                    last.then_inc(s_lor.h, 1)
                    take("qd")
                    act.wait_ge(s_sg.h, s_sg.at(it, 1))
                    act.activation(eP[:, :, 0:n], Ls[:, :, 0:n], ACT.Exp, scale=-DECAY)
                    if B.prompt:
                        act.activation(eN[:, :, :], Ls[:, :, :], ACT.Exp, scale=DECAY)
                        last = act.activation(eK[:, :, :], T3[:, :, :], ACT.Exp, scale=-DECAY)
                    else:
                        last = act.activation(eN[:, :, 0:n], Ls[:, :, 0:n], ACT.Copy)
                    last.then_inc(s_dec.h, 1)
                    take("mq")
                    act.wait_ge(s_rw.h, s_rw.at(it, 1))
                    act.activation(T2[:, :, 0:n], T2[:, :, 0:n], ACT.Sqrt)
                    act.activation(sqn[:, 0:2, 0:n], sqn[:, 0:2, 0:n], ACT.Sqrt).then_inc(s_rd.h, 1)
                    take("cx")
                    act.wait_ge(s_qp.h, s_qp.at(it, 1))
                    for i in range(2):
                        q = PP[4 + i][NOPE:NOPE + RD, :].rearrange("p (a t) -> p a t", a=2)[:, :, 0:n]
                        last = act.activation(qr[:, 2 * i:2 * i + 2, 0:n], q, ACT.Copy)
                    last.then_inc(s_qpr.h, 1)
                    for i in range(2):
                        last = act.activation(Q96[0:NOPE, 2 * i:2 * i + 2, 0:n], halves(4 + i, n, NOPE), ACT.Copy)
                    last.then_inc(s_qpr.h, 1)

                    def gate(i):
                        t = DVE_TILES[4 + i]
                        act.wait_ge(s_pj.h, s_pj.at(it, t + 1))
                        act.wait_ge(s_pv.h, s_pv.at(it, i + 3))
                        act.activation(ge[:, i % 2, 0:n], PP[t % 4][:, 0:n], ACT.Tanh, scale=0.5).then_inc(s_ge.h, 1)
                    act.wait_ge(s_ql.h, s_ql.at(it, 1))
                    for i in range(2):
                        if B.prompt:
                            o = keysT[0:NOPE, 2 * i:2 * i + 2, bass.ds(B.tok, n)]
                            last = act.activation(o, halves(4 + i, n, NOPE), ACT.Copy)
                        else:
                            last = act.activation(ql[:, 2 * i:2 * i + 2, :], halves(4 + i, n), ACT.Copy)
                    last.then_inc(s_qla.h, 1)
                    gate(0)
                    gate(1)
                    act.wait_ge(s_co.h, s_co.at(it, 0))
                    act.wait_ge(s_kvd.h, s_kvd.at(it, 1))
                    act.activation(cko[0:w, 0:B.tiles, :], PP[5][0:w, 0:B.tiles * P].rearrange("p (a t) -> p a t", t=P), ACT.Copy)
                    gate(2)
                    gate(3)
                    act.wait_ge(s_kn.h, s_kn.at(it, 1))
                    act.activation(kro[0:w, 0:B.tiles, :], PP[6][0:w, 0:B.tiles * RD].rearrange("p (a t) -> p a t", t=RD), ACT.Copy).then_inc(s_coe.h, 1)
                    act.wait_ge(s_coe.h, s_coe.at(it, 1))
                    for out, src in ((a["ckv"], cko), (a["krope"], kro)):
                        if B.prompt:
                            o = out[sl, bass.ds(B.tok, T), :].rearrange("a (t p) c -> p (a t) c", p=P)
                            act.dma_start(o, src[:, :, :]).then_inc(s_co.h, 16)
                        else:
                            act.dma_start(out[sl, S:S + NS, :].rearrange("a p c -> p (a c)"), src[0:NS, 0, :]).then_inc(s_co.h, 16)
                    for i in range(4, 8):
                        gate(i)

                def output_weights(it, k0, k1):
                    for k in range(k0, k1):
                        act.wait_ge(s_const.h, 32)
                        act.wait_ge(s_wou.h, s_wou.at(it, max(k - 1, 0)))
                        src = a["w_out"][sl, k * P:(k + 1) * P, :].rearrange("a p n -> (a p) n")
                        act.dma_start(wout[:, k % 2, :], src).then_inc(s_wo[k % 2].h, 16)

                def finish(B):
                    it, w = B.it, min(B.n, P)
                    output_weights(it, 2, KD)
                    act.wait_ge(s_wou.h, s_wou.at(it, KD))
                    for j in range(B.tiles):
                        for i in range(2):
                            last = act.activation(junk[0:w, (2 * j + i) * 512:(2 * j + i + 1) * 512], PP[4 + 2 * j + i][0:w, :], ACT.Square,
                                                  accum_out=st[0:w, 8 + 2 * j + i:9 + 2 * j + i])
                    last.then_inc(s_os.h, 1)
                    act.wait_ge(s_of.h, s_of.at(it, 1))
                    if B.prompt:
                        o = xres[sn, bass.ds(B.tok, T), :].rearrange("a (t p) d -> p (a t) d", p=P)
                        act.dma_start(o, xin[:, :, :]).then_inc(s_od.h, 16)
                    else:
                        act.dma_start(xres[sn, S:S + NS, :].rearrange("a p d -> p (a d)"), xin[0:NS, 0, :]).then_inc(s_od.h, 16)

                def variance_root(B):
                    act.wait_ge(s_rw.h, s_rw.at(B.it, 2))
                    act.activation(T1[:, :, 0:B.n], T1[:, :, 0:B.n], ACT.Sqrt).then_inc(s_rd.h, 1)

                def block(B, m, e):
                    ip = B.ip
                    begin(B)
                    def natural(j, bank, c0):
                        for p in range(2):
                            act.wait_ge(s_nt.h, s_nt.at(ip, 2 * j + p + 1))
                            act.activation(nat[:, p, :, :], PP[bank + p][:, c0:c0 + 3 * P].rearrange("p (a t) -> p a t", t=P), ACT.Copy).then_inc(s_ntr.h, 1)
                    natural(0, 4, 0)
                    sum_squares(B.it + 1)
                    normalise(B.it + 1, 0)
                    for lev in range(5):
                        for j in range(2):
                            for p in range(2):
                                k = lev * 4 + 2 * j + p + 1
                                act.wait_ge(s_q.h, s_q.at(ip, k))
                                if lev:
                                    act.wait_ge(s_xx.h, s_xx.at(ip, k - 4))
                                act.activation(Qs[j][:, 2 * p:2 * p + 2, :], PP[2 * j + p][:, 0:T].rearrange("p (a t) -> p a t", t=P), ACT.Copy).then_inc(s_qrd.h, 1)
                    take_h(B.it + 1, 0, 0, KD)
                    normalise(B.it + 1, 1)
                    natural(1, 2, P)
                    take_h(B.it + 1, 1, 0, KD)
                    variance_root(B)
                    with act.Fori(0, m + 1) as kc:
                        n0 = act.snap(steps_before(l, m, e) + kc * 8)

                        def probs(s):
                            act.wait_ge(s_an.h, n0 + (s + 1))
                            act.activation(Sm[:, s % 2, :], Sm[:, s % 2, :], ACT.Exp, bias=ml[:, 4, s:s + 1],
                                           scale=MLA_SCALE, accum_out=ml[:, 7, s:s + 1])
                            act.activation(ml[:, 6, s:s + 1], ml[:, 5, s:s + 1], ACT.Exp, scale=MLA_SCALE).then_inc(s_ae.h, 1)

                        def take(s):
                            act.wait_ge(s_at.h, n0 + (s + 1) + s_at.base)
                            act.wait_ge(s_av.h, n0 + max(s - 1, 0) + s_av.base)
                            act.activation(PT[:, s % 2, :, :], PP[2 + s % 2][:, :].rearrange("p (a t) -> p a t", a=4), ACT.Copy).then_inc(s_ar.h, 1)
                        probs(0)
                        for s in range(8):
                            if s < 7:
                                probs(s + 1)
                            take(s)
                    act.wait_ge(s_ot.h, s_ot.at(ip, 1))
                    for j in range(2):
                        last = act.activation(OT[:, :, j * P:(j + 1) * P], PP[6 + j][:, :].rearrange("p (h t) -> p h t", h=NH), ACT.Copy)
                    last.then_inc(s_otr.h, 1)
                    for j in range(2):
                        act.wait_ge(s_mx.h, s_mx.at(ip, j + 1))
                        for q in range(4):
                            last = act.activation(Pm[j][:, q, :], PP[4 * j + q // 2][:, (q % 2) * T:(q % 2) * T + T], ACT.Exp,
                                                  bias=mst[j][1][:, q:q + 1], scale=MEM_SCALE, accum_out=mst[j][2][:, q:q + 1])
                        last.then_inc(s_me.h, 1)
                    for j in range(2):
                        act.wait_ge(s_mt.h, s_mt.at(ip, j + 1))
                        for q in range(2):
                            last = act.activation(PTm[j][:, q, :, :], PP[2 - 2 * j + q][:, :].rearrange("p (a t) -> p a t", a=4), ACT.Copy)
                        last.then_inc(s_mtr.h, 1)
                    finish(B)
                act.wait_ge(s_vr.h, s_vr.at(l, 1))
                act.mul(nvec[:, 0:2], V("w0", 0, 2), 0.5)
                act.mul(nvec[:, 2:4], V("a0", 0, 2), 0.5)
                act.drain()
                act.wait_ge(s_mem["ktr"].h, s_mem["ktr"].at(l, 1))
                sum_squares(l * IT)
                for j in range(2):
                    normalise(l * IT, j)
                    take_h(l * IT, j, 0, KD)
                prompt_loop(lambda: act, block, l)
                act.wait_ge(s_fpr.h, s_fpr.at(l, 1))
                act.dma_start(a["shift_p"][sl, :].rearrange("a (n p) -> (a n) p", p=P), fst[0:7, 0:P]).then_inc(s_state.h, 16)
                act.dma_start(a["conv_p"][sl].rearrange("a k c -> (a k) c"), fst[0:2, P:3 * P]).then_inc(s_state.h, 16)
                for h in range(NH):
                    q, c = slice(64 * (h % 2), 64 * (h % 2) + 64), 3 * P + (h // 2) * P + 64 * (h % 2)
                    act.dma_start(a["st_p"][sl, h].rearrange("a i j -> (a i) j"), fst[q, c:c + 64]).then_inc(s_state.h, 16)
                B = Block(l, None)
                begin(B)
                variance_root(B)
                act.wait_ge(s_sst2.h, s_sst2.at(l, 1))
                for b in range(NS):
                    act.dma_start(a["st_s"][sl, b].rearrange("a (p h) i j -> (h i) (a p) j", p=2), SD[:, 2 * b:2 * b + 2, :]).then_inc(s_state.h, 16)
                act.wait_ge(s_srr.h, s_srr.at(l, 1))
                act.dma_start(a["shift_s"][sl].rearrange("a b c -> (a b) c"), shn[:, :]).then_inc(s_state.h, 16)
                act.dma_start(a["conv_s"][sl, :, 1, :].rearrange("a b c -> (a b) c"), cvn[0:NS, :]).then_inc(s_state.h, 16)
                act.dma_start(a["conv_s"][sl, :, 0, :].rearrange("a b c -> (a b) c"), a["state_conv"][sl, :, 1, :].rearrange("a b c -> (a b) c")).then_inc(s_state.h, 16)

                def copies(i, k, g0, g1):
                    n = l * NS + i * 2 + k
                    for g in range(g0, g1):
                        act.wait_ge(s_dt.h, n * 8 + (g + 1))
                        act.wait_ge(s_ds.h, n * 8 + (max(g - 1, 0) + s_ds.base))
                        act.activation(PT[:, g % 2, :, :], PP[g % 2][:, :].rearrange("p (a t) -> p a t", a=4), ACT.Copy)
                        act.activation(T2f[:, (g % 2) * P:(g % 2) * P + P], PP[2 + g % 2][:, 0:P], ACT.Copy).then_inc(s_dtr.h, 1)

                def exponentials(i, k):
                    act.wait_ge(s_dx.h, l * NS + i * 2 + (k + 1))
                    act.activation(Pb[:, 0:P + 4], T1f[:, 0:P + 4], ACT.Exp, scale=MLA_SCALE).then_inc(s_dxe.h, 1)

                def step(i, k):
                    nxt = (i, 1) if k == 0 else (i + 1, 0)
                    copies(*nxt, 0, 3)
                    exponentials(i, k)
                    copies(*nxt, 3, 8)
                copies(0, 0, 0, 8)
                with act.Fori(0, NS // 2 - 1) as i:
                    step(i, 0)
                    step(i, 1)
                step(NS // 2 - 1, 0)
                exponentials(NS // 2 - 1, 1)
                for q in range(2):
                    act.wait_ge(s_dms.h, s_dms.at(l, q + 1))
                    act.activation(Pb[:, 0:32], st[:, 0:32], ACT.Exp, scale=MEM_SCALE).then_inc(s_dme.h, 1)
                finish(B)

        @blk.gpsimd
        def _(pool):
            pool.memset(zero[:, :], 0)
            pool.memset(zerof[:, :], 0.0)
            pool.memset(mhalf[:, :], -0.5)
            pool.drain()
            pool.wait_ge(s_const.h, 32)
            with nc.allow_non_contiguous_dma(reason="page numbers"):
                for s in range(4):
                    pool.dma_start(pgi[s * NPG:(s + 1) * NPG, :], a["page_table"].rearrange("b n -> n b")).then_inc(s_pg.h, 16)
            pool.wait_ge(s_pg.h, 16 * 4)
            pool.tensor_copy(pgf[:, :], pgi[:, :])
            pool.drain()
            pool.tensor_scalar(pgf[:, :], pgf[:, :], 4.0, K("sub"), MULT, ADD)
            pool.drain()

            def root(want, done, it, n, ap, k=1):
                pool.wait_ge(s_const.h, 32)
                pool.wait_ge(want.h, want.at(it, n))
                half = mhalf[0:ap.shape[0], :]
                if len(ap.shape) == 3:
                    half = half.unsqueeze(2)
                pool.tensor_tensor(ap, ap, half.broadcast_to(list(ap.shape)), POW).then_inc(done.h, k)

            def x_roots(it):
                for j in range(2):
                    pool.wait_ge(s_const.h, 32)
                    pool.wait_ge(s_ss.h, s_ss.at(it, j + 1))
                    pool.tensor_tensor(st[:, 4 + j:5 + j], st[:, j:j + 1], zerof[:, 0:1], ADD)
                    pool.drain()
                    pool.tensor_scalar(st[:, 4 + j:5 + j], st[:, 4 + j:5 + j], 1.0 / D, EPS, MULT, ADD)
                    pool.drain()
                    pool.tensor_tensor(st[:, 4 + j:5 + j], st[:, 4 + j:5 + j], mhalf[:, :], POW).then_inc(s_xr.h, 1)

            def out_roots(B):
                w, k = min(B.n, P), 2 // B.tiles
                for j in range(B.tiles):
                    root(s_pw, s_pr, B.it, (j + 1) * k, st[0:w, 32 + j:33 + j], k)
            with pool.Fori(0, L) as l:
                for j in range(2):
                    root(s_mem["pw"], s_mem["pr"], l, j + 1, st[:, 4 + j:5 + j])

                x_roots(l * IT)

                def block(B, m, e):
                    x_roots(B.it + 1)
                    out_roots(B)
                prompt_loop(lambda: pool, block, l)
                B = Block(l, None)
                pool.tensor_copy(idx[:, :], pgf[:, :])
                pool.drain()
                pool.tensor_scalar(pgf[:, :], pgf[:, :], float(NPHYS * 4), None, ADD)
                pool.drain()

                def gather(b):
                    if b == 0:
                        pool.wait_ge(s_rt.h, s_rt.at(l * IT + NB, 1))
                    elif b == 1:
                        pool.wait_ge(s_pj.h, s_pj.at(l * IT + NB, NTILES))
                    else:
                        pool.wait_ge(s_dv.h, s_dv.at(l, b - 1))
                    pool.tensor_tensor(idc[:, b:b + 1], idx[:, b:b + 1], zero[:, :], ADD)
                    pool.drain()
                    for dst, cache in ((gat[b % 2], "cache_ckv"), (krg[b % 2], "cache_krope")):
                        pool.indirect_dma_start(dst, None, a[cache].rearrange("l n (g k) r -> (l n g) (k r)", g=4),
                                                bass.IndirectOffsetOnAxis(ap=idc[:, b:b + 1], axis=0)).then_inc(s_dg[b % 2].h, 16)
                gather(0)
                gather(1)
                for b in range(NS):
                    pool.wait_ge(s_dm1.h, l * NS + (b + 1))
                    pool.tensor_tensor(st[:, 12:16], st[:, 0:4], zerof[:, 0:4], ADD)
                    pool.drain()
                    pool.partition_all_reduce(st[:, 4:8], st[:, 12:16], P, bass.bass_isa.ReduceOp.max).then_inc(s_dm2.h, 1)
                    if b + 2 < NS:
                        gather(b + 2)
                for q in range(2):
                    pool.wait_ge(s_dmx.h, s_dmx.at(l, q + 1))
                    pool.tensor_tensor(T1f[:, 56:72], T1f[:, 0:16], zerof[:, :], ADD)
                    pool.drain()
                    pool.partition_all_reduce(T1f[:, 16:32], T1f[:, 56:72], P, bass.bass_isa.ReduceOp.max).then_inc(s_dmr.h, 1)
                out_roots(B)
    return nc


_OUTS = [("xres", (L + 1, S + T, D)), ("ckv", (L, S + NS, R)), ("krope", (L, S + NS, RD)),
         ("mem_k", (L, NM, 256)), ("mem_v", (L, NM, 256)), ("conv_p", (L, 2, 256)), ("conv_s", (L, NS, 2, 256)),
         ("shift_p", (L, 896)), ("shift_s", (L, NS, 896)), ("st_p", (L, NH, HD, HD)), ("st_s", (L, NS, NH, HD, HD))]


def kernel(**inputs):
    import concourse.bacc as bacc
    import ml_dtypes
    from concourse.bass_utils import run_bass_kernel_spmd

    nc = bacc.Bacc("TRN2", target_bir_lowering=False, num_devices=1)
    arrays = {k: np.ascontiguousarray(x) for k, x in inputs.items()}
    arrays["cst"] = constants()
    arrays["cs"] = rope_tables()
    q, c = np.arange(P)[:, None], np.arange(FMW)[None, :]
    arrays["fm"] = np.where(c <= q + FMZ, 0.0, NEG).astype(ml_dtypes.bfloat16)
    args = {k: nc.dram_tensor(f"in_{k}", x.shape, mybir.dt.from_np(x.dtype), kind="ExternalInput").ap()
            for k, x in arrays.items()}
    for k, shape in _OUTS:
        args[k] = nc.dram_tensor(f"out_{k}", shape, F32, kind="ExternalOutput").ap()
    build_program(nc, args)
    r = run_bass_kernel_spmd(nc, [{f"in_{k}": x for k, x in arrays.items()}], core_ids=[0])
    g = {k: r.results[0][f"out_{k}"] for k, _ in _OUTS}
    return (g["xres"][L, :S][None], g["xres"][L, S:S + NS][:, None],
            g["ckv"][:, :S][:, None], g["ckv"][:, S:][:, :, None],
            g["krope"][:, :S][:, None], g["krope"][:, S:][:, :, None],
            g["mem_k"].reshape(L, 1, NM, NH, HD), g["mem_v"].reshape(L, 1, NM, NH, HD),
            g["conv_p"][:, None], g["conv_s"], g["shift_p"][:, None], g["shift_s"],
            g["st_p"][:, None], g["st_s"])
```

```python
from contextlib import ExitStack

import concourse.bass as bass
import numpy as np
from concourse import mybir

F32 = mybir.dt.float32
BF16 = mybir.dt.bfloat16
I32 = mybir.dt.int32
ALU = mybir.AluOpType
ACT = mybir.ActivationFunctionType
AX = mybir.AxisListType.X
MULT, ADD, SUB, POW, MAX, MIN = ALU.mult, ALU.add, ALU.subtract, ALU.pow, ALU.max, ALU.min

P = 128
D = 1024
KD = D // P
L = 2
S = 2048
NS = 8
T = 256
NB = S // T
IT = NB + 1
C = 64
HD = 64
NH = 4
PAST, PAGE, NPHYS = 4096, 128, 320
NPG = PAST // PAGE
R, RD, NOPE = 128, 32, 64
NM = 256
KC = 512
DECAY = 0.6065306597
EPS, LN_EPS = 1e-6, 64e-5
MLA_SCALE = (NOPE + RD) ** -0.5
MEM_SCALE = HD ** -0.5
NEG = -1e30
STEPS = sum((b // 2 + 1) * 8 for b in range(NB))

GROUPS = [("wlal", 1792, 128), ("k", 1280, 256), ("r", 1024, 256), ("v", 1536, 256), ("ckv", 2432, 160),
          ("qd", 2176, 256), ("mq", 2848, 256), ("cx", 512, 256), ("cc", 256, 256), ("cb", 0, 256),
          ("cg", 768, 256), ("rg", 1920, 256), ("ag", 2592, 256), ("mg", 3104, 256)]
NG = len(GROUPS)
TILES = [(g, i, 128 * i, min(128, w - 128 * i)) for g, (_, _, w) in enumerate(GROUPS) for i in range((w + 127) // 128)]
NTILES = len(TILES)
BY_ACT = {"wlal", "k", "r", "v", "ckv", "qd", "mq", "cx"}
ACT_TILES = [t for t, x in enumerate(TILES) if GROUPS[x[0]][0] in BY_ACT]
LAST = [max(t for t, x in enumerate(TILES) if x[0] == g) for g in range(NG)]
DVE_TILES = [t for t, x in enumerate(TILES) if GROUPS[x[0]][0] not in BY_ACT]

OUT_ORDER = [0, 1, 4, 5, 6, 7, 2, 3]

VECS = [("pre", 8), ("conv", 6), ("mu", 7), ("w0", 2), ("a0", 2), ("kk", 2), ("ka", 2), ("rk", 2),
        ("lg", 2), ("lb", 2), ("qn", 2), ("kn", 1), ("mn", 8)]
VOFF, _o = {}, 0
for _n, _c in VECS:
    VOFF[_n] = _o
    _o += _c
NVEC = _o

CONSTS = [("ident", 128), ("bones", 128), ("ones", 128), ("mgram", 512), ("m1t", 128), ("mlev", 6 * 128),
          ("id64", 64), ("scan", 256), ("rot", 32), ("rep", 128),
          ("tmask", 4), ("sub", 1)]
COFF, _o = {}, 0
for _n, _c in CONSTS:
    COFF[_n] = _o
    _o += _c
NCONST = _o
FMZ = 15 * 128
FMW = FMZ + KC


def loads_of_slot(g):
    return 16 * sum(2 if GROUPS[q][1] == 0 else 1 for q in range(g % 2, g + 1, 2))


def constants():
    c = np.zeros((P, NCONST), np.float32)
    i = np.arange(P)
    r, q = i[:, None], i[None, :]

    def put(name, a):
        c[:, COFF[name]:COFF[name] + a.shape[1]] = a
    put("ident", (r == q) * 1.0)
    put("bones", (r // 64 == q // 64) * 1.0)
    put("ones", np.ones((P, P)))
    same = r // C == q // C
    put("mgram", np.concatenate([same & (r < q), same & (r <= q)] * 2, 1) * 1.0)
    lev = [(r // (2 * w) == q // (2 * w)) & (r % (2 * w) >= w) & (q % (2 * w) < w) for w in (1, 2, 4, 8, 16, 32)]
    put("m1t", lev[0].T * 1.0)
    put("mlev", np.concatenate(lev, 1) * 1.0)
    put("id64", (r % 64 == np.arange(64)[None, :]) * 1.0)
    put("scan", np.broadcast_to((np.arange(T) % C != 0)[None, :] * 1.0, (P, T)))
    rot = np.zeros((P, 32))
    for a in range(16):
        rot[a + 16, a] = -1.0
        rot[a, a + 16] = 1.0
    put("rot", rot)
    put("rep", (r == q % 32) * 1.0)
    put("tmask", (r // 32 == np.arange(4)[None, :]) * 1.0)
    put("sub", (i // 32)[:, None] * 1.0)
    return c


def rope_tables():
    half = RD // 2
    inv = np.power(np.float32(10000.0), (-np.arange(half, dtype=np.float32) / np.float32(half)))
    pos = np.concatenate([np.arange(S), np.full(NS, PAST)]).astype(np.float32)
    ang = inv.astype(np.float32)[:, None] * pos[None, :]
    ang = np.concatenate([ang, ang], 0)
    return np.stack([np.cos(ang), np.sin(ang)]).astype(np.float32)


class Block:

    def __init__(self, l, block, m=None, e=None):
        self.m, self.e = m, e
        self.l, self.block, self.prompt = l, block, block is not None
        self.px = l * (IT + 1) + block + 1 if self.prompt else l * (IT + 1)
        if self.prompt:
            self.it, self.ip, self.tok, self.n, self.tiles = l * IT + block, l * NB + block, block * T, T, 2
        else:
            self.it, self.n, self.tiles = l * IT + NB, NS, 1


class Sig:

    def __init__(self, ctx, nc, name, n, base=0):
        self.h, self.n, self.base = ctx.enter_context(nc.semaphore(name)), n, base

    def at(self, it, k):
        return it * self.n + (k + self.base)


def build_program(nc, a):
    ctx = ExitStack()
    with ctx:
        def sb(name, shape, dt=F32):
            return ctx.enter_context(nc.sbuf_tensor(name, shape, dt))

        begun = []

        def sig(name, n, base=0):
            s = Sig(ctx, nc, name, n, base)
            if base:
                begun.append(s)
            return s

        cst = sb("cst", [P, NCONST])
        fmask = sb("fmask", [P, FMW], BF16)
        win = sb("win", [P, 2, KD, 256])
        wout = sb("wout", [P, 2, D])
        hT = sb("hT", [P, KD, T + NS])
        sproj = sb("sproj", [P, NTILES, NS])
        mix = sb("mix", [P, 8, T])
        pr = sb("pr", [P, 7, T + 1])
        halo = sb("halo", [P, 7])
        qd = sb("qd", [P, 2, T])
        ckr = sb("ckr", [P, T])
        krr = sb("krr", [RD, T])
        mq = sb("mq", [P, 2, T])
        cxs = sb("cxs", [P, 2, T])
        u = sb("u", [P, 2, T + 2])
        kv = sb("kv", [P, 8192 + 2048])
        memKT = sb("memKT", [P, 2, NM])
        memV = sb("memV", [P, 2, 256])
        wuq = sb("wuq", [P, 2, 384])
        wukn = sb("wukn", [P, 256])
        wukT = sb("wukT", [64, NH, R])
        wuv = sb("wuv", [P, 256])
        w2a2 = sb("w2a2", [P, 256])
        vecrow = sb("vecrow", [NVEC, P])
        vec = sb("vec", [P, NVEC])
        postg = sb("postg", [P, D])
        cs = sb("cs", [RD, 2, T])
        xin = sb("xin", [P, 2, D])
        xn = sb("xn", [P, D])
        st = sb("st", [P, 48])
        T12 = sb("T12", [P, 4, T]); T1, T2 = T12[:, 0:2, :], T12[:, 2:4, :]
        sw = sb("sw", [P, 2, T]); aa = sb("aa", [P, 2, T])
        Ls = sb("Ls", [P, 2, T]); eP = sb("eP", [P, 2, T]); Bp = sb("Bp", [P, 2, T]); Kt = sb("Kt", [P, 2, T])
        bon = sb("bon", [P, 2, T])
        T3 = sb("T3", [P, 2, T])
        KR = sb("KR", [P, 2, 2, 2, P])
        nat = sb("nat", [P, 2, 3, P])
        G = sb("G", [P, NH, 4, P])
        XX = sb("XX", [P, NH, 2, P])
        X0 = sb("X0", [P, 2, P]); SA = sb("SA", [P, 2, P]); BD = sb("BD", [P, 2, P]);
        qr = sb("qr", [RD, NH, T])
        Q96 = sb("Q96", [NOPE + RD, NH, T])
        ql = sb("ql", [P, NH, NS]); qr2 = sb("qr2", [RD, NH, NS])
        Sm = sb("Sm", [P, 2, KC]); PT = sb("PT", [P, 2, 4, P]); OO = sb("OO", [P, 8, P]);
        ml = sb("ml", [P, 6, 8])
        shs = sb("shs", [P, 7, NS]); cvs = sb("cvs", [P, 2, NS, 2]); raw = sb("raw", [P, 7, NS])
        nvec = sb("nvec", [P, 4])
        cko = sb("cko", [P, 2, P]); kro = sb("kro", [P, 2, RD])
        sns = sb("sns", [P, NS, NH])
        pgi = sb("pgi", [P, NS], I32); pgf = sb("pgf", [P, NS]); idx = sb("idx", [P, NS], I32)
        idc = sb("idc", [P, NS], I32); zero = sb("zero", [P, 1], I32); zerof = sb("zerof", [P, 32]); mhalf = sb("mhalf", [P, 1])
        PP = [ctx.enter_context(nc.psum_tensor(f"bank{i}", [P, 512], F32)) for i in range(8)]

        keysT = kv[0:NOPE + RD, 0:8192].rearrange("p (h s) -> p h s", h=NH)
        ckvN = kv[:, 8192:10240].rearrange("p (t r) -> p t r", r=R)
        heads = lambda t: t[:, :, :].rearrange("p a t -> p (a t)").rearrange("p (h t) -> p h t", t=P)
        An, Om = [OO[:, 0:4, :], heads(sw)], [OO[:, 4:8, :], heads(aa)]
        ge = OO[:, 0:4, :].rearrange("p a t -> p (a t)").rearrange("p (i t) -> p i t", i=2)
        sqn = nat[:, :, :, :].rearrange("p a b t -> p (a b t)").rearrange("p (i t) -> p i t", i=3)
        yy = cxs
        Pm = [Sm[:, :, :].rearrange("p a (b t) -> p (a b) t", b=2), OO[:, :, :].rearrange("p (q b) t -> p q (b t)", b=2)]
        PTm = [PT, XX[:, :, :, :].rearrange("p h a t -> p (h a t)").rearrange("p (q i t) -> p q i t", q=2, i=4)]
        mst = [[st[:, 16 + 4 * i:20 + 4 * i] for i in range(4)], [ml[:, i, 0:4] for i in range(4)]]
        Qs, BT = [PT[:, 0, :, :], heads(Ls)], PT[:, 1, 0:2, :]
        XI = [XX[:, :, :, :].rearrange("p h k t -> p k h t"),
              T12[:, :, :].rearrange("p a t -> p (a t)").rearrange("p (k h t) -> p k h t", k=2, h=NH)]
        Smg = Sm[:, :, :].rearrange("p a k -> p (a k)").rearrange("p (h k t) -> p h k t", h=NH, k=2)
        gram2 = [G[:, :, 1:3, :], Smg]
        gramF = [G[:, :, 3, :], heads(T3)]
        eN, eK = (OO[:, 4 * i:4 * i + 4, :].rearrange("p a t -> p (a t)").rearrange("p (i t) -> p i t", i=2) for i in range(2))
        OT = XX[:, :, :, :].rearrange("p h a t -> p h (a t)")
        junk = G[:, :, :, :].rearrange("p h a t -> p (h a t)")
        fst = KR[:, :, :, :, :].rearrange("p a j k t -> p (a j k t)")[:, 0:5 * P]
        QR4 = KR[:, :, :, :, :].rearrange("p a j k t -> p (a j k t)")[:, 5 * P:6 * P].rearrange("p (b i) -> p b i", b=NS)
        Pb = nat[:, :, :, :].rearrange("p a b t -> p (a b t)")[:, 5 * P - 4:6 * P]
        shn = Q96[0:NS, :, :].rearrange("p h t -> p (h t)")[:, 0:896]
        cvn = qr[0:2 * NS, 0, :]
        memx = hT[:, :, :].rearrange("p k t -> p (k t)")[:, 0:2 * D].rearrange("p (j d) -> p j d", j=2)
        winf = win[:, :, :, :].rearrange("p s k n -> p (s k n)")
        gat = [kv[:, 0:4096], winf]
        krg = [kv[:, 4096:5120], hT[:, :, :].rearrange("p k t -> p (k t)")[:, 0:1024]]
        kvg = [x.rearrange("p (c r) -> p c r", r=R) for x in gat]
        mem2 = [kv[:, 6144:10240], kv[:, 0:4096]]
        dmk = [x[:, 0:2048].rearrange("p (b t c) -> p b t c", b=4, t=2) for x in mem2]
        dmv = [x[:, 2048:4096].rearrange("p (b t c) -> p b t c", b=4, t=2) for x in mem2]
        woutd = [wout[:, 0, :], wout[:, 1, :]] + [winf[:, i * D:(i + 1) * D] for i in range(4)] \
            + [kv[:, 6144 + i * D:6144 + (i + 1) * D] for i in range(2)]
        dmp = [Sm[:, :, :].rearrange("p a k -> p (a k)"), kv[:, 5120:6144]]
        S0 = Sm[:, :, :].rearrange("p a (b j) -> p (a b) j", j=64)
        SD = OO[:, :, :].rearrange("p a (b j) -> p (a b) j", j=64)
        SW = XX[:, :, :, :].rearrange("p a c (b j) -> p (a c b) j", j=64)
        qB = G[:, :, :, :].rearrange("p h a t -> p (h a t)").rearrange("p (b a c) -> p b a c", b=NS, a=2)
        T1f, T2f, T3f = (t[:, :, :].rearrange("p a t -> p (a t)") for t in (T1, T2, T3))
        msc, mmx, mpx, mgx, mrs, mpr = (T3f[:, a:b] for a, b in
                                        ((64, 128), (128, 160), (160, 192), (192, 224), (224, 256), (256, 272)))
        dav = T3f[0:NH, 272:272 + P]

        def K(name, n=None, m=P):
            w = dict(CONSTS)[name] if n is None else n
            return cst[0:m, COFF[name]:COFF[name] + w]

        def V(name, i=0, n=1):
            return vec[:, VOFF[name] + i:VOFF[name] + i + n]
        ident, bones, ones = K("ident"), K("bones"), K("ones")
        mgram = K("mgram").rearrange("p (a q) -> p a q", a=4)
        mlev = K("mlev").rearrange("p (a q) -> p a q", a=6)

        def bc(ap, shape):
            return ap.broadcast_to(shape)

        s_const = sig("const_loaded", 0)
        s_xcopy = sig("first_rows_copied", 0)
        s_xrest = sig("prompt_copied", 0)
        s_lvl = sig("layer_vectors_loaded", 16 * len(VECS))
        s_lw = sig("layer_weights_loaded", 16 * 8)
        s_mtl = sig("memory_tokens_loaded", 16)
        s_mw = sig("memory_weights_loaded", 32)
        s_vt = sig("vectors_transposed", 1)
        s_vr = sig("vectors_ready", 1, base=1)
        s_wr = sig("small_weights_read", 1)
        s_wt = sig("small_weights_transposed", 1)
        s_mem = {n: sig("mem_" + n, c, int(n == "out")) for n, c in dict(ss=2, xn=2, tp=2, hT=1, kv=2, kvr=1, kt=1, out=64, pw=2, pr=2).items()}
        s_state = sig("states_stored", 16 * (2 + NH + NS + 3), base=1)
        s_fp = sig("prompt_states_turned", 1)
        s_fpr = sig("prompt_states_read", 1)
        s_x = sig("x_loaded", 16)
        s_xl = sig("residual_loaded", 16)
        s_cs = sig("rope_tables_loaded", 16)
        s_ss = sig("x_squares_summed", 2)
        s_xr = sig("x_root_done", 2)
        s_xn = sig("x_normalised", 2, base=1)
        s_xt = sig("x_transposed", 2)
        s_hT = sig("h_ready", 2)
        s_wi = [sig(f"w_in_loaded{i}", loads_of_slot(NG - 2 + i)) for i in range(2)]
        s_pj = sig("projected", NTILES, base=1)
        s_pa = sig("projection_read_by_act", len(ACT_TILES))
        s_pv = sig("projection_read_by_dve", len(DVE_TILES))
        s_shift = sig("token_shift_done", 4)
        s_th = sig("tanh_ready", 1)
        s_lo = sig("lora_done", 1)
        s_lor = sig("lora_read", 1)
        s_sg = sig("decay_summed", 1)
        s_dec = sig("decay_factors_ready", 1)
        s_sq = sig("key_squares_ready", 1)
        s_sqd = sig("key_norms_done", 1)
        s_bo = sig("bonus_products_ready", 1)
        s_bod = sig("bonus_summed", 1)
        s_bor = sig("bonus_read", 1)
        s_nq = sig("latent_squares_ready", 1)
        s_nqd = sig("latent_norms_done", 1)
        s_qn = sig("latents_normalised", 1)
        s_qp = sig("queries_projected", 1)
        s_qpr = sig("queries_read", 2)
        s_ql = sig("latent_queries_done", 2)
        s_qla = sig("latent_queries_read", 1)
        s_qlr = sig("queries_rotated", 1)
        s_kr = sig("key_partner_and_latents_turned", 2)
        s_krr = sig("keys_rotated", 1)
        s_kn = sig("rotary_rows_done", 1)
        s_kvd = sig("latents_cached", 1, base=1)
        s_coe = sig("latent_rows_read", 1, base=1)
        s_ge = sig("gate_tanh_ready", 8)
        s_an = sig("running_max_ready", STEPS)
        s_co = sig("latents_written", 32, base=1)
        s_rt = sig("rwkv_operands_ready", 1)
        s_nt = sig("rwkv_transposed", 4)
        s_ntr = sig("rwkv_natural_ready", 4)
        s_gr = sig("grams_done", 4)
        s_gm = sig("grams_read", 4)
        s_ga = sig("natural_grams_done", 2)
        s_anr = sig("natural_grams_read", 2)
        s_grr = sig("grams_masked", 2)
        s_om = sig("level_block_ready", 10)
        s_q = sig("inverse_first_product", 20)
        s_qrd = sig("inverse_first_read", 20)
        s_xx = sig("inverse_second_product", 20)
        s_xxr = sig("inverse_updated", 20)
        s_x0 = sig("chunk_rhs_done", 8)
        s_x0r = sig("chunk_rhs_read", 8)
        s_sa = sig("chunk_solved", 8)
        s_sar = sig("chunk_solution_read", 8)
        s_su = sig("state_increment_done", 8)
        s_sur = sig("state_updated", 8)
        s_y = sig("rwkv_out_done", 4)
        s_yr = sig("rwkv_out_read", 4)
        s_lm = sig("mean_summed", 1)
        s_lc = sig("centred_squares_ready", 1)
        s_lv = sig("variance_summed", 1)
        s_lvr = sig("rwkv_group_done", 1)
        s_as = sig("scores_done", STEPS)
        s_am = sig("scores_masked", STEPS)
        s_ae = sig("probs_ready", STEPS)
        s_at = sig("probs_transposed", STEPS, base=1)
        s_ar = sig("probs_transposed_read", STEPS)
        s_av = sig("values_summed", STEPS, base=1)
        s_ao = sig("values_read", STEPS, base=1)
        s_on = sig("attention_normalised", 1)
        s_ot = sig("attention_transposed", 1)
        s_otr = sig("attention_transposed_read", 1)
        s_uv = sig("attention_projected", 1)
        s_uvr = sig("attention_gated", 1)
        s_ms = sig("mem_scores_done", 2)
        s_mx = sig("mem_max_ready", 2)
        s_me = sig("mem_exp_done", 2)
        s_mn = sig("mem_probs_ready", 2)
        s_mt = sig("mem_probs_transposed", 2)
        s_mtr = sig("mem_probs_read", 2)
        s_mo = sig("mem_values_done", 1)
        s_mix = sig("mixed_ready", 1)
        s_wo = [sig(f"w_out_loaded{i}", 16 * 4) for i in range(2)]
        s_wou = sig("w_out_used", KD, base=1)
        s_os = sig("out_squares_summed", 1)
        s_of = sig("residual_added", 1, base=1)
        s_od = sig("residual_stored", 16, base=1)
        s_pw = sig("root_wanted", 2)
        s_pr = sig("root_done", 2)
        s_rw = sig("square_root_wanted", 1)
        s_rd = sig("square_root_done", 1)
        s_vw = sig("variance_ready", 1)
        s_vd = sig("deviation_ready", 1)
        s_pg = sig("pages_loaded", 0)
        s_se = sig("spread_operand_ready", 5)
        s_sb = sig("rows_spread", 5)
        s_sl = sig("decode_states_loaded", 16 * NS)
        s_sst2 = sig("decode_states_updated", 1)
        s_sy = sig("decode_rwkv_out", 1)
        s_sr = sig("decode_rows_turned", 1)
        s_srr = sig("decode_rows_read", 1)
        s_dp = sig("own_score_products", 1)
        s_dq = sig("own_scores_and_spread_queries", 1)
        s_dqr = sig("decode_queries_ready", 1)
        s_dg = [sig(f"pages_gathered{i}", 32 * NS // 2) for i in range(2)]
        s_dt = sig("decode_keys_turned", 8 * NS)
        s_dtr = sig("decode_latents_read", 8 * NS, base=1)
        s_ds = sig("decode_scores_done", 8 * NS, base=1)
        s_dm1 = sig("decode_partition_max", NS)
        s_dm2 = sig("decode_max", NS)
        s_dx = sig("decode_scores_shifted", NS)
        s_dxe = sig("decode_exponentials", NS)
        s_de = sig("decode_probs_summed", NS)
        s_dv = sig("decode_values_done", NS, base=1)
        s_dvc = sig("decode_values_copied", NS)
        s_dvt = sig("decode_values_turned", NS)
        s_qe = sig("memory_query_operand", 2)
        s_qb = sig("memory_queries_spread", 2)
        s_dml = [sig(f"decode_memory_loaded{i}", 16 * 8) for i in range(2)]
        s_dmx = sig("memory_partition_max", 1)
        s_dmr = sig("memory_max", 1)
        s_dms = sig("memory_scores_shifted", 1)
        s_dme = sig("memory_exponentials", 1)
        s_dmo = sig("memory_values_done", 1)
        s_dmk = sig("first_memory_keys_used", 1)
        s_dm = sig("decode_memory_done", 1, base=1)

        xres, csd = a["xres"], a["cs"]
        blk = ctx.enter_context(nc.Block())

        def prompt_loop(eng, body, l):
            with eng().Fori(0, NB // 2) as m:
                with eng().Fori(0, 2) as e:
                    body(Block(l, m * 2 + e, m, e), m, e)

        def steps_before(l, m, e):
            return l * STEPS + (m + e) * (m + 1) * 8

        def steps_done(B):
            return steps_before(B.l, B.m, B.e) + (B.m + 1) * 8

        @blk.sync
        def _(sp):
            for s in begun:
                sp.sem_inc(s.h, 1)
            sp.dma_start(cst[:, :], a["cst"]).then_inc(s_const.h, 16)
            sp.dma_start(fmask[:, :], a["fm"]).then_inc(s_const.h, 16)
            sp.wait_ge(s_const.h, 32)
            with sp.Fori(0, L) as l:
                sl = bass.ds(l, 1)
                count = [0]

                def put(dst, src):
                    sp.dma_start(dst, src).then_inc(s_lw.h, 16)
                    count[0] += 16

                sp.wait_ge(s_const.h, 32)
                sp.wait_ge(s_dv.h, s_dv.at(l, 0))
                sp.dma_start(memx, a["mem_prompt"][0].rearrange("(t p) d -> p t d", p=P)).then_inc(s_mtl.h, 16)

                def rows(name, src):
                    n = dict(VECS)[name]
                    sp.dma_start(vecrow[VOFF[name]:VOFF[name] + n, :], src.rearrange("a (n p) -> (a n) p", p=P)).then_inc(s_lvl.h, 16)
                sp.wait_ge(s_const.h, 32)
                sp.wait_ge(s_vr.h, s_vr.at(l, 0))
                rows("pre", a["pre_norm_g"][sl, :])
                rows("conv", a["conv_w"][sl].rearrange("a k c -> a (k c)"))
                rows("mu", a["rwkv_mu"][sl, :])
                rows("w0", a["rwkv_w0"][sl, :])
                rows("a0", a["rwkv_a0"][sl, :])
                rows("kk", a["rwkv_k_k"][sl, :])
                rows("ka", a["rwkv_k_a"][sl, :])
                rows("rk", a["rwkv_r_k"][sl].rearrange("a h d -> a (h d)"))
                rows("lg", a["rwkv_lnx_g"][sl, :])
                rows("lb", a["rwkv_lnx_b"][sl, :])
                rows("qn", a["mla_q_norm_g"][sl, :])
                rows("kn", a["mla_kv_norm_g"][sl, :])
                rows("mn", a["mem_norm_g"][sl, :])
                wm = kv[:, 0:4096].rearrange("p (k n) -> p k n", k=KD)
                sp.wait_ge(s_const.h, 32)
                sp.wait_ge(s_dm.h, s_dm.at(l, 0))
                sp.dma_start(wm[:, :, 0:256], a["w_mem_k"][sl].rearrange("a (k p) n -> p (a k) n", p=P)).then_inc(s_mw.h, 16)
                sp.dma_start(wm[:, :, 256:512], a["w_mem_v"][sl].rearrange("a (k p) n -> p (a k) n", p=P)).then_inc(s_mw.h, 16)
                sp.wait_ge(s_const.h, 32)
                sp.wait_ge(s_od.h, s_od.at(l * IT, 0))
                def load_x(px, tok):
                    sp.wait_ge(s_xn.h, s_xn.at(px, 0))
                    sp.wait_ge(s_const.h, 32)
                    src = xres[sl, bass.ds(tok, T), :].rearrange("a (t p) d -> p (a t) d", p=P)
                    sp.dma_start(xin[:, :, :], src).then_inc(s_x.h, 16)

                sp.wait_ge(s_xcopy.h, 32 + 16 * L)
                load_x(l * (IT + 1), S)
                put(postg[:, :], a["post_norm_g"][sl, :].broadcast_to([P, D]))
                put(wuq[:, :, :], a["mla_w_uq"][sl].rearrange("a (t p) n -> p (a t) n", p=P))
                put(wukn[:, :], a["mla_w_uk"][sl].rearrange("a r h d -> (a r) (h d)"))
                put(wuv[:, :], a["mla_w_uv"][sl].rearrange("a r h d -> (a r) (h d)"))
                put(w2a2[0:64, :], a["rwkv_w2"][sl].rearrange("a r c -> (a r) c"))
                put(w2a2[64:128, :], a["rwkv_a2"][sl].rearrange("a r c -> (a r) c"))
                sp.wait_ge(s_const.h, 32)
                sp.wait_ge(s_state.h, s_state.at(l, 0))
                put(shn[:, :], a["state_rwkv_shift"][sl].rearrange("a b c -> (a b) c"))
                put(cvn[:, :], a["state_conv"][sl].rearrange("a b k c -> (a b k) c"))
                assert count[0] == s_lw.n
                with sp.If(l == 0):
                    sp.wait_ge(s_xcopy.h, 32 + 16 * L)
                    sp.dma_start(xres[0, T:S, :], a["x_prompt"][0, T:S, :]).then_inc(s_xrest.h, 16)

                sp.wait_ge(s_xrest.h, 16)

                def block(B):
                    it, tok, n = B.it, (B.tok if B.prompt else S), B.n
                    sp.wait_ge(s_const.h, 32)
                    sp.wait_ge(s_kvd.h, s_kvd.at(it, 0))
                    dst = cs[:, :, 0:n]
                    sp.dma_start(dst, csd[:, :, bass.ds(tok, n)].rearrange("c p t -> p c t")).then_inc(s_cs.h, 16)
                    if not B.prompt:
                        sp.wait_ge(s_const.h, 32)
                        sp.wait_ge(s_od.h, s_od.at(it, 0))
                        sp.dma_start(xin[0:n, 0, :], xres[sl, tok:tok + n, :].rearrange("a p d -> p (a d)")).then_inc(s_xl.h, 16)
                        return
                    for g, (_, c0, w) in enumerate(GROUPS):
                        if g == 6:
                            sp.wait_ge(s_const.h, 32)
                            sp.wait_ge(s_od.h, s_od.at(it, 0))
                            load_x(B.px + 1, tok + T)
                        sp.wait_ge(s_const.h, 32)
                        sp.wait_ge(s_pj.h, s_pj.at(B.ip, 0 if g < 2 else LAST[g - 2] + 1))
                        src = a["w_in"][sl, :, c0:c0 + w].rearrange("a (k p) n -> p (a k) n", p=P)
                        for k0, k1 in ([(0, KD)] if c0 else [(1, KD), (0, 1)]):
                            sp.dma_start(win[:, g % 2, k0:k1, 0:w], src[:, k0:k1, :]).then_inc(s_wi[g % 2].h, 16)

                def prompt_block(B, m, e):
                    block(B)
                    sp.wait_ge(s_const.h, 32)
                    sp.wait_ge(s_xn.h, s_xn.at(B.px + 1, 2))
                    src = xres[sl, bass.ds(B.tok, T), :].rearrange("a (t p) d -> p (a t) d", p=P)
                    sp.dma_start(xin[:, :, :], src).then_inc(s_xl.h, 16)
                prompt_loop(lambda: sp, prompt_block, l)
                block(Block(l, None))
                sp.wait_ge(s_const.h, 32)
                sp.wait_ge(s_rt.h, s_rt.at(l * IT + NB, 1))
                for b in range(NS):
                    sp.dma_start(S0[:, 2 * b:2 * b + 2, :],
                                 a["state_rwkv"][sl, b].rearrange("a (p h) i j -> (h i) (a p) j", p=2)).then_inc(s_sl.h, 16)
                for q in range(2):
                    if q:
                        sp.wait_ge(s_const.h, 32)
                        sp.wait_ge(s_dv.h, s_dv.at(l, NS - 1))
                    for b in range(4):
                        sp.dma_start(dmk[q][:, b, :, :], a["cache_mem_k"][sl, 4 * q + b].rearrange("a (t p) h d -> p (a t) (h d)", p=P)).then_inc(s_dml[q].h, 16)
                        sp.dma_start(dmv[q][:, b, :, :], a["cache_mem_v"][sl, 4 * q + b].rearrange("a (t p) h d -> p (a t) (h d)", p=P)).then_inc(s_dml[q].h, 16)
            sp.wait_ge(s_od.h, L * IT * s_od.n + 1)
            sp.wait_ge(s_state.h, L * s_state.n + 1)
            sp.wait_ge(s_co.h, L * IT * s_co.n + 1)
            sp.wait_ge(s_mem["out"].h, L * s_mem["out"].n + 1)

        @blk.tensor
        def _(pe):
            def mm(out, lhsT, rhs, start=True, stop=True):
                return pe.matmul(out, lhsT, rhs, start=start, stop=stop, skip_group_check=True)

            def tr(out, in_, w):
                return pe.transpose(out, in_, ident[0:w, 0:w])

            def transpose_rows(sig_in, sig_out, it, tiles, w, k):
                for j in range(tiles):
                    pe.wait_ge(s_const.h, 32)
                    pe.wait_ge(sig_in.h, sig_in.at(it, j + 1))
                    for dt in range(KD):
                        c = (dt % 2) * T + j * P
                        last = tr(PP[dt // 2][:, c:c + w], xn[0:w, dt * P:(dt + 1) * P], w)
                    last.then_inc(sig_out.h, k)

            def turn_x(px, j, k=1):
                if j:
                    pe.wait_ge(s_hT.h, s_hT.at(px, j))
                pe.wait_ge(s_const.h, 32)
                pe.wait_ge(s_xn.h, s_xn.at(px, j + k))
                for dt in range(KD):
                    last = tr(PP[6 + dt // 4][:, (dt % 4) * P:(dt % 4 + 1) * P], xn[:, dt * P:(dt + 1) * P], P)
                last.then_inc(s_xt.h, k)

            def halves(bank, n, parts=P):
                return PP[bank][0:parts, :].rearrange("p (a t) -> p a t", a=2)[:, :, 0:n]

            def project(B):
                it, n, w = B.it, B.n, min(B.n, P)
                for t, (g, i, c, f) in enumerate(TILES):
                    if B.prompt and i == 0:
                        pe.wait_ge(s_wi[g % 2].h, s_wi[g % 2].at(B.ip, loads_of_slot(g)))
                    if B.prompt and t >= 4:
                        q = t - 4
                        if q in ACT_TILES:
                            pe.wait_ge(s_pa.h, s_pa.at(it, ACT_TILES.index(q) + 1))
                        else:
                            pe.wait_ge(s_pv.h, s_pv.at(it, DVE_TILES.index(q) + 1))
                    if B.prompt:
                        for k in range(KD):
                            last = mm(PP[t % 4][0:f, 0:T + NS], win[:, g % 2, k, c:c + f], hT[:, k, :], k == 0, k == KD - 1)
                        last.then_inc(s_pj.h, 1)
                    if (t + 1 == NTILES) or TILES[t + 1][0] != g:
                        side = SIDE.get(GROUPS[g][0])
                        if side:
                            side(B)

            def lora(B):
                pe.wait_ge(s_const.h, 32)
                pe.wait_ge(s_of.h, s_of.at(B.it, 0))
                pe.wait_ge(s_th.h, s_th.at(B.it, 1))
                for r0, bank in ((0, 4), (64, 5)):
                    for p in range(2):
                        last = mm(halves(bank, B.n)[:, p, :], w2a2[r0:r0 + 64, p * P:(p + 1) * P],
                                  pr[r0:r0 + 64, 6, 1:1 + B.n])
                last.then_inc(s_lo.h, 1)

            def key_norms(B):
                pe.wait_ge(s_sq.h, s_sq.at(B.it, 1))
                mm(halves(6, B.n), bones, T2[:, :, 0:B.n]).then_inc(s_sqd.h, 1)

            def latent_norms(B):
                pe.wait_ge(s_nq.h, s_nq.at(B.it, 1))
                mm(PP[7][:, 0:B.n], ones, sqn[:, 0, 0:B.n])
                mm(PP[7][:, T:T + B.n], ones, sqn[:, 1, 0:B.n], True, False)
                mm(PP[7][:, T:T + B.n], ones, sqn[:, 2, 0:B.n], False, True).then_inc(s_nqd.h, 1)

            def bonus(B):
                pe.wait_ge(s_bo.h, s_bo.at(B.it, 1))
                mm(halves(6, B.n), bones, T2[:, :, 0:B.n]).then_inc(s_bod.h, 1)

            def queries(B):
                n = B.n
                pe.wait_ge(s_qn.h, s_qn.at(B.it, 1))
                pe.wait_ge(s_lor.h, s_lor.at(B.it, 1))
                for h in range(NH):
                    for t in range(2):
                        last = mm(PP[4 + h // 2][0:96, (h % 2) * T:(h % 2) * T + n], wuq[:, t, h * 96:h * 96 + 96],
                                  qd[:, t, 0:n], t == 0, t == 1)
                last.then_inc(s_qp.h, 1)

            def latent_queries(B):
                n = B.n
                pe.wait_ge(s_bor.h, s_bor.at(B.it, 1))
                pe.wait_ge(s_qpr.h, s_qpr.at(B.it, 2))
                for h in range(NH):
                    cols = slice((h % 2) * T, (h % 2) * T + n)
                    if B.prompt:
                        last = mm(PP[4 + h // 2][0:NOPE, cols], wukn[:, h * NOPE:(h + 1) * NOPE], ckr[:, 0:n])
                    else:
                        last = mm(PP[4 + h // 2][:, cols], wukT[:, h, :], Q96[0:NOPE, h, 0:n])
                last.then_inc(s_ql.h, 1)
                for i in range(2):
                    last = mm(halves(6 + i, n, RD), K("rot", m=RD), qr[:, 2 * i:2 * i + 2, 0:n])
                last.then_inc(s_ql.h, 1)

            def latents(B):
                w = min(B.n, P)
                pe.wait_ge(s_const.h, 32)
                pe.wait_ge(s_qla.h, s_qla.at(B.it, 1))
                mm(PP[4][0:RD, 0:B.n], K("rot", m=RD), krr[:, 0:B.n]).then_inc(s_kr.h, 1)
                for j in range(B.tiles):
                    last = tr(PP[5][0:w, j * P:j * P + P], ckr[:, j * P:j * P + w], P)
                last.then_inc(s_kr.h, 1)

            def rotary_rows(B):
                w = min(B.n, P)
                pe.wait_ge(s_const.h, 32)
                pe.wait_ge(s_qlr.h, s_qlr.at(B.it, 1))
                pe.wait_ge(s_krr.h, s_krr.at(B.it, 1))
                for j in range(B.tiles):
                    last = tr(PP[6][0:w, j * RD:(j + 1) * RD], krr[:, j * P:j * P + w], RD)
                last.then_inc(s_kn.h, 1)

            SIDE = dict(ckv=lora, qd=key_norms, mq=latent_norms, cc=bonus, cb=queries, cg=latent_queries,
                        rg=latents, ag=rotary_rows)

            def rwkv_chunks(B):
                ip = B.ip
                pe.wait_ge(s_rt.h, s_rt.at(B.it, 1))
                pe.wait_ge(s_kvd.h, s_kvd.at(B.it, 1))
                pe.wait_ge(s_coe.h, s_coe.at(B.it, 1))
                def natural(j, bank, c0):
                    for p in range(2):
                        if j:
                            pe.wait_ge(s_sur.h, s_sur.at(ip, 2 + p + 1))
                        for i, src in enumerate((pr[:, 4 + p, 1 + j * P:1 + (j + 1) * P], Kt[:, p, j * P:(j + 1) * P],
                                                 Bp[:, p, j * P:(j + 1) * P])):
                            last = tr(PP[bank + p][:, c0 + i * P:c0 + (i + 1) * P], src, P)
                        last.then_inc(s_nt.h, 1)

                natural(0, 4, 0)
                pe.wait_ge(s_pv.h, s_pv.at(B.it, len(DVE_TILES)))
                for j in range(2):
                    J = slice(j * P, (j + 1) * P)
                    for p in range(2):
                        if j:
                            pe.wait_ge(s_gm.h, s_gm.at(ip, p + 1))
                        for h in range(2):
                            q = slice(64 * h, 64 * h + 64)
                            mm(PP[2 * p + h][:, 0:T], Bp[q, p, J], KR[q, p, j, :, :])
                            last = mm(PP[2 * p + h][:, T:2 * T], Kt[q, p, J], KR[q, p, j, :, :])
                        last.then_inc(s_gr.h, 1)
                    if j:
                        pe.wait_ge(s_anr.h, s_anr.at(ip, 1))
                    for p in range(2):
                        for h in range(2):
                            q = slice(64 * h, 64 * h + 64)
                            last = mm(PP[6 + h][:, p * P:(p + 1) * P], KR[q, p, j, 0, :], Bp[q, p, J])
                    last.then_inc(s_ga.h, 1)
                for lev in range(5):
                    for j in range(2):
                        pe.wait_ge(s_om.h, s_om.at(ip, lev * 2 + j + 1))
                        if lev == 0:
                            pe.wait_ge(s_gm.h, s_gm.at(ip, 4))
                            pe.wait_ge(s_grr.h, s_grr.at(ip, j + 1))
                        for p in range(2):
                            if lev:
                                pe.wait_ge(s_xxr.h, s_xxr.at(ip, (lev - 1) * 4 + 2 * j + p + 1))
                            for h in range(2):
                                last = mm(PP[2 * j + p][:, h * P:(h + 1) * P], Om[j][:, 2 * p + h, :], XI[j][:, 0, 2 * p + h, :])
                            last.then_inc(s_q.h, 1)
                    if lev == 0:
                        pe.wait_ge(s_ntr.h, s_ntr.at(ip, 2))
                        pe.wait_ge(s_anr.h, s_anr.at(ip, 2))
                    for j in range(2):
                        for p in range(2):
                            pe.wait_ge(s_qrd.h, s_qrd.at(ip, lev * 4 + 2 * j + p + 1))
                            for h in range(2):
                                q, o = 2 * p + h, PP[4 + 2 * j + p]
                                last = mm(o[:, h * T:h * T + P], XI[j][:, 1, q, :], Qs[j][:, q, :])
                                if lev < 4:
                                    last = mm(o[:, h * T + P:(h + 1) * T], Qs[j][:, q, :], XI[j][:, 1, q, :])
                            last.then_inc(s_xx.h, 1)
                for j in range(2):
                    if j:
                        natural(1, 2, P)
                    for c in range(2):
                        n0 = (j * 2 + c) * 2
                        Q = slice(64 * c, 64 * c + 64)
                        for p in range(2):
                            if n0:
                                pe.wait_ge(s_sur.h, s_sur.at(ip, n0 - 2 + p + 1))
                            if c == 0:
                                pe.wait_ge(s_ntr.h, s_ntr.at(ip, j * 2 + p + 1))
                                pe.wait_ge(s_xxr.h, s_xxr.at(ip, 16 + 2 * j + p + 1))
                            mm(PP[p][Q, 0:P], KR[:, p, j, 0, Q], BD[:, p, :], True, False)
                            for h in range(2):
                                last = mm(PP[p][Q, 64 * h:64 * h + 64], gram2[j][:, 2 * p + h, 1, Q],
                                          nat[:, p, 0, 64 * h:64 * h + 64], False, h == 1)
                            last.then_inc(s_x0.h, 1)
                        for p in range(2):
                            if j and c == 0:
                                pe.wait_ge(s_yr.h, s_yr.at(ip, p + 1))
                            mm(PP[4 + p][:, Q], BD[:, p, :], KR[:, p, j, 1, Q], c == 0, False)
                        for p in range(2):
                            pe.wait_ge(s_x0r.h, s_x0r.at(ip, n0 + p + 1))
                            for h in range(2):
                                last = mm(PP[p][Q, P + 64 * h:P + 64 * h + 64], XI[j][:, 0, 2 * p + h, Q],
                                          X0[:, p, 64 * h:64 * h + 64])
                            last.then_inc(s_sa.h, 1)
                        for p in range(2):
                            pe.wait_ge(s_sar.h, s_sar.at(ip, n0 + p + 1))
                            mm(PP[2 + p][:, 0:P], nat[Q, p, 1, :], nat[Q, p, 0, :], True, False)
                            mm(PP[2 + p][:, 0:P], nat[Q, p, 2, :], SA[Q, p, :], False, True)\
                                .then_inc(s_su.h, 1)
                        if c == 0:
                            if j == 0:
                                pe.wait_ge(s_xxr.h, s_xxr.at(ip, 20))
                            turn_x(B.px + 1, j)
                    for p in range(2):
                        for h in range(2):
                            q = slice(64 * h, 64 * h + 64)
                            mm(PP[4 + p][q, 0:P], nat[:, p, 0, q], gramF[j][:, 2 * p + h, :], False, False)
                            last = mm(PP[4 + p][q, 0:P], SA[:, p, q], gram2[j][:, 2 * p + h, 0, :], False, h == 1)
                        last.then_inc(s_y.h, 1)

            def attention(B, l, m, e):
                n0 = steps_before(l, m, e)

                def scores(kc, s):
                    h, j = s % NH, s % 8 // NH
                    if s >= 2:
                        pe.wait_ge(s_am.h, n0 + (kc * 8 + (s - 1)))
                    mm(PP[s % 2][:, :], Q96[:, h, j * P:(j + 1) * P],
                       keysT[:, h, bass.ds((kc + s // 8) * KC, KC)]).then_inc(s_as.h, 1)

                def turn(kc, s):
                    pe.wait_ge(s_ae.h, n0 + (kc * 8 + (s + 1)))
                    if s >= 2:
                        pe.wait_ge(s_ar.h, n0 + (kc * 8 + (s - 1)))
                    for i in range(4):
                        last = tr(PP[2 + s % 2][:, i * P:(i + 1) * P], Sm[:, s % 2, i * P:(i + 1) * P], P)
                    last.then_inc(s_at.h, 1)

                def values(kc, s):
                    pe.wait_ge(s_ar.h, n0 + (kc * 8 + (s + 1)))
                    pe.wait_ge(s_ao.h, n0 + (kc * 8 + max(s - 1, 0) + s_ao.base))
                    for i in range(4):
                        last = mm(PP[4 + s % 2][:, 0:R], PT[:, s % 2, i, :], ckvN[:, bass.ds(kc * 4 + i, 1), :],
                                  i == 0, i == 3)
                    last.then_inc(s_av.h, 1)

                def step(kc, ahead):
                    for s in range(8):
                        if s + 1 < 8 or ahead:
                            turn(kc, s + 1)
                        if s + 3 < 8 or ahead:
                            scores(kc, s + 3)
                        values(kc, s)
                scores(0, 0)
                scores(0, 1)
                turn(0, 0)
                scores(0, 2)
                with pe.If(m > 0):
                    with pe.Fori(0, m) as kc:
                        step(kc, True)
                step(m, False)

            def attention_out(B):
                if B.prompt:
                    group_norm(B, 0)
                    pe.wait_ge(s_hT.h, s_hT.at(B.px + 1, 2))
                    pe.wait_ge(s_on.h, s_on.at(B.ip, 1))
                    for j in range(2):
                        for h in range(NH):
                            last = tr(PP[6 + j][:, h * P:(h + 1) * P], OO[:, j * NH + h, :], P)
                    last.then_inc(s_ot.h, 1)
                    group_norm(B, 1)
                pe.wait_ge(s_otr.h, s_otr.at(B.it, 1))
                for h in range(NH):
                    last = mm(PP[4 + h // 2][64 * (h % 2):64 * (h % 2) + 64, 0:B.n], wuv[:, 64 * h:64 * h + 64],
                              OT[:, h, 0:B.n])
                last.then_inc(s_uv.h, 1)

            def memory(B):
                def scores(j):
                    J = slice(j * P, (j + 1) * P)
                    for h in range(2):
                        q = slice(64 * h, 64 * h + 64)
                        for p in range(2):
                            last = mm(PP[4 * j + h][:, p * NM:(p + 1) * NM], mq[q, p, J], memKT[q, p, :])
                    last.then_inc(s_ms.h, 1)

                def turn(j):
                    if j == 0:
                        pe.wait_ge(s_vw.h, s_vw.at(B.it, 1))
                    pe.wait_ge(s_mn.h, s_mn.at(B.ip, j + 1))
                    b0 = 2 - 2 * j
                    for q in range(4):
                        for t in range(2):
                            last = tr(PP[b0 + q // 2][:, (q % 2) * T + t * P:(q % 2) * T + (t + 1) * P],
                                      Pm[j][:, q, t * P:(t + 1) * P], P)
                    last.then_inc(s_mt.h, 1)

                def values(j):
                    pe.wait_ge(s_mtr.h, s_mtr.at(B.ip, j + 1))
                    for h in range(2):
                        for p in range(2):
                            for t in range(2):
                                last = mm(PP[6][64 * h:64 * h + 64, p * T + j * P:p * T + (j + 1) * P],
                                          memV[:, t, (2 * p + h) * 64:(2 * p + h) * 64 + 64],
                                          PTm[j][:, h, 2 * p + t, :], t == 0, t == 1)
                    return last
                scores(0)
                pe.wait_ge(s_uvr.h, s_uvr.at(B.ip, 1))
                scores(1)
                turn(0)
                turn(1)
                values(0)
                values(1).then_inc(s_mo.h, 1)

            def group_norm(B, part):
                if part == 0:
                    if B.prompt:
                        pe.wait_ge(s_yr.h, s_yr.at(B.ip, 4))
                    else:
                        pe.wait_ge(s_sy.h, s_sy.at(B.l, 1))
                    if B.prompt:
                        pe.wait_ge(s_ar.h, steps_done(B))
                    mm(halves(2, B.n), bones, yy[:, :, 0:B.n]).then_inc(s_lm.h, 1)
                else:
                    pe.wait_ge(s_lc.h, s_lc.at(B.it, 1))
                    mm(halves(3, B.n), bones, T2[:, :, 0:B.n]).then_inc(s_lv.h, 1)

            def project_out(B):
                w = min(B.n, P)
                pe.wait_ge(s_mix.h, s_mix.at(B.it, 1))
                for i0, k in enumerate(OUT_ORDER):
                    if B.prompt:
                        pe.wait_ge(s_wo[i0 % 2].h, s_wo[i0 % 2].at(B.it, 16 * (i0 // 2 + 1)))
                    elif i0 < 2:
                        pe.wait_ge(s_wo[i0].h, s_wo[i0].at(B.it, 16 * KD // 2))
                    wo = wout[:, i0 % 2, :] if B.prompt else woutd[i0]
                    if k == 2:
                        pe.wait_ge(s_lvr.h, s_lvr.at(B.it, 1))
                    for j in range(B.tiles):
                        for i in range(2):
                            last = mm(PP[4 + 2 * j + i][0:w, :], mix[:, k, j * P:j * P + w], wo[:, i * 512:(i + 1) * 512],
                                      i0 == 0, i0 == KD - 1)
                    last.then_inc(s_wou.h, 1)

            def prompt_states(l):
                tr(PP[0][0:7, 0:P], halo[:, :], P)
                for p in range(2):
                    tr(PP[0][0:2, P + p * P:P + (p + 1) * P], u[:, p, 0:2], P)
                    last = tr(PP[1][:, p * P:(p + 1) * P], BD[:, p, :], P)
                last.then_inc(s_fp.h, 1)

            def sample_rwkv(l):
                pe.wait_ge(s_pv.h, s_pv.at(l * IT + NB, len(DVE_TILES)))
                for i in range(5):
                    pe.wait_ge(s_se.h, s_se.at(l, i + 1))
                    for q in range(2):
                        last = mm(PP[2 * (i % 2) + q][:, :], bones, xn[:, q * 512:(q + 1) * 512])
                    last.then_inc(s_sb.h, 1)
                for i in range(7):
                    tr(PP[4 + i // 4][0:NS, (i % 4) * P:(i % 4 + 1) * P], raw[:, i, :], P)
                for p in range(2):
                    last = tr(PP[7][0:NS, p * P:(p + 1) * P], u[:, p, 2:2 + NS], P)
                last.then_inc(s_sr.h, 1)

            def sample_attention(l):
                pe.wait_ge(s_dp.h, s_dp.at(l, 1))
                mm(PP[4][:, 0:32], K("rep", m=RD), qr2[:, :, 0:NS])
                mm(PP[4][:, 64:96], ones, T1f[:, 0:32], True, False)
                mm(PP[4][:, 64:96], ones[0:RD, :], T3f[0:RD, 0:32], False, True).then_inc(s_dq.h, 1)
                pe.wait_ge(s_const.h, 32)
                pe.wait_ge(s_dqr.h, s_dqr.at(l, 1))

                def keys(n, slot, g):
                    pe.wait_ge(s_dtr.h, n * 8 + (max(g - 1, 0) + s_dtr.base))
                    for i in range(4):
                        tr(PP[g % 2][:, i * P:(i + 1) * P], kvg[slot][:, 4 * g + i, :], P)
                    tr(PP[2 + g % 2][:, 0:P], krg[slot][:, g * P:(g + 1) * P], P).then_inc(s_dt.h, 1)

                def score(n, b, slot, g):
                    pe.wait_ge(s_dtr.h, n * 8 + (g + 1 + s_dtr.base))
                    o = PP[5 - slot]
                    mm(o[:, 16 * g:16 * g + 16], T2f[:, (g % 2) * P:(g % 2) * P + P], QR4[:, bass.ds(b, 1), :], True, False)
                    for i in range(4):
                        last = mm(o[:, 16 * g + 4 * i:16 * g + 4 * i + 4], PT[:, g % 2, i, :],
                                  ql[:, :, bass.ds(b, 1)], False, i == 3)
                    last.then_inc(s_ds.h, 1)

                def values(n, slot):
                    pe.wait_ge(s_de.h, n + 1)
                    mm(PP[6][:, 64:68], ones, st[:, 16:20])
                    for i in range(32):
                        last = mm(PP[6][0:NH, P:2 * P], Pb[:, 4 * i:4 * i + 4], kvg[slot][:, i, :], i == 0, i == 31)
                    last.then_inc(s_dv.h, 1)

                def turn_values(n):
                    pe.wait_ge(s_dvc.h, n + 1)
                    mm(PP[6][:, 0:NH], dav, ident[0:NH, 0:NH]).then_inc(s_dvt.h, 1)

                def turn(i, k, g0, g1):
                    n, b = l * NS + i * 2 + k, i * 2 + k
                    if g0 == 0:
                        pe.wait_ge(s_dg[k].h, l * (16 * NS) + (i * 32 + 32))
                        keys(n, k, 0)
                    for g in range(g0, g1):
                        if g < 7:
                            keys(n, k, g + 1)
                        score(n, b, k, g)

                def step(i, k):
                    nxt = (i, 1) if k == 0 else (i + 1, 0)
                    turn(*nxt, 0, 4)
                    values(l * NS + i * 2 + k, k)
                    turn(*nxt, 4, 5)
                    turn_values(l * NS + i * 2 + k)
                    turn(*nxt, 5, 8)

                def spread_queries(p):
                    pe.wait_ge(s_qe.h, s_qe.at(l, p + 1))
                    for q in range(2):
                        last = mm(PP[6 + q][:, :], ones, xn[:, q * 512:(q + 1) * 512])
                    last.then_inc(s_qb.h, 1)
                turn(0, 0, 0, 2)
                spread_queries(0)
                turn(0, 0, 2, 5)
                spread_queries(1)
                turn(0, 0, 5, 8)
                with pe.Fori(0, NS // 2 - 1) as i:
                    step(i, 0)
                    step(i, 1)
                step(NS // 2 - 1, 0)
                values(l * NS + NS - 1, 1)
                turn_values(l * NS + NS - 1)

            def sample_memory(l):
                pe.wait_ge(s_dme.h, s_dme.at(l, 1))
                mm(PP[7][:, 0:64], ones, Pb[:, 0:64])
                for b in range(NS):
                    for p in range(2):
                        for t in range(2):
                            c, w = (b * 2 + p) * 2, ((b // 4 * 2 + t) * 4 + b % 4) * 4 + 2 * p
                            last = mm(PP[6][:, c:c + 2], dmv[b // 4][:, b % 4, t, p * P:(p + 1) * P], Pb[:, w:w + 2], t == 0, t == 1)
                last.then_inc(s_dmo.h, 1)

            pe.wait_ge(s_const.h, 32)
            with pe.Fori(0, L) as l:
                pe.wait_ge(s_const.h, 32)
                pe.wait_ge(s_lvl.h, s_lvl.at(l, s_lvl.n))
                mm(PP[7][:, 0:NVEC], vecrow[:, :], ident[0:NVEC, 0:NVEC]).then_inc(s_vt.h, 1)
                transpose_rows(s_mem["xn"], s_mem["tp"], l, 2, P, 1)
                pe.wait_ge(s_mw.h, s_mw.at(l, s_mw.n))
                pe.wait_ge(s_mem["hT"].h, s_mem["hT"].at(l, 1))
                wm = kv[:, 0:4096].rearrange("p (k n) -> p k n", k=KD)
                for j in range(2):
                    for k in range(KD):
                        last = mm(PP[4 + j][:, :], hT[:, k, j * P:(j + 1) * P], wm[:, k, :], k == 0, k == KD - 1)
                    last.then_inc(s_mem["kv"].h, 1)
                    if j == 0:
                        turn_x(l * (IT + 1), 0, 2)
                pe.wait_ge(s_mem["kvr"].h, s_mem["kvr"].at(l, 1))
                for p in range(2):
                    for j in range(2):
                        last = tr(PP[1][:, p * T + j * P:p * T + (j + 1) * P], T1[:, j, p * P:(p + 1) * P], P)
                last.then_inc(s_mem["kt"].h, 1)
                pe.wait_ge(s_const.h, 32)
                pe.wait_ge(s_lw.h, s_lw.at(l, s_lw.n))
                mm(PP[0][:, 0:NS], shn[:, 0:P], ident[0:NS, 0:NS])
                for i in range(1, 7):
                    tr(PP[0][:, i * NS:(i + 1) * NS], shn[:, i * P:(i + 1) * P], NS)
                for p in range(2):
                    tr(PP[0][:, 64 + 16 * p:80 + 16 * p], cvn[:, p * P:(p + 1) * P], 16)
                for h in range(NH):
                    last = tr(PP[2][0:64, h * P:(h + 1) * P], wukn[:, h * 64:(h + 1) * 64], P)
                last.then_inc(s_wt.h, 1)
                pe.wait_ge(s_const.h, 32)
                pe.wait_ge(s_hT.h, s_hT.at(l * (IT + 1), 2))
                turn_x(l * (IT + 1) + 1, 0)
                pe.wait_ge(s_wr.h, s_wr.at(l, 1))
                turn_x(l * (IT + 1) + 1, 1)

                def block(B, m, e):
                    pe.wait_ge(s_hT.h, s_hT.at(B.px, 2))
                    project(B)
                    rwkv_chunks(B)
                    attention(B, l, m, e)
                    attention_out(B)
                    memory(B)
                    project_out(B)
                prompt_loop(lambda: pe, block, l)
                B = Block(l, None)
                prompt_states(l)
                pe.wait_ge(s_const.h, 32)
                pe.wait_ge(s_fpr.h, s_fpr.at(l, 1))
                project(B)
                sample_rwkv(l)
                group_norm(B, 0)
                group_norm(B, 1)
                sample_attention(l)
                attention_out(B)
                sample_memory(l)
                project_out(B)

        @blk.vector
        def _(v):
            def drain():
                v.drain()

            def scalars(ap, n):
                return ap.unsqueeze(2).broadcast_to([ap.shape[0], ap.shape[1], n])

            def inverse_roots(want, done, last, it, upto, k=1):
                last.then_inc(want.h, k)
                v.wait_ge(done.h, done.at(it, upto))

            def normalise_rows(sums, ready, turned, want, done, it, tiles, w, k):
                for j in range(tiles):
                    v.wait_ge(sums.h, sums.at(it, (j + 1) if tiles == 2 else 2))
                    if j:
                        v.wait_ge(turned.h, turned.at(it, j))
                    last = v.tensor_scalar(st[0:w, 4 + j:5 + j], st[0:w, j:j + 1], 1.0 / D, EPS, MULT, ADD)
                    inverse_roots(want, done, last, it, (j + 1) * k, k)
                    v.tensor_scalar(xn[0:w, :], memx[0:w, j, :], st[0:w, 4 + j:5 + j], None, MULT).then_inc(ready.h, k)

            def halves(bank, n, parts=P):
                return PP[bank][0:parts, :].rearrange("p (a t) -> p a t", a=2)[:, :, 0:n]

            def take_h(turned, ready, it, gain, n):
                v.wait_ge(turned.h, turned.at(it, 2))
                for i in range(4):
                    last = v.tensor_tensor(hT[:, 2 * i:2 * i + 2, 0:n], halves(i, n), scalars(V(gain, 2 * i, 2), n), MULT)
                last.then_inc(ready.h, 1)

            def shift(B, a0, a1, seen):
                n = B.n
                v.wait_ge(s_pa.h, s_pa.at(B.it, seen))
                cur = pr[:, a0:a1, 1:1 + n]
                d = T3[:, 0:a1 - a0, 0:n]
                if B.prompt:
                    v.tensor_copy(halo[:, a0:a1], pr[:, a0:a1, n:n + 1].rearrange("p a o -> p (a o)"))
                    v.tensor_tensor(d, pr[:, a0:a1, 0:n], cur, SUB)
                else:
                    v.tensor_copy(raw[:, a0:a1, :], cur)
                    v.tensor_tensor(d, shs[:, a0:a1, 0:n], cur, SUB)
                drain()
                v.tensor_tensor(d, d, scalars(V("mu", a0, a1 - a0), n), MULT)
                drain()
                last = v.tensor_tensor(cur, cur, d, ADD)
                if B.prompt:
                    last = v.tensor_copy(pr[:, a0:a1, 0:1], halo[:, a0:a1].unsqueeze(2))
                last.then_inc(s_shift.h, 1)
                drain()

            def rwkv_prepare(B):
                it, n = B.it, B.n
                kx, rx, vx = (pr[:, i:i + 2, 1:1 + n] for i in (2, 0, 4))
                t1, t2, t3, s_, a_ = (t[:, :, 0:n] for t in (T1, T2, T3, sw, aa))
                shift(B, 6, 7, 1)
                shift(B, 2, 4, 3)
                v.tensor_tensor(t1, kx, scalars(V("kk", 0, 2), n), MULT)
                drain()
                v.tensor_tensor(t2, t1, t1, MULT).then_inc(s_sq.h, 1)
                shift(B, 0, 2, 5)
                shift(B, 4, 6, 7)
                v.wait_ge(s_lor.h, s_lor.at(it, 1))
                v.tensor_scalar(s_, s_, 0.5, 0.5, MULT, ADD)
                last = v.tensor_scalar(a_, a_, 0.5, 0.5, MULT, ADD)
                drain()
                if B.prompt:
                    for p in range(2):
                        v.tensor_tensor_scan(Ls[:, p, :], K("scan"), sw[:, p, :], 0.0, MULT, ADD)
                    drain()
                    last = v.tensor_tensor(T3[:, :, :], Ls[:, :, :], sw[:, :, :], SUB)
                    last.then_inc(s_sg.h, 1)
                else:
                    v.tensor_copy(Ls[:, :, 0:n], s_).then_inc(s_sg.h, 1)
                v.wait_ge(s_pa.h, s_pa.at(it, 11))
                v.tensor_tensor(sqn[:, 0, 0:n], ckr[:, 0:n], ckr[:, 0:n], MULT)
                v.tensor_tensor(sqn[:, 1:3, 0:n], qd[:, :, 0:n], qd[:, :, 0:n], MULT).then_inc(s_nq.h, 1)
                v.wait_ge(s_sqd.h, s_sqd.at(it, 1))
                v.tensor_scalar(t2, halves(6, n), 1e-12, None, ADD)
                v.wait_ge(s_nqd.h, s_nqd.at(B.it, 1))
                v.tensor_scalar(sqn[:, 0, 0:n], PP[7][:, 0:n], 1.0 / R, EPS, MULT, ADD)
                v.tensor_scalar(sqn[:, 1, 0:n], PP[7][:, T:T + n], 1.0 / 256, EPS, MULT, ADD).then_inc(s_rw.h, 1)
                v.wait_ge(s_rd.h, s_rd.at(it, 1))
                v.reciprocal(t2, t2)
                v.reciprocal(sqn[:, 0:2, 0:n], sqn[:, 0:2, 0:n])
                drain()
                v.tensor_tensor(t1, t1, t2, MULT)
                drain()
                for p in range(2):
                    v.tensor_scalar(T2[:, p, 0:n], aa[:, p, 0:n], -1.0, V("ka", p), ADD, MULT)
                drain()
                v.scalar_tensor_tensor(kx, t2, 1.0, kx, ADD, MULT)
                drain()
                v.tensor_tensor(t2, rx, kx, MULT)
                drain()
                v.tensor_tensor(t2, t2, scalars(V("rk", 0, 2), n), MULT).then_inc(s_bo.h, 1)
                b_ = Bp[:, :, 0:n]
                v.tensor_tensor(b_, t1, a_, MULT)
                v.wait_ge(s_const.h, 32)
                v.wait_ge(s_dec.h, s_dec.at(it, 1))
                if B.prompt:
                    drain()
                    v.tensor_tensor(b_, b_, eN[:, :, :], MULT)
                    v.tensor_tensor(Kt[:, :, :], kx, eN[:, :, :], MULT)
                    tt = lambda t: t.rearrange("p a (j t) -> p a j t", j=2)
                    v.tensor_tensor(KR[:, :, :, 0, :], tt(T1[:, :, :]), tt(eK[:, :, :]), MULT)
                    last = v.tensor_tensor(KR[:, :, :, 1, :], tt(rx), tt(eP[:, :, :]), MULT)
                else:
                    drain()
                    last = v.tensor_copy(Ls[:, :, 0:n], t1)
                last.then_inc(s_rt.h, 1)
                drain()

            def latents(B):
                n = B.n
                v.scalar_tensor_tensor(ckr[:, 0:n], ckr[:, 0:n], V("kn"), sqn[:, 0, 0:n], MULT, MULT)
                for t in range(2):
                    last = v.scalar_tensor_tensor(qd[:, t, 0:n], qd[:, t, 0:n], V("qn", t), sqn[:, 1, 0:n], MULT, MULT)
                last.then_inc(s_qn.h, 1)
                drain()
                v.wait_ge(s_bod.h, s_bod.at(B.it, 1))
                v.tensor_tensor(bon[:, :, 0:n], halves(6, n), pr[:, 4:6, 1:1 + n], MULT).then_inc(s_bor.h, 1)

            def projected(B, t):
                if not B.prompt:
                    return sproj[:, t, :]
                v.wait_ge(s_pj.h, s_pj.at(B.ip, t + 1))
                v.tensor_copy(sproj[:, t, :], PP[t % 4][:, T:T + NS])
                return PP[t % 4][:, 0:T]

            def convolution(B):
                n, it = B.n, B.it
                t0 = DVE_TILES[0]
                v.wait_ge(s_pa.h, s_pa.at(it, 15))
                for p in range(2):
                    v.tensor_tensor(u[:, p, 2:2 + n], projected(B, t0 + p), cxs[:, p, 0:n], MULT).then_inc(s_pv.h, 1)
                drain()
                for p in range(2):
                    taps = [u[:, p, 0:n], u[:, p, 1:1 + n]] if B.prompt else [cvs[:, p, :, 0], cvs[:, p, :, 1]]
                    v.tensor_scalar(T3[:, p, 0:n], taps[0], V("conv", p), None, MULT)
                    drain()
                    v.scalar_tensor_tensor(T3[:, p, 0:n], taps[1], V("conv", 2 + p), T3[:, p, 0:n], MULT, ADD)
                    drain()
                    v.scalar_tensor_tensor(T3[:, p, 0:n], u[:, p, 2:2 + n], V("conv", 4 + p), T3[:, p, 0:n], MULT, ADD)
                if B.prompt:
                    drain()
                    v.tensor_copy(u[:, :, 0:2], u[:, :, n:n + 2])
                drain()
                for p in range(2):
                    t = DVE_TILES[2 + p]
                    v.tensor_tensor(mix[:, p, 0:n], projected(B, t), T3[:, p, 0:n], MULT).then_inc(s_pv.h, 1)

            def gates(B, which, dst):
                n = B.n
                for p in range(2):
                    i = 2 * which + p
                    t = DVE_TILES[4 + i]
                    g = ge[:, i % 2, 0:n]
                    x = PP[t % 4][:, 0:n] if B.prompt else sproj[:, t, :]
                    v.wait_ge(s_ge.h, s_ge.at(B.it, i + 1))
                    if which == 0:
                        v.scalar_tensor_tensor(g, g, 1.0, x, ADD, MULT)
                        drain()
                        v.scalar_tensor_tensor(mix[:, p, 0:n], mix[:, p, 0:n], 0.5, g, MULT, MULT).then_inc(s_pv.h, 1)
                    else:
                        v.scalar_tensor_tensor(mix[:, dst + p, 0:n], g, 1.0, x, ADD, MULT).then_inc(s_pv.h, 1)

            def rotate_queries(B):
                n = B.n
                cos, sin = (cs[:, i:i + 1, 0:n].broadcast_to([RD, NH, n]) for i in range(2))
                v.wait_ge(s_cs.h, s_cs.at(B.it, 16))
                v.wait_ge(s_ql.h, s_ql.at(B.it, 2))
                v.wait_ge(s_qpr.h, s_qpr.at(B.it, 2))
                tmp = OT[0:RD, :, 0:n]
                for i in range(2):
                    v.tensor_tensor(OT[0:RD, 2 * i:2 * i + 2, 0:n], halves(6 + i, n, RD),
                                    cs[:, 1:2, 0:n].broadcast_to([RD, 2, n]), MULT)
                v.tensor_tensor(qr[:, :, 0:n], qr[:, :, 0:n], cos, MULT)
                drain()
                out = Q96[NOPE:NOPE + RD, :, :] if B.prompt else qr2[:, :, :]
                v.tensor_tensor(out, qr[:, :, 0:n], tmp, ADD).then_inc(s_qlr.h, 1)

            def store_latents(B):
                n = B.n
                v.wait_ge(s_kr.h, s_kr.at(B.it, 1))
                v.tensor_tensor(T3[0:RD, 0, 0:n], PP[4][0:RD, 0:n], cs[:, 1, 0:n], MULT)
                v.tensor_tensor(krr[:, 0:n], krr[:, 0:n], cs[:, 0, 0:n], MULT)
                drain()
                v.tensor_tensor(krr[:, 0:n], krr[:, 0:n], T3[0:RD, 0, 0:n], ADD).then_inc(s_krr.h, 1)
                drain()
                v.wait_ge(s_kr.h, s_kr.at(B.it, 2))
                if B.prompt:
                    v.tensor_scalar(ckvN[:, bass.ds(B.block * 2, 2), :], PP[5][:, 0:T].rearrange("p (a t) -> p a t", a=2), 1.0, None, MULT)
                    v.tensor_scalar(keysT[NOPE:NOPE + RD, :, bass.ds(B.tok, n)], krr[:, :].unsqueeze(1).broadcast_to([RD, NH, n]), 1.0, None, MULT)
                v.tensor_copy(st[:, 47:48], st[:, 46:47]).then_inc(s_kvd.h, 1)
                drain()

            def rwkv_chunks(B):
                ip = B.ip

                def level_block(lev, j):
                    if lev:
                        v.wait_ge(s_q.h, s_q.at(ip, (lev - 1) * 4 + 2 * j + 2))
                    v.tensor_tensor(Om[j], An[j], mlev[:, lev + 1:lev + 2, :].broadcast_to([P, NH, P]), MULT).then_inc(s_om.h, 1)
                for j in range(2):
                    for p in range(2):
                        v.wait_ge(s_gr.h, s_gr.at(ip, 2 * j + p + 1))
                        for h in range(2):
                            q = 2 * p + h
                            g4 = PP[q][:, :].rearrange("p (a t) -> p a t", a=4)
                            v.tensor_tensor(XI[j][:, 0, q, :], g4[:, 0, :], K("m1t"), MULT)
                            v.tensor_tensor(gram2[j][:, q, :, :], g4[:, 1:3, :], mgram[:, 1:3, :], MULT)
                            last = v.tensor_tensor(gramF[j][:, q, :], g4[:, 3, :], mgram[:, 3, :], MULT)
                        last.then_inc(s_gm.h, 1)
                    v.wait_ge(s_ga.h, s_ga.at(ip, j + 1))
                    for h in range(2):
                        last = v.tensor_copy(An[j][:, h:h + 3:2, :], PP[6 + h][:, 0:2 * P].rearrange("p (a t) -> p a t", a=2))
                    last.then_inc(s_anr.h, 1)
                    drain()
                    v.tensor_tensor(XI[j][:, 1, :, :], An[j], mlev[:, 0:1, :].broadcast_to([P, NH, P]), MULT)
                    drain()
                    for k in range(2):
                        last = v.tensor_tensor(XI[j][:, k, :, :], ident.unsqueeze(1).broadcast_to([P, NH, P]), XI[j][:, k, :, :], SUB)
                    last.then_inc(s_grr.h, 1)
                    level_block(0, j)
                for lev in range(5):
                    if lev < 4:
                        for j in range(2):
                            level_block(lev + 1, j)
                    for j in range(2):
                        for p in range(2):
                            v.wait_ge(s_xx.h, s_xx.at(ip, lev * 4 + 2 * j + p + 1))
                            k = 2 if lev < 4 else 1
                            x = XI[j][:, 0:k, 2 * p:2 * p + 2, :]
                            d = PP[4 + 2 * j + p][:, :].rearrange("p (h k t) -> p k h t", h=2, k=2)[:, 0:k, :, :]
                            v.tensor_tensor(x, x, d, SUB).then_inc(s_xxr.h, 1)
                    drain()
                for j in range(2):
                    J = slice(j * P, (j + 1) * P)
                    for c in range(2):
                        Q = slice(64 * c, 64 * c + 64)
                        n0 = (j * 2 + c) * 2
                        for p in range(2):
                            v.wait_ge(s_x0.h, s_x0.at(ip, n0 + p + 1))
                            v.tensor_copy(X0[Q, p, :], PP[p][Q, 0:P]).then_inc(s_x0r.h, 1)
                        for p in range(2):
                            v.wait_ge(s_sa.h, s_sa.at(ip, n0 + p + 1))
                            v.tensor_scalar(SA[Q, p, :], PP[p][Q, P:2 * P], -1.0, None, MULT).then_inc(s_sar.h, 1)
                        for p in range(2):
                            dec = eP[:, p, j * P + c * 64 + 63:j * P + c * 64 + 64]
                            v.wait_ge(s_su.h, s_su.at(ip, n0 + p + 1))
                            v.scalar_tensor_tensor(BT[:, p, :], PP[2 + p][:, 0:P], dec, bones, MULT, MULT)
                            drain()
                            v.scalar_tensor_tensor(BD[:, p, :], BD[:, p, :], dec, BT[:, p, :], MULT, ADD).then_inc(s_sur.h, 1)
                            drain()
                    for p in range(2):
                        v.wait_ge(s_y.h, s_y.at(ip, 2 * j + p + 1))
                        v.tensor_copy(yy[:, p, J], PP[4 + p][:, 0:P]).then_inc(s_yr.h, 1)
                drain()

            def centre(B):
                n = B.n
                y = yy[:, :, 0:n]
                v.wait_ge(s_lm.h, s_lm.at(B.it, 1))
                v.scalar_tensor_tensor(y, halves(2, n), -1.0 / HD, y, MULT, ADD)
                drain()
                v.tensor_tensor(T2[:, :, 0:n], y, y, MULT).then_inc(s_lc.h, 1)

            def variance(B):
                n = B.n
                v.wait_ge(s_lv.h, s_lv.at(B.it, 1))
                v.tensor_scalar(T1[:, :, 0:n], halves(3, n), 1.0 / HD, LN_EPS, MULT, ADD).then_inc(s_vw.h, 1)

            def rwkv_finish(B):
                n = B.n
                y, t = yy[:, :, 0:n], T1[:, :, 0:n]
                v.wait_ge(s_vd.h, s_vd.at(B.it, 1))
                v.reciprocal(t, t)
                drain()
                v.tensor_tensor(y, y, t, MULT)
                drain()
                for p in range(2):
                    v.tensor_scalar(yy[:, p, 0:n], yy[:, p, 0:n], V("lg", p), V("lb", p), MULT, ADD)
                drain()
                v.tensor_tensor(y, y, bon[:, :, 0:n], ADD)
                drain()
                v.scalar_tensor_tensor(mix[:, 2:4, 0:n], mix[:, 2:4, 0:n], 0.5, y, MULT, MULT).then_inc(s_lvr.h, 1)

            def attention_begin(B):
                v.memset(ml[:, 0, :], -NEG)
                v.memset(ml[:, 1, :], 0.0)
                drain()

            def attention(B, l, m, e):
                n0 = steps_before(l, m, e)

                def masked_max(kc, s):
                    u, j = s % 8, s % 8 // NH
                    o = nc.s_assert_within(FMZ - 128 * j + (kc + s // 8 - m) * KC - e * T, 0, FMZ,
                                           skip_runtime_bounds_check_because="the step is at most m")
                    v.wait_ge(s_at.h, n0 + (kc * 8 + max(s - 1, 0) + s_at.base))
                    v.wait_ge(s_as.h, n0 + (kc * 8 + (s + 1)))
                    v.tensor_tensor(Sm[:, s % 2, :], PP[s % 2][:, :], fmask[:, bass.ds(o, KC)], ADD).then_inc(s_am.h, 1)
                    drain()
                    v.tensor_reduce(ml[:, 2, u:u + 1], Sm[:, s % 2, :], AX, MAX)
                    drain()
                    v.scalar_tensor_tensor(ml[:, 3, u:u + 1], ml[:, 2, u:u + 1], -MLA_SCALE, ml[:, 0, u:u + 1], MULT, MIN).then_inc(s_an.h, 1)

                def sums(kc, s):
                    u = s % 8
                    v.wait_ge(s_ae.h, n0 + (kc * 8 + (s + 1)))
                    v.scalar_tensor_tensor(ml[:, 1, u:u + 1], ml[:, 1, u:u + 1], ml[:, 4, u:u + 1], ml[:, 5, u:u + 1], MULT, ADD)
                    v.tensor_copy(ml[:, 0, u:u + 1], ml[:, 3, u:u + 1])

                def accumulate(kc, s):
                    v.wait_ge(s_av.h, n0 + (kc * 8 + (s + 1) + s_av.base))
                    v.scalar_tensor_tensor(OO[:, s, :], OO[:, s, :], ml[:, 4, s:s + 1], PP[4 + s % 2][:, 0:R], MULT, ADD)\
                        .then_inc(s_ao.h, 1)

                def step(kc, ahead):
                    for s in range(8):
                        if s + 3 < 8 or ahead:
                            masked_max(kc, s + 3)
                        if s + 2 < 8 or ahead:
                            sums(kc, s + 2)
                        accumulate(kc, s)
                masked_max(0, 0)
                masked_max(0, 1)
                v.memset(OO[:, :, :], 0.0)
                sums(0, 0)
                masked_max(0, 2)
                sums(0, 1)
                drain()
                with v.If(m > 0):
                    with v.Fori(0, m) as kc:
                        step(kc, True)
                step(m, False)
                drain()
                v.reciprocal(ml[:, 2, :], ml[:, 1, :])
                drain()
                v.tensor_tensor(OO[:, :, :], OO[:, :, :], scalars(ml[:, 2, :], P), MULT).then_inc(s_on.h, 1)

            def gate_attention(B):
                n = B.n
                v.wait_ge(s_uv.h, s_uv.at(B.it, 1))
                for p in range(2):
                    last = v.scalar_tensor_tensor(mix[:, 4 + p, 0:n], mix[:, 4 + p, 0:n], 0.5, PP[4 + p][:, 0:n], MULT, MULT)
                if B.prompt:
                    last.then_inc(s_uvr.h, 1)

            def memory(B):
                for j in range(2):
                    top, neg, _, _ = mst[j]
                    v.wait_ge(s_ms.h, s_ms.at(B.ip, j + 1))
                    for h in range(2):
                        v.tensor_reduce(top[:, 2 * h:2 * h + 2], halves(4 * j + h, T), AX, MAX)
                    drain()
                    v.tensor_scalar(neg, top, -MEM_SCALE, None, MULT).then_inc(s_mx.h, 1)
                for j in range(2):
                    _, _, total, inv = mst[j]
                    v.wait_ge(s_me.h, s_me.at(B.ip, j + 1))
                    v.reciprocal(inv, total)
                    drain()
                    v.tensor_tensor(Pm[j], Pm[j], scalars(inv, T), MULT).then_inc(s_mn.h, 1)
                v.wait_ge(s_mo.h, s_mo.at(B.ip, 1))
                v.scalar_tensor_tensor(mix[:, 6:8, :], mix[:, 6:8, :], 0.5, halves(6, T), MULT, MULT).then_inc(s_mix.h, 1)

            def residual(B):
                w, it = min(B.n, P), B.it
                v.wait_ge(s_xl.h, s_xl.at(it, 16))
                v.wait_ge(s_os.h, s_os.at(it, 1))
                for j in range(B.tiles):
                    r = st[0:w, 32 + j:33 + j]
                    v.tensor_tensor(r, st[0:w, 8 + 2 * j:9 + 2 * j], st[0:w, 9 + 2 * j:10 + 2 * j], ADD)
                    drain()
                    last = v.tensor_scalar(r, r, 1.0 / D, EPS, MULT, ADD)
                    k = 2 // B.tiles
                    inverse_roots(s_pw, s_pr, last, it, (j + 1) * k, k)
                    for i in range(2):
                        q = slice(i * 512, (i + 1) * 512)
                        v.scalar_tensor_tensor(xn[0:w, q], PP[4 + 2 * j + i][0:w, :], r, postg[0:w, q], MULT, MULT)
                    drain()
                    last = v.tensor_tensor(xin[0:w, j, :], xin[0:w, j, :], xn[0:w, :], ADD)
                    if j == B.tiles - 1:
                        last.then_inc(s_of.h, 1)
                    drain()

            def spread(vec3, sig_out, l, i):
                if i >= 1:
                    v.wait_ge(s_sb.h, s_sb.at(l, i))
                e4 = xn[:, :].rearrange("p (b a j) -> p b a j", b=NS, a=2)
                for a_ in range(2):
                    last = v.tensor_tensor(e4[:, :, a_, :], vec3[:, a_, :].unsqueeze(2).broadcast_to([P, NS, 64]),
                                           K("id64").unsqueeze(1).broadcast_to([P, NS, 64]), MULT)
                last.then_inc(sig_out.h, 1)

            def sample_rwkv(l):
                n = NS
                vecs = [eP[:, :, 0:n], Ls[:, :, 0:n], Bp[:, :, 0:n], pr[:, 2:4, 1:1 + n], pr[:, 0:2, 1:1 + n]]
                v.wait_ge(s_sl.h, s_sl.at(l, s_sl.n))
                spread(vecs[0], s_se, l, 0)
                sab = st[:, 0:16]
                for i in range(5):
                    if i < 4:
                        spread(vecs[i + 1], s_se, l, i + 1)
                    v.wait_ge(s_sb.h, s_sb.at(l, i + 1))
                    for q in range(2):
                        rows = PP[2 * (i % 2) + q][:, :].rearrange("p (a j) -> p a j", j=64)
                        s_ = S0[:, 8 * q:8 * q + 8, :]
                        w_ = SW[:, 8 * q:8 * q + 8, :]
                        if i == 0:
                            v.tensor_tensor(SD[:, 8 * q:8 * q + 8, :], s_, rows, MULT)
                        elif i == 1:
                            v.tensor_tensor(w_, s_, rows, MULT)
                            drain()
                            v.tensor_reduce(sab[:, 8 * q:8 * q + 8], w_, AX, ADD)
                            drain()
                        elif i == 2:
                            v.tensor_tensor(w_, rows, scalars(sab[:, 8 * q:8 * q + 8], 64), MULT)
                            drain()
                            v.tensor_tensor(SD[:, 8 * q:8 * q + 8, :], SD[:, 8 * q:8 * q + 8, :], w_, SUB)
                        elif i == 3:
                            for b in range(4):
                                vb = pr[:, 4:6, 1 + 4 * q + b:2 + 4 * q + b].broadcast_to([P, 2, 64])
                                v.tensor_tensor(w_[:, 2 * b:2 * b + 2, :], rows[:, 2 * b:2 * b + 2, :], vb, MULT)
                            drain()
                            v.tensor_tensor(SD[:, 8 * q:8 * q + 8, :], SD[:, 8 * q:8 * q + 8, :], w_, ADD)
                        else:
                            v.tensor_tensor(w_, SD[:, 8 * q:8 * q + 8, :], rows, MULT)
                            drain()
                            v.tensor_reduce(sab[:, 8 * q:8 * q + 8], w_, AX, ADD)
                    if i == 3:
                        drain()
                        v.tensor_copy(st[:, 47:48], st[:, 46:47]).then_inc(s_sst2.h, 1)
                drain()
                v.tensor_copy(yy[:, :, 0:n], sab.rearrange("p (b a) -> p a b", a=2)).then_inc(s_sy.h, 1)
                drain()

            def memory_scores(l, q):
                v.wait_ge(s_dml[q].h, s_dml[q].at(l, 128))
                qb = qB[:, 4 * q:4 * q + 4, :, :].rearrange("p b a c -> p b (a c)")
                for t in range(2):
                    v.tensor_tensor(dmp[t].rearrange("p (b c) -> p b c", b=4), dmk[q][:, :, t, :], qb, MULT)
                drain()
                for t in range(2):
                    c = (2 * q + t) * 16
                    v.tensor_reduce(msc[:, c:c + 16], dmp[t].rearrange("p (x d) -> p x d", d=HD), AX, ADD)
                drain()

            def sample_attention(l):
                n = NS
                f = lambda t: t.rearrange("p (h b) -> p h b", h=NH)
                v.tensor_tensor(f(T1f[:, 0:32]), ql[:, :, 0:n], ckr[:, 0:n].unsqueeze(1).broadcast_to([P, NH, n]), MULT)
                v.tensor_tensor(f(T3f[0:RD, 0:32]), qr2[:, :, 0:n], krr[:, 0:n].unsqueeze(1).broadcast_to([RD, NH, n]), MULT)\
                    .then_inc(s_dp.h, 1)
                v.wait_ge(s_dq.h, s_dq.at(l, 1))
                src = PP[4][:, 0:32].rearrange("p (h b) -> p b h", h=NH)
                for t in range(4):
                    v.tensor_scalar(QR4[:, :, 4 * t:4 * t + 4], src, K("tmask")[:, t:t + 1], None, MULT)
                v.tensor_copy(sns[:, :, :], PP[4][:, 64:96].rearrange("p (h b) -> p b h", h=NH)).then_inc(s_dqr.h, 1)
                drain()
                for p in range(2):
                    if p:
                        v.wait_ge(s_qb.h, s_qb.at(l, 1))
                    v.tensor_tensor(xn[:, :].rearrange("p (b c) -> p b c", b=NS), mq[:, p, 0:NS].unsqueeze(2).broadcast_to([P, NS, P]),
                                    ident.unsqueeze(1).broadcast_to([P, NS, P]), MULT).then_inc(s_qe.h, 1)
                    v.wait_ge(s_qb.h, s_qb.at(l, p + 1))
                    for q in range(2):
                        v.tensor_copy(qB[:, 4 * q:4 * q + 4, p, :], PP[6 + q][:, :].rearrange("p (b c) -> p b c", b=4))
                drain()
                memory_scores(l, 0)
                v.tensor_copy(st[:, 47:48], st[:, 46:47]).then_inc(s_dmk.h, 1)

                def softmax_of(i, slot):
                    b, k = i * 2 + slot, l * NS + i * 2 + slot
                    o = PP[5 - slot][:, 0:P]
                    v.wait_ge(s_ds.h, k * 8 + (8 + s_ds.base))
                    v.tensor_reduce(st[:, 0:4], o.rearrange("p (c h) -> p h c", h=NH), AX, MAX).then_inc(s_dm1.h, 1)
                    v.wait_ge(s_dm2.h, k + 1)
                    sn = sns[:, bass.ds(b, 1), :].rearrange("p o h -> p (o h)")
                    v.tensor_copy(st[:, 47:48], st[:, 46:47])
                    v.tensor_tensor(st[:, 8:12], st[:, 4:8], sn, MAX)
                    drain()
                    v.tensor_tensor(T1f[:, 0:P].rearrange("p (c h) -> p c h", h=NH), o.rearrange("p (c h) -> p c h", h=NH),
                                    st[:, 8:12].unsqueeze(1).broadcast_to([P, 32, NH]), SUB)
                    v.tensor_tensor(T1f[:, P:P + 4], sn, st[:, 8:12], SUB).then_inc(s_dx.h, 1)
                    v.wait_ge(s_dxe.h, k + 1)
                    v.tensor_reduce(st[:, 16:20], Pb[:, 0:P].rearrange("p (c h) -> p h c", h=NH), AX, ADD).then_inc(s_de.h, 1)
                    v.wait_ge(s_dv.h, k + (1 + s_dv.base))
                    v.tensor_tensor(st[:, 20:24], PP[6][:, 64:68], Pb[:, P:P + 4], ADD)
                    v.tensor_copy(dav, PP[6][0:NH, P:2 * P]).then_inc(s_dvc.h, 1)
                    drain()
                    v.reciprocal(st[:, 20:24], st[:, 20:24])
                    cn = ckr[:, bass.ds(b, 1)].broadcast_to([P, NH])
                    v.tensor_tensor(st[:, 24:28], Pb[:, P:P + 4], cn, MULT)
                    drain()
                    v.wait_ge(s_dvt.h, k + 1)
                    v.tensor_tensor(st[:, 24:28], st[:, 24:28], PP[6][:, 0:4], ADD)
                    drain()
                    v.tensor_tensor(OT[:, :, bass.ds(b, 1)], st[:, 24:28].unsqueeze(2), st[:, 20:24].unsqueeze(2), MULT)
                    drain()
                with v.Fori(0, NS // 2) as i:
                    softmax_of(i, 0)
                    softmax_of(i, 1)
                drain()
                v.tensor_copy(st[:, 47:48], st[:, 46:47]).then_inc(s_otr.h, 1)
                memory_scores(l, 1)

            def sample_memory(l):
                s4 = msc.rearrange("p (q t x) -> p q t x", q=2, t=2)
                x3 = lambda t: t.rearrange("p (q x) -> p q x", q=2)
                v.tensor_tensor(x3(mmx), s4[:, :, 0, :], s4[:, :, 1, :], MAX).then_inc(s_dmx.h, 1)
                v.wait_ge(s_dmr.h, s_dmr.at(l, 1))
                for t in range(2):
                    last = v.tensor_tensor(s4[:, :, t, :], s4[:, :, t, :], x3(mgx), SUB)
                last.then_inc(s_dms.h, 1)
                v.wait_ge(s_dmo.h, s_dmo.at(l, 1))
                d4 = PP[7][:, 0:64].rearrange("p (q t x) -> p q t x", q=2, t=2)
                v.tensor_copy(x3(mrs), d4[:, :, 0, :])
                drain()
                v.tensor_tensor(x3(mrs), x3(mrs), d4[:, :, 1, :], ADD)
                drain()
                v.reciprocal(mrs, mrs)
                drain()
                o4 = PP[6][:, 0:32].rearrange("p (b a h) -> p b a h", b=NS, a=2)
                for h in range(2):
                    H = slice(64 * h, 64 * h + 64)
                    rr = mrs[H, :].rearrange("p (b a h) -> p b a h", b=NS, a=2)[:, :, :, h]
                    t4 = mpr[H, :].rearrange("p (b a) -> p b a", b=NS)
                    v.tensor_tensor(t4, o4[H, :, :, h], rr, MULT)
                    drain()
                    mx = mix[H, 6:8, 0:NS].rearrange("p a b -> p b a")
                    v.scalar_tensor_tensor(mx, mx, 0.5, t4, MULT, MULT)
                drain()
                v.tensor_copy(st[:, 45:46], st[:, 46:47]).then_inc(s_dm.h, 1)
                v.tensor_copy(st[:, 47:48], st[:, 46:47]).then_inc(s_mix.h, 1)

            v.memset(st[:, 40:48], 0.0)
            v.memset(kv[:, 4096:10240], 0.0)
            v.memset(X0[:, :, :], 0.0)
            v.memset(SA[:, :, :], 0.0)
            drain()
            v.wait_ge(s_const.h, 32)
            with v.Fori(0, L) as l:
                v.wait_ge(s_vt.h, s_vt.at(l, 1))
                v.tensor_copy(vec[:, :], PP[7][:, 0:NVEC]).then_inc(s_vr.h, 1)
                v.memset(pr[:, :, 0:1], 0.0)
                v.memset(u[:, :, 0:2], 0.0)
                v.memset(BD[:, :, :], 0.0)
                drain()
                normalise_rows(s_mem["ss"], s_mem["xn"], s_mem["tp"], s_mem["pw"], s_mem["pr"], l, 2, P, 1)
                take_h(s_mem["tp"], s_mem["hT"], l, "mn", T)
                v.wait_ge(s_mem["kv"].h, s_mem["kv"].at(l, 2))
                for j in range(2):
                    v.tensor_copy(T1[:, j, :], PP[4 + j][:, 0:256])
                    last = v.tensor_copy(memV[:, j, :], PP[4 + j][:, 256:512])
                last.then_inc(s_mem["kvr"].h, 1)
                v.wait_ge(s_mem["kt"].h, s_mem["kt"].at(l, 1))
                v.tensor_copy(memKT[:, :, :], PP[1][:, :].rearrange("p (a m) -> p a m", a=2))
                v.wait_ge(s_wt.h, s_wt.at(l, 1))
                v.tensor_copy(wukT[:, :, :], PP[2][0:64, :].rearrange("p (h r) -> p h r", h=NH))
                v.tensor_copy(shs[:, :, :], PP[0][:, 0:56].rearrange("p (a b) -> p a b", a=7))
                v.tensor_copy(cvs[:, :, :, :], PP[0][:, 64:96].rearrange("p (a b k) -> p a b k", a=2, b=NS)).then_inc(s_wr.h, 1)
                v.wait_ge(s_mem["out"].h, s_mem["out"].at(l, 64))
                v.tensor_copy(st[:, 47:48], st[:, 46:47])
                drain()

                def begin(B):
                    rwkv_prepare(B)
                    latents(B)
                    convolution(B)
                    rotate_queries(B)
                    gates(B, 0, 0)
                    store_latents(B)
                    gates(B, 1, 2)
                    gates(B, 2, 4)
                    gates(B, 3, 6)
                    drain()

                def block(B, m, e):
                    begin(B)
                    rwkv_chunks(B)
                    attention_begin(B)
                    attention(B, l, m, e)
                    centre(B)
                    drain()
                    variance(B)
                    gate_attention(B)
                    memory(B)
                    rwkv_finish(B)
                    residual(B)
                prompt_loop(lambda: v, block, l)
                B = Block(l, None)
                v.wait_ge(s_fp.h, s_fp.at(l, 1))
                v.tensor_copy(fst[0:7, 0:P], PP[0][0:7, 0:P])
                v.tensor_copy(fst[0:2, P:3 * P], PP[0][0:2, P:3 * P])
                v.tensor_copy(fst[:, 3 * P:5 * P], PP[1][:, 0:2 * P]).then_inc(s_fpr.h, 1)
                begin(B)
                sample_rwkv(l)
                v.wait_ge(s_sr.h, s_sr.at(l, 1))
                for i in range(2):
                    w = 512 if i == 0 else 384
                    v.tensor_copy(shn[:, i * 512:i * 512 + w], PP[4 + i][0:NS, 0:w])
                v.tensor_copy(cvn[0:NS, :], PP[7][0:NS, 0:256]).then_inc(s_srr.h, 1)
                centre(B)
                drain()
                variance(B)
                rwkv_finish(B)
                drain()
                sample_attention(l)
                gate_attention(B)
                drain()
                sample_memory(l)
                residual(B)

        @blk.scalar
        def _(act):
            act.wait_ge(s_mw.h, 32)
            act.dma_start(xres[0, S:S + NS, :], a["x_sample"][:, 0, :]).then_inc(s_xcopy.h, 16)
            act.dma_start(xres[0, 0:T, :], a["x_prompt"][0, 0:T, :]).then_inc(s_xcopy.h, 16)
            for l in range(L):
                act.dma_start(xres[l, S + NS:S + T, :], a["x_prompt"][0, 0:T - NS, :]).then_inc(s_xcopy.h, 16)
            act.wait_ge(s_const.h, 32)
            with nc.allow_non_contiguous_dma(reason="rows of small states"), act.Fori(0, L) as l:
                sl, sn = bass.ds(l, 1), bass.ds(l + 1, 1)

                def squares(sums, it, tiles, w, k):
                    for j in range(tiles):
                        act.activation(junk[0:w, j * D:(j + 1) * D], memx[0:w, j, :], ACT.Square, accum_out=st[0:w, j:j + 1]).then_inc(sums.h, k)
                act.wait_ge(s_mtl.h, s_mtl.at(l, 16))
                squares(s_mem["ss"], l, 2, P, 1)

                def memory_out():
                    act.wait_ge(s_const.h, 32)
                    act.wait_ge(s_mem["kvr"].h, s_mem["kvr"].at(l, 1))
                    for j in range(2):
                        act.dma_start(a["mem_k"][sl, j * P:(j + 1) * P, :].rearrange("a m c -> (a m) c"), T1[:, j, :]).then_inc(s_mem["out"].h, 16)
                        act.dma_start(a["mem_v"][sl, j * P:(j + 1) * P, :].rearrange("a m c -> (a m) c"), memV[:, j, :]).then_inc(s_mem["out"].h, 16)

                def sum_squares(px, tiles=2, out=xn):
                    act.wait_ge(s_x.h, s_x.at(px, 16))
                    for j in range(tiles):
                        if j:
                            act.drain()
                        act.activation(out[:, 0:D], xin[:, j, :], ACT.Square, accum_out=st[:, j:j + 1]).then_inc(s_ss.h, 2 // tiles)
                    act.drain()

                def normalise(px, j, k=1):
                    if j:
                        act.wait_ge(s_xt.h, s_xt.at(px, j))
                    act.wait_ge(s_xr.h, s_xr.at(px, j + k))
                    act.mul(xn[:, :], xin[:, j, :], st[:, 4 + j:5 + j]).then_inc(s_xn.h, k)

                def take_h(px, j, cols, k=1):
                    act.wait_ge(s_xt.h, s_xt.at(px, j + k))
                    w = cols.stop - cols.start
                    for dt in range(KD):
                        last = act.mul(hT[:, dt, cols], PP[6 + dt // 4][:, (dt % 4) * P:(dt % 4) * P + w], V("pre", dt))
                    last.then_inc(s_hT.h, k)

                def tile_cols(j):
                    return slice(j * P, (j + 1) * P)

                def begin(B):
                    it, n, w = B.it, B.n, min(B.n, P)
                    output_weights(it, 0, 2)
                    dst = {"wlal": pr[:, 6:7], "k": pr[:, 2:4], "r": pr[:, 0:2], "v": pr[:, 4:6], "qd": qd, "mq": mq, "cx": cxs}

                    def take(name):
                        for t, (g, i, c, f) in enumerate(TILES):
                            if GROUPS[g][0] != name:
                                continue
                            if B.prompt:
                                act.wait_ge(s_pj.h, s_pj.at(B.ip, t + 1))
                            if name == "ckv":
                                if i == 0:
                                    act.wait_ge(s_coe.h, s_coe.at(it, 0))
                                o = ckr[:, 0:n] if i == 0 else krr[:, 0:n]
                            elif name in ("wlal", "k", "r", "v"):
                                o = dst[name][:, i, 1:1 + n]
                            else:
                                o = dst[name][:, i, 0:n]
                            if B.prompt:
                                act.activation(o, PP[t % 4][0:f, 0:n], ACT.Copy)
                                act.activation(sproj[0:f, t, :], PP[t % 4][0:f, T:T + NS], ACT.Copy).then_inc(s_pa.h, 1)
                            else:
                                act.activation(o, sproj[0:f, t, :], ACT.Copy).then_inc(s_pa.h, 1)

                    def halves(bank, m, parts=P):
                        return PP[bank][0:parts, :].rearrange("p (a t) -> p a t", a=2)[:, :, 0:m]
                    take("wlal")
                    act.wait_ge(s_shift.h, s_shift.at(it, 1))
                    act.activation(pr[0:64, 6, 1:1 + n], pr[0:64, 6, 1:1 + n], ACT.Tanh).then_inc(s_th.h, 1)
                    take("k")
                    take("r")
                    take("v")
                    take("ckv")
                    act.wait_ge(s_lo.h, s_lo.at(it, 1))
                    for p in range(2):
                        act.activation(sw[:, p, 0:n], halves(4, n)[:, p, :], ACT.Tanh, bias=nvec[:, p:p + 1], scale=0.5)
                        last = act.activation(aa[:, p, 0:n], halves(5, n)[:, p, :], ACT.Tanh, bias=nvec[:, 2 + p:3 + p], scale=0.5)
                    last.then_inc(s_lor.h, 1)
                    take("qd")
                    act.wait_ge(s_sg.h, s_sg.at(it, 1))
                    act.activation(eP[:, :, 0:n], Ls[:, :, 0:n], ACT.Exp, scale=-DECAY)
                    if B.prompt:
                        act.activation(eN[:, :, :], Ls[:, :, :], ACT.Exp, scale=DECAY)
                        last = act.activation(eK[:, :, :], T3[:, :, :], ACT.Exp, scale=-DECAY)
                    else:
                        last = act.activation(eN[:, :, 0:n], Ls[:, :, 0:n], ACT.Copy)
                    last.then_inc(s_dec.h, 1)
                    take("mq")
                    act.wait_ge(s_rw.h, s_rw.at(it, 1))
                    act.activation(T2[:, :, 0:n], T2[:, :, 0:n], ACT.Sqrt)
                    act.activation(sqn[:, 0:2, 0:n], sqn[:, 0:2, 0:n], ACT.Sqrt).then_inc(s_rd.h, 1)
                    take("cx")
                    act.wait_ge(s_qp.h, s_qp.at(it, 1))
                    for i in range(2):
                        q = PP[4 + i][NOPE:NOPE + RD, :].rearrange("p (a t) -> p a t", a=2)[:, :, 0:n]
                        last = act.activation(qr[:, 2 * i:2 * i + 2, 0:n], q, ACT.Copy)
                    last.then_inc(s_qpr.h, 1)
                    for i in range(2):
                        last = act.activation(Q96[0:NOPE, 2 * i:2 * i + 2, 0:n], halves(4 + i, n, NOPE), ACT.Copy)
                    last.then_inc(s_qpr.h, 1)

                    def gate(i):
                        t = DVE_TILES[4 + i]
                        if B.prompt:
                            act.wait_ge(s_pj.h, s_pj.at(B.ip, t + 1))
                        act.wait_ge(s_pv.h, s_pv.at(it, i + 3))
                        x = sproj[:, t, :]
                        if B.prompt:
                            x = PP[t % 4][:, 0:n]
                            act.activation(sproj[:, t, :], PP[t % 4][:, T:T + NS], ACT.Copy)
                        act.activation(ge[:, i % 2, 0:n], x, ACT.Tanh, scale=0.5).then_inc(s_ge.h, 1)
                    act.wait_ge(s_ql.h, s_ql.at(it, 1))
                    for i in range(2):
                        if B.prompt:
                            o = keysT[0:NOPE, 2 * i:2 * i + 2, bass.ds(B.tok, n)]
                            last = act.activation(o, halves(4 + i, n, NOPE), ACT.Copy)
                        else:
                            last = act.activation(ql[:, 2 * i:2 * i + 2, :], halves(4 + i, n), ACT.Copy)
                    last.then_inc(s_qla.h, 1)
                    gate(0)
                    gate(1)
                    act.wait_ge(s_co.h, s_co.at(it, 0))
                    act.wait_ge(s_kvd.h, s_kvd.at(it, 1))
                    act.activation(cko[0:w, 0:B.tiles, :], PP[5][0:w, 0:B.tiles * P].rearrange("p (a t) -> p a t", t=P), ACT.Copy)
                    gate(2)
                    gate(3)
                    act.wait_ge(s_kn.h, s_kn.at(it, 1))
                    act.activation(kro[0:w, 0:B.tiles, :], PP[6][0:w, 0:B.tiles * RD].rearrange("p (a t) -> p a t", t=RD), ACT.Copy).then_inc(s_coe.h, 1)
                    act.wait_ge(s_coe.h, s_coe.at(it, 1))
                    for out, src in ((a["ckv"], cko), (a["krope"], kro)):
                        if B.prompt:
                            o = out[sl, bass.ds(B.tok, T), :].rearrange("a (t p) c -> p (a t) c", p=P)
                            act.dma_start(o, src[:, :, :]).then_inc(s_co.h, 16)
                        else:
                            act.dma_start(out[sl, S:S + NS, :].rearrange("a p c -> p (a c)"), src[0:NS, 0, :]).then_inc(s_co.h, 16)
                    for i in range(4, 8):
                        gate(i)

                def output_weights(it, k0, k1):
                    for i in range(k0, k1):
                        act.wait_ge(s_const.h, 32)
                        act.wait_ge(s_wou.h, s_wou.at(it, max(i - 1, 0)))
                        k = OUT_ORDER[i]
                        src = a["w_out"][sl, k * P:(k + 1) * P, :].rearrange("a p n -> (a p) n")
                        act.dma_start(wout[:, i % 2, :], src).then_inc(s_wo[i % 2].h, 16)

                def decode_output_weights(it, i0, i1):
                    for i in range(i0, i1):
                        k = OUT_ORDER[i]
                        act.dma_start(woutd[i], a["w_out"][sl, k * P:(k + 1) * P, :].rearrange("a p n -> (a p) n")).then_inc(s_wo[i % 2].h, 16)

                def finish(B):
                    it, w = B.it, min(B.n, P)
                    if B.prompt:
                        output_weights(it, 2, KD)
                    act.wait_ge(s_wou.h, s_wou.at(it, KD))
                    for j in range(B.tiles):
                        for i in range(2):
                            last = act.activation(junk[0:w, (2 * j + i) * 512:(2 * j + i + 1) * 512], PP[4 + 2 * j + i][0:w, :], ACT.Square,
                                                  accum_out=st[0:w, 8 + 2 * j + i:9 + 2 * j + i])
                    last.then_inc(s_os.h, 1)
                    act.wait_ge(s_of.h, s_of.at(it, 1))
                    if B.prompt:
                        o = xres[sn, bass.ds(B.tok, T), :].rearrange("a (t p) d -> p (a t) d", p=P)
                        act.dma_start(o, xin[:, :, :]).then_inc(s_od.h, 16)
                    else:
                        act.dma_start(xres[sn, S:S + NS, :].rearrange("a p d -> p (a d)"), xin[0:NS, 0, :]).then_inc(s_od.h, 16)

                def variance_root(B):
                    act.wait_ge(s_vw.h, s_vw.at(B.it, 1))
                    act.activation(T1[:, :, 0:B.n], T1[:, :, 0:B.n], ACT.Sqrt).then_inc(s_vd.h, 1)

                def block(B, m, e):
                    ip = B.ip
                    begin(B)
                    def natural(j, bank, c0):
                        for p in range(2):
                            act.wait_ge(s_nt.h, s_nt.at(ip, 2 * j + p + 1))
                            act.activation(nat[:, p, :, :], PP[bank + p][:, c0:c0 + 3 * P].rearrange("p (a t) -> p a t", t=P), ACT.Copy).then_inc(s_ntr.h, 1)
                    natural(0, 4, 0)
                    sum_squares(B.px + 1)
                    normalise(B.px + 1, 0)
                    for lev in range(5):
                        for j in range(2):
                            for p in range(2):
                                k = lev * 4 + 2 * j + p + 1
                                act.wait_ge(s_q.h, s_q.at(ip, k))
                                if lev:
                                    act.wait_ge(s_xx.h, s_xx.at(ip, k - 4))
                                act.activation(Qs[j][:, 2 * p:2 * p + 2, :], PP[2 * j + p][:, 0:T].rearrange("p (a t) -> p a t", t=P), ACT.Copy).then_inc(s_qrd.h, 1)
                    take_h(B.px + 1, 0, tile_cols(0))
                    normalise(B.px + 1, 1)
                    natural(1, 2, P)
                    take_h(B.px + 1, 1, tile_cols(1))
                    n0 = steps_before(l, m, e)

                    def probs(kc, s):
                        u = s % 8
                        act.wait_ge(s_an.h, n0 + (kc * 8 + (s + 1)))
                        act.activation(Sm[:, s % 2, :], Sm[:, s % 2, :], ACT.Exp, bias=ml[:, 3, u:u + 1],
                                       scale=MLA_SCALE, accum_out=ml[:, 5, u:u + 1])
                        act.activation(ml[:, 4, u:u + 1], ml[:, 0, u:u + 1], ACT.Exp, bias=ml[:, 3, u:u + 1], scale=-1.0).then_inc(s_ae.h, 1)

                    def take(kc, s):
                        act.wait_ge(s_at.h, n0 + (kc * 8 + (s + 1) + s_at.base))
                        act.wait_ge(s_av.h, n0 + (kc * 8 + max(s - 1, 0) + s_av.base))
                        act.activation(PT[:, s % 2, :, :], PP[2 + s % 2][:, :].rearrange("p (a t) -> p a t", a=4), ACT.Copy).then_inc(s_ar.h, 1)

                    def step(kc, ahead):
                        for s in range(8):
                            if s + 1 < 8 or ahead:
                                probs(kc, s + 1)
                            take(kc, s)
                    probs(0, 0)
                    with act.If(m > 0):
                        with act.Fori(0, m) as kc:
                            step(kc, True)
                    step(m, False)
                    act.wait_ge(s_ot.h, s_ot.at(ip, 1))
                    for j in range(2):
                        last = act.activation(OT[:, :, j * P:(j + 1) * P], PP[6 + j][:, :].rearrange("p (h t) -> p h t", h=NH), ACT.Copy)
                    last.then_inc(s_otr.h, 1)
                    for j in range(2):
                        act.wait_ge(s_mx.h, s_mx.at(ip, j + 1))
                        for q in range(4):
                            last = act.activation(Pm[j][:, q, :], PP[4 * j + q // 2][:, (q % 2) * T:(q % 2) * T + T], ACT.Exp,
                                                  bias=mst[j][1][:, q:q + 1], scale=MEM_SCALE, accum_out=mst[j][2][:, q:q + 1])
                        last.then_inc(s_me.h, 1)
                    for j in range(2):
                        act.wait_ge(s_mt.h, s_mt.at(ip, j + 1))
                        for q in range(2):
                            last = act.activation(PTm[j][:, q, :, :], PP[2 - 2 * j + q][:, :].rearrange("p (a t) -> p a t", a=4), ACT.Copy)
                        last.then_inc(s_mtr.h, 1)
                    variance_root(B)
                    finish(B)
                act.wait_ge(s_vr.h, s_vr.at(l, 1))
                act.mul(nvec[:, 0:2], V("w0", 0, 2), 0.5)
                act.mul(nvec[:, 2:4], V("a0", 0, 2), 0.5)
                act.drain()
                px = l * (IT + 1)
                act.wait_ge(s_mem["tp"].h, s_mem["tp"].at(l, 2))
                sum_squares(px, 1, junk)
                normalise(px, 0, 2)
                act.wait_ge(s_const.h, 32)
                act.wait_ge(s_xn.h, s_xn.at(px, 2))
                act.dma_start(xin[:, :, :], xres[sl, 0:T, :].rearrange("a (t p) d -> p (a t) d", p=P)).then_inc(s_x.h, 16)
                sum_squares(px + 1, 2, junk)
                act.wait_ge(s_xt.h, s_xt.at(px, 2))
                normalise(px + 1, 0)
                act.wait_ge(s_mem["kv"].h, s_mem["kv"].at(l, 2))
                take_h(px, 0, slice(T, T + NS), 2)
                memory_out()
                take_h(px + 1, 0, tile_cols(0))
                normalise(px + 1, 1)
                take_h(px + 1, 1, tile_cols(1))
                prompt_loop(lambda: act, block, l)
                act.wait_ge(s_fpr.h, s_fpr.at(l, 1))
                act.dma_start(a["shift_p"][sl, :].rearrange("a (n p) -> (a n) p", p=P), fst[0:7, 0:P]).then_inc(s_state.h, 16)
                act.dma_start(a["conv_p"][sl].rearrange("a k c -> (a k) c"), fst[0:2, P:3 * P]).then_inc(s_state.h, 16)
                for h in range(NH):
                    q, c = slice(64 * (h % 2), 64 * (h % 2) + 64), 3 * P + (h // 2) * P + 64 * (h % 2)
                    act.dma_start(a["st_p"][sl, h].rearrange("a i j -> (a i) j"), fst[q, c:c + 64]).then_inc(s_state.h, 16)
                B = Block(l, None)
                begin(B)
                variance_root(B)
                act.wait_ge(s_sst2.h, s_sst2.at(l, 1))
                for b in range(NS):
                    act.dma_start(a["st_s"][sl, b].rearrange("a (p h) i j -> (h i) (a p) j", p=2), SD[:, 2 * b:2 * b + 2, :]).then_inc(s_state.h, 16)
                act.wait_ge(s_srr.h, s_srr.at(l, 1))
                act.dma_start(a["shift_s"][sl].rearrange("a b c -> (a b) c"), shn[:, :]).then_inc(s_state.h, 16)
                act.dma_start(a["conv_s"][sl, :, 1, :].rearrange("a b c -> (a b) c"), cvn[0:NS, :]).then_inc(s_state.h, 16)
                act.dma_start(a["conv_s"][sl, :, 0, :].rearrange("a b c -> (a b) c"), a["state_conv"][sl, :, 1, :].rearrange("a b c -> (a b) c")).then_inc(s_state.h, 16)

                def copies(i, k, g0, g1):
                    n = l * NS + i * 2 + k
                    for g in range(g0, g1):
                        act.wait_ge(s_dt.h, n * 8 + (g + 1))
                        act.wait_ge(s_ds.h, n * 8 + (max(g - 1, 0) + s_ds.base))
                        act.activation(PT[:, g % 2, :, :], PP[g % 2][:, :].rearrange("p (a t) -> p a t", a=4), ACT.Copy)
                        act.activation(T2f[:, (g % 2) * P:(g % 2) * P + P], PP[2 + g % 2][:, 0:P], ACT.Copy).then_inc(s_dtr.h, 1)

                def exponentials(i, k):
                    act.wait_ge(s_dx.h, l * NS + i * 2 + (k + 1))
                    act.activation(Pb[:, 0:P + 4], T1f[:, 0:P + 4], ACT.Exp, scale=MLA_SCALE).then_inc(s_dxe.h, 1)

                def step(i, k):
                    nxt = (i, 1) if k == 0 else (i + 1, 0)
                    copies(*nxt, 0, 3)
                    exponentials(i, k)
                    copies(*nxt, 3, 8)
                copies(0, 0, 0, 8)
                with act.Fori(0, NS // 2 - 1) as i:
                    step(i, 0)
                    step(i, 1)
                step(NS // 2 - 1, 0)
                exponentials(NS // 2 - 1, 1)
                act.wait_ge(s_const.h, 32)
                act.wait_ge(s_dv.h, s_dv.at(l, NS))
                act.wait_ge(s_dmk.h, s_dmk.at(l, 1))
                decode_output_weights(B.it, 2, 8)
                act.wait_ge(s_dms.h, s_dms.at(l, 1))
                act.activation(Pb[:, 0:64], msc, ACT.Exp, scale=MEM_SCALE).then_inc(s_dme.h, 1)
                finish(B)

        @blk.gpsimd
        def _(pool):
            pool.memset(zero[:, :], 0)
            pool.memset(zerof[:, :], 0.0)
            pool.memset(mhalf[:, :], -0.5)
            pool.drain()
            pool.wait_ge(s_const.h, 32)
            with nc.allow_non_contiguous_dma(reason="page numbers"):
                for s in range(4):
                    pool.dma_start(pgi[s * NPG:(s + 1) * NPG, :], a["page_table"].rearrange("b n -> n b")).then_inc(s_pg.h, 16)
            pool.wait_ge(s_pg.h, 16 * 4)
            pool.tensor_copy(pgf[:, :], pgi[:, :])
            pool.drain()
            pool.tensor_scalar(pgf[:, :], pgf[:, :], 4.0, K("sub"), MULT, ADD)
            pool.drain()

            def root(want, done, it, n, ap, k=1):
                pool.wait_ge(s_const.h, 32)
                pool.wait_ge(want.h, want.at(it, n))
                half = mhalf[0:ap.shape[0], :]
                if len(ap.shape) == 3:
                    half = half.unsqueeze(2)
                pool.tensor_tensor(ap, ap, half.broadcast_to(list(ap.shape)), POW).then_inc(done.h, k)

            def x_roots(px, tiles=2):
                k = 2 // tiles
                for j in range(tiles):
                    pool.wait_ge(s_const.h, 32)
                    pool.wait_ge(s_ss.h, s_ss.at(px, j + k))
                    pool.tensor_tensor(st[:, 4 + j:5 + j], st[:, j:j + 1], zerof[:, 0:1], ADD)
                    pool.drain()
                    pool.tensor_scalar(st[:, 4 + j:5 + j], st[:, 4 + j:5 + j], 1.0 / D, EPS, MULT, ADD)
                    pool.drain()
                    pool.tensor_tensor(st[:, 4 + j:5 + j], st[:, 4 + j:5 + j], mhalf[:, :], POW).then_inc(s_xr.h, k)

            def out_roots(B):
                w, k = min(B.n, P), 2 // B.tiles
                for j in range(B.tiles):
                    root(s_pw, s_pr, B.it, (j + 1) * k, st[0:w, 32 + j:33 + j], k)
            with pool.Fori(0, L) as l:
                for j in range(2):
                    root(s_mem["pw"], s_mem["pr"], l, j + 1, st[:, 4 + j:5 + j])

                x_roots(l * (IT + 1), 1)
                x_roots(l * (IT + 1) + 1)

                def block(B, m, e):
                    x_roots(B.px + 1)
                    out_roots(B)
                prompt_loop(lambda: pool, block, l)
                B = Block(l, None)
                pool.tensor_copy(idx[:, :], pgf[:, :])
                pool.drain()
                pool.tensor_scalar(pgf[:, :], pgf[:, :], float(NPHYS * 4), None, ADD)
                pool.drain()

                def gather(b):
                    if b == 0:
                        pool.wait_ge(s_rt.h, s_rt.at(l * IT + NB, 1))
                    elif b == 1:
                        pool.wait_ge(s_pj.h, s_pj.at(l * NB + NB - 1, NTILES))
                    else:
                        pool.wait_ge(s_dv.h, s_dv.at(l, b - 1))
                    pool.tensor_tensor(idc[:, b:b + 1], idx[:, b:b + 1], zero[:, :], ADD)
                    pool.drain()
                    for dst, cache in ((gat[b % 2], "cache_ckv"), (krg[b % 2], "cache_krope")):
                        pool.indirect_dma_start(dst, None, a[cache].rearrange("l n (g k) r -> (l n g) (k r)", g=4),
                                                bass.IndirectOffsetOnAxis(ap=idc[:, b:b + 1], axis=0)).then_inc(s_dg[b % 2].h, 16)
                gather(0)
                gather(1)
                for b in range(NS):
                    pool.wait_ge(s_dm1.h, l * NS + (b + 1))
                    pool.tensor_tensor(st[:, 12:16], st[:, 0:4], zerof[:, 0:4], ADD)
                    pool.drain()
                    pool.partition_all_reduce(st[:, 4:8], st[:, 12:16], P, bass.bass_isa.ReduceOp.max).then_inc(s_dm2.h, 1)
                    if b + 2 < NS:
                        gather(b + 2)
                pool.wait_ge(s_dmx.h, s_dmx.at(l, 1))
                pool.tensor_tensor(mpx, mmx, zerof[:, :], ADD)
                pool.drain()
                pool.partition_all_reduce(mgx, mpx, P, bass.bass_isa.ReduceOp.max).then_inc(s_dmr.h, 1)
                out_roots(B)
    return nc


_OUTS = [("xres", (L + 1, S + T, D)), ("ckv", (L, S + NS, R)), ("krope", (L, S + NS, RD)),
         ("mem_k", (L, NM, 256)), ("mem_v", (L, NM, 256)), ("conv_p", (L, 2, 256)), ("conv_s", (L, NS, 2, 256)),
         ("shift_p", (L, 896)), ("shift_s", (L, NS, 896)), ("st_p", (L, NH, HD, HD)), ("st_s", (L, NS, NH, HD, HD))]


def kernel(**inputs):
    import concourse.bacc as bacc
    import ml_dtypes
    from concourse.bass_utils import run_bass_kernel_spmd

    nc = bacc.Bacc("TRN2", target_bir_lowering=False, num_devices=1)
    arrays = {k: np.ascontiguousarray(x) for k, x in inputs.items()}
    arrays["cst"] = constants()
    arrays["cs"] = rope_tables()
    q, c = np.arange(P)[:, None], np.arange(FMW)[None, :]
    arrays["fm"] = np.where(c <= q + FMZ, 0.0, NEG).astype(ml_dtypes.bfloat16)
    args = {k: nc.dram_tensor(f"in_{k}", x.shape, mybir.dt.from_np(x.dtype), kind="ExternalInput").ap()
            for k, x in arrays.items()}
    for k, shape in _OUTS:
        args[k] = nc.dram_tensor(f"out_{k}", shape, F32, kind="ExternalOutput").ap()
    build_program(nc, args)
    r = run_bass_kernel_spmd(nc, [{f"in_{k}": x for k, x in arrays.items()}], core_ids=[0])
    g = {k: r.results[0][f"out_{k}"] for k, _ in _OUTS}
    return (g["xres"][L, :S][None], g["xres"][L, S:S + NS][:, None],
            g["ckv"][:, :S][:, None], g["ckv"][:, S:][:, :, None],
            g["krope"][:, :S][:, None], g["krope"][:, S:][:, :, None],
            g["mem_k"].reshape(L, 1, NM, NH, HD), g["mem_v"].reshape(L, 1, NM, NH, HD),
            g["conv_p"][:, None], g["conv_s"], g["shift_p"][:, None], g["shift_s"],
            g["st_p"][:, None], g["st_s"])
```
